# Optimizing a Trainium2 kernel written in Bass

```python
import math
import jax, jax.numpy as jnp
from jax import lax
import numpy as np

D_MODEL = 1024
BATCH = 1
SEQ = 256
DEPTH = 2

N_META = 16
CHUNK = 128
D_MIX = D_MODEL
RET_HEADS = 4
RET_DK = 128
RET_DV = 128
RET_WIDTH = RET_HEADS * RET_DV
RET_THETA = 10000.0
DIFF_HEADS = 4
DIFF_D = 64
DIFF_DV = 2 * DIFF_D
DIFF_WIDTH = DIFF_HEADS * DIFF_DV
ROPE_THETA = 500000.0
ROPE_DIMS = DIFF_D // 4
D_FF = 2816
EPS = 1e-6

IN_SIZES = (
    RET_HEADS * RET_DK,
    RET_HEADS * RET_DK,
    RET_WIDTH,
    RET_WIDTH,
    DIFF_HEADS * 2 * DIFF_D,
    DIFF_HEADS * 2 * DIFF_D,
    DIFF_WIDTH,
)
D_IN = sum(IN_SIZES)


def rmsnorm(x, g):
    xf = x.astype(jnp.float32)
    y = xf * lax.rsqrt(jnp.mean(xf * xf, axis=-1, keepdims=True) + EPS)
    return (y * g.astype(jnp.float32)).astype(x.dtype)

def swiglu(x, w_gate, w_up, w_down):
    return (jax.nn.silu(x @ w_gate) * (x @ w_up)) @ w_down

def retention_rotate(x, pos):
    d = x.shape[-1]
    angle = RET_THETA ** (-jnp.linspace(0.0, 1.0, d // 2, dtype=jnp.float32))
    freqs = pos[:, None] * angle[None, :]
    cos = jnp.cos(freqs)[None, :, None, :]
    sin = jnp.sin(freqs)[None, :, None, :]
    x1, x2 = x[..., 0::2], x[..., 1::2]
    out = jnp.stack([x1 * cos - x2 * sin, x1 * sin + x2 * cos], axis=-1)
    return out.reshape(x.shape)

def partial_rope(x, pos):
    r = ROPE_DIMS
    inv = ROPE_THETA ** (-jnp.arange(0, r, 2, dtype=jnp.float32) / r)
    freqs = pos[:, None] * inv[None, :]
    emb = jnp.concatenate([freqs, freqs], axis=-1)
    cos = jnp.cos(emb)[None, :, None, None, :]
    sin = jnp.sin(emb)[None, :, None, None, :]
    xr, xp = x[..., :r], x[..., r:]
    rot = jnp.concatenate([-xr[..., r // 2:], xr[..., :r // 2]], axis=-1)
    return jnp.concatenate([xr * cos + rot * sin, xp], axis=-1)

def retention_group(q, k, v, g, gn_w):
    B, T = q.shape[0], q.shape[1]
    f32 = jnp.float32
    pos = jnp.arange(T, dtype=f32)
    q = retention_rotate(q.reshape(B, T, RET_HEADS, RET_DK).astype(f32), pos)
    k = retention_rotate(k.reshape(B, T, RET_HEADS, RET_DK).astype(f32), pos) * (RET_DK ** -0.5)
    v = v.reshape(B, T, RET_HEADS, RET_DV).astype(f32)

    n_chunks = -(-T // CHUNK)
    pad = n_chunks * CHUNK - T

    def to_chunks(t):
        t = jnp.pad(t, ((0, 0), (pad, 0), (0, 0), (0, 0)))
        return t.reshape(B, n_chunks, CHUNK, t.shape[2], t.shape[3]).transpose(0, 3, 1, 2, 4)

    qc, kc, vc = to_chunks(q), to_chunks(k), to_chunks(v)

    log_gamma = jnp.log(1.0 - 2.0 ** (-5.0 - jnp.arange(RET_HEADS, dtype=f32)))
    idx = jnp.arange(CHUNK, dtype=f32)
    rel = idx[:, None] - idx[None, :]
    decay_intra = jnp.where(rel >= 0, jnp.exp(log_gamma[:, None, None] * jnp.maximum(rel, 0.0)), 0.0)
    k_decay = jnp.exp(log_gamma[:, None] * (CHUNK - 1 - idx)[None, :])
    q_decay = jnp.exp(log_gamma[:, None] * (idx + 1.0)[None, :])
    chunk_decay = jnp.exp(log_gamma * CHUNK)

    scores = jnp.einsum('bhnid,bhnjd->bhnij', qc, kc) * decay_intra[None, :, None]
    o_intra = jnp.einsum('bhnij,bhnje->bhnie', scores, vc)

    chunk_state = jnp.einsum('bhnjd,bhnje,hj->bhnde', kc, vc, k_decay)

    def step(R, s):
        return R * chunk_decay[None, :, None, None] + s, R

    R0 = jnp.zeros((B, RET_HEADS, RET_DK, RET_DV), f32)
    _, R_prev = lax.scan(step, R0, jnp.moveaxis(chunk_state, 2, 0))
    R_prev = jnp.moveaxis(R_prev, 0, 2)
    o_cross = jnp.einsum('bhnid,bhnde,hi->bhnie', qc, R_prev, q_decay)

    o = (o_intra + o_cross).transpose(0, 2, 3, 1, 4).reshape(B, n_chunks * CHUNK, RET_HEADS, RET_DV)[:, pad:]
    mu = jnp.mean(o, axis=-1, keepdims=True)
    var = jnp.mean((o - mu) ** 2, axis=-1, keepdims=True)
    o = ((o - mu) * lax.rsqrt(var + EPS)).reshape(B, T, RET_WIDTH) * gn_w.astype(f32)
    return (jax.nn.silu(g.astype(f32)) * o).astype(g.dtype)

def diff_attention_group(q, k, v, subln_w, lq1, lk1, lq2, lk2, lambda_init):
    B, T = q.shape[0], q.shape[1]
    f32 = jnp.float32
    pos = jnp.arange(T, dtype=f32)
    q = partial_rope(q.reshape(B, T, DIFF_HEADS, 2, DIFF_D).astype(f32), pos)
    k = partial_rope(k.reshape(B, T, DIFF_HEADS, 2, DIFF_D).astype(f32), pos)
    v = v.reshape(B, T, DIFF_HEADS, DIFF_DV).astype(f32)

    lam = (jnp.exp(jnp.sum(lq1.astype(f32) * lk1.astype(f32)))
           - jnp.exp(jnp.sum(lq2.astype(f32) * lk2.astype(f32))) + lambda_init)

    n_blocks = -(-T // CHUNK)
    pad = n_blocks * CHUNK - T
    q = jnp.pad(q, ((0, 0), (pad, 0), (0, 0), (0, 0), (0, 0))).transpose(0, 2, 3, 1, 4)
    k = jnp.pad(k, ((0, 0), (pad, 0), (0, 0), (0, 0), (0, 0))).transpose(0, 2, 3, 1, 4)
    v = jnp.pad(v, ((0, 0), (pad, 0), (0, 0), (0, 0))).transpose(0, 2, 1, 3)
    scale = DIFF_D ** -0.5

    outs = []
    for nb in range(n_blocks):
        n_keys = (nb + 1) * CHUNK
        qb = q[:, :, :, nb * CHUNK:(nb + 1) * CHUNK]
        s = jnp.einsum('bhmid,bhmjd->bhmij', qb, k[:, :, :, :n_keys]) * scale
        qi = nb * CHUNK + jnp.arange(CHUNK)
        kj = jnp.arange(n_keys)
        allowed = (kj[None, :] <= qi[:, None]) & (kj[None, :] >= pad)
        p = jax.nn.softmax(jnp.where(allowed, s, -1e30), axis=-1)
        a = p[:, :, 0] - lam * p[:, :, 1]
        outs.append(jnp.einsum('bhij,bhje->bhie', a, v[:, :, :n_keys]))
    o = jnp.concatenate(outs, axis=2)[:, :, pad:].transpose(0, 2, 1, 3)
    o = o * lax.rsqrt(jnp.mean(o * o, axis=-1, keepdims=True) + EPS) * subln_w.astype(f32)
    o = o * (1.0 - lambda_init)
    return o.reshape(B, T, DIFF_WIDTH).astype(q.dtype)

def first_inputs(seed: int = 0) -> dict:
    key = jax.random.key(seed)
    ks = jax.random.split(key, 24)
    f32 = jnp.float32
    nrm = lambda k, shape, s: jax.random.normal(k, shape, f32) * s
    gain = lambda k, shape: 1.0 + 0.1 * jax.random.normal(k, shape, f32)
    return {
        "x": jax.random.normal(ks[0], (BATCH, SEQ, D_MODEL), f32),
        "meta_tokens": nrm(ks[1], (N_META, D_MODEL), 1.0),
        "ffn1_norm": gain(ks[2], (DEPTH, D_MODEL)),
        "ffn1_w_gate": nrm(ks[3], (DEPTH, D_MODEL, D_FF), D_MODEL ** -0.5),
        "ffn1_w_up": nrm(ks[4], (DEPTH, D_MODEL, D_FF), D_MODEL ** -0.5),
        "ffn1_w_down": nrm(ks[5], (DEPTH, D_FF, D_MODEL), D_FF ** -0.5),
        "mix_norm": gain(ks[6], (DEPTH, D_MODEL)),
        "w_in": nrm(ks[7], (DEPTH, D_MODEL, D_IN), D_MODEL ** -0.5),
        "ret_gn_w": gain(ks[8], (DEPTH, RET_WIDTH)),
        "diff_subln_w": gain(ks[9], (DEPTH, DIFF_DV)),
        "diff_lambda_q1": nrm(ks[10], (DEPTH, DIFF_D), 0.1),
        "diff_lambda_k1": nrm(ks[11], (DEPTH, DIFF_D), 0.1),
        "diff_lambda_q2": nrm(ks[12], (DEPTH, DIFF_D), 0.1),
        "diff_lambda_k2": nrm(ks[13], (DEPTH, DIFF_D), 0.1),
        "w_out": nrm(ks[14], (DEPTH, D_MIX, D_MODEL), D_MIX ** -0.5),
        "ffn2_norm": gain(ks[15], (DEPTH, D_MODEL)),
        "ffn2_w_gate": nrm(ks[16], (DEPTH, D_MODEL, D_FF), D_MODEL ** -0.5),
        "ffn2_w_up": nrm(ks[17], (DEPTH, D_MODEL, D_FF), D_MODEL ** -0.5),
        "ffn2_w_down": nrm(ks[18], (DEPTH, D_FF, D_MODEL), D_FF ** -0.5),
        "final_norm": gain(ks[19], (D_MODEL,)),
    }

def first_block(x, meta_tokens, ffn1_norm, ffn1_w_gate, ffn1_w_up, ffn1_w_down,
              mix_norm, w_in, ret_gn_w, diff_subln_w, diff_lambda_q1, diff_lambda_k1,
              diff_lambda_q2, diff_lambda_k2, w_out, ffn2_norm, ffn2_w_gate,
              ffn2_w_up, ffn2_w_down, final_norm):
    B = x.shape[0]
    meta = jnp.broadcast_to(meta_tokens.astype(x.dtype)[None], (B, N_META, D_MODEL))
    h = jnp.concatenate([meta, x], axis=1)
    offs = np.cumsum((0,) + IN_SIZES)

    for l in range(DEPTH):
        h = h + 0.5 * swiglu(rmsnorm(h, ffn1_norm[l]), ffn1_w_gate[l], ffn1_w_up[l], ffn1_w_down[l])

        proj = rmsnorm(h, mix_norm[l]) @ w_in[l]
        parts = [proj[..., int(offs[i]):int(offs[i + 1])] for i in range(len(IN_SIZES))]
        rq, rk, rv, rg, dq, dk, dv = parts
        lambda_init = 0.8 - 0.6 * math.exp(-0.3 * l)
        y_ret = retention_group(rq, rk, rv, rg, ret_gn_w[l])
        y_diff = diff_attention_group(dq, dk, dv, diff_subln_w[l], diff_lambda_q1[l],
                                      diff_lambda_k1[l], diff_lambda_q2[l], diff_lambda_k2[l],
                                      lambda_init)
        h = h + jnp.concatenate([y_ret, y_diff], axis=-1) @ w_out[l]

        h = h + 0.5 * swiglu(rmsnorm(h, ffn2_norm[l]), ffn2_w_gate[l], ffn2_w_up[l], ffn2_w_down[l])

    h = rmsnorm(h, final_norm)
    return h[:, N_META:]


DEPTH_2 = 1

GRID_W = 64
CTX_LEN = 256
HEAD_DIM = 64
A_WIDTH = D_MODEL // 4
A_HEADS = A_WIDTH // HEAD_DIM
A_CHUNK = 128
B_WIDTH = D_MODEL // 2
B_HEADS = B_WIDTH // HEAD_DIM
B_KV_HEADS = 2
B_GROUP = B_HEADS // B_KV_HEADS
B_KV_WIDTH = B_KV_HEADS * HEAD_DIM
Q_BLOCK = 128
ROPE_AXIS_DIM = HEAD_DIM // 2
ROPE_BASE = 10000.0
C_WIDTH = D_MODEL // 4
C_HEADS = C_WIDTH // HEAD_DIM
C_CHUNK = 64
MIX_WIDTH = A_WIDTH + B_WIDTH + C_WIDTH
OFF_B = 2 * A_WIDTH
OFF_KV = OFF_B + B_WIDTH
OFF_C = OFF_KV + 2 * B_KV_WIDTH
OFF_G = OFF_C + 4 * C_WIDTH
IN_WIDTH = OFF_G + C_WIDTH
N_GROUPS = 4
EXPERTS_PER_GROUP = 8
N_EXPERTS = N_GROUPS * EXPERTS_PER_GROUP
TOP_K = 2
D_FF_EXPERT = D_MODEL // 2
MOE_BLOCK = 128


def _rms(x):
    xf = x.astype(jnp.float32)
    return (xf * lax.rsqrt(jnp.mean(xf * xf, axis=-1, keepdims=True) + EPS)).astype(x.dtype)

def axial_rope_tables(rows):
    row = jnp.repeat(jnp.arange(rows), GRID_W).astype(jnp.float32)
    col = jnp.tile(jnp.arange(GRID_W), rows).astype(jnp.float32)
    inv_freq = 1.0 / (ROPE_BASE ** (jnp.arange(0, ROPE_AXIS_DIM, 2, dtype=jnp.float32) / ROPE_AXIS_DIM))
    ang = jnp.stack([row[:, None] * inv_freq, col[:, None] * inv_freq], axis=1)
    return jnp.cos(ang)[:, None, :, None, :], jnp.sin(ang)[:, None, :, None, :]

def apply_rope(x, cos, sin):
    b, t, h, _ = x.shape
    xr = x.astype(jnp.float32).reshape(b, t, h, 2, 2, ROPE_AXIS_DIM // 2)
    rot = jnp.stack([-xr[..., 1, :], xr[..., 0, :]], axis=-2)
    return (xr * cos + rot * sin).reshape(b, t, h, HEAD_DIM).astype(x.dtype)

def chunk_mlp(z, w_s, b_s):
    b, t, _ = z.shape
    u, v = jnp.split(jax.nn.gelu(z), 2, axis=-1)
    v = _rms(v.reshape(b, t // A_CHUNK, A_CHUNK, A_HEADS, HEAD_DIM))
    mixed = jnp.einsum('hts,bnshd->bnthd', w_s, v) + b_s.T[:, :, None]
    return u * mixed.reshape(b, t, A_WIDTH)

def _gqa(q, k, v):
    s = jnp.einsum('bqkgd,bskd->bkgqs', q, k).astype(jnp.float32) * (HEAD_DIM ** -0.5)
    p = jax.nn.softmax(s, axis=-1).astype(v.dtype)
    return jnp.einsum('bkgqs,bskd->bqkgd', p, v)

def latent_attention(q, k, v, kc, vc):
    b, t, _, _ = q.shape
    keys = jnp.concatenate([k, kc], axis=1)
    vals = jnp.concatenate([v, vc], axis=1)
    qb = q.reshape(b, t // Q_BLOCK, Q_BLOCK, B_KV_HEADS, B_GROUP, HEAD_DIM).transpose(1, 0, 2, 3, 4, 5)
    out = lax.map(lambda qblk: _gqa(qblk, keys, vals), qb)
    return out.transpose(1, 0, 2, 3, 4, 5).reshape(b, t, B_WIDTH)

def forget_gate(zf, lb):
    zf32 = zf.astype(jnp.float32)
    lbh = lb.reshape(C_HEADS, HEAD_DIM)
    pos = lbh > 0.0
    log_lb = jnp.log(jnp.where(pos, lbh, 1.0))
    log_rest = jnp.log1p(-lbh) + jax.nn.log_sigmoid(zf32)
    log_f = jnp.where(pos, jnp.logaddexp(log_lb, log_rest), log_rest)
    k = (1.0 - lbh) * jax.nn.sigmoid(-zf32)
    return k, log_f

def hgrn_inputs(z, lb):
    b, t, _ = z.shape
    q, zf, zb, v = [a.reshape(b, t, C_HEADS, HEAD_DIM) for a in jnp.split(z, 4, axis=-1)]
    kf, logf_f = forget_gate(zf, lb[0])
    kb, logf_b = forget_gate(zb, lb[1])
    return jax.nn.silu(q), v, kf, logf_f, kb, logf_b

def hgrn_scan(q, k, v, log_f, s0, with_output):
    b, t, h, _ = q.shape
    nc = t // C_CHUNK

    def chunks(a):
        return a.astype(jnp.float32).reshape(b, nc, C_CHUNK, h, a.shape[-1]).transpose(1, 0, 3, 2, 4)

    qc, kc, vc = chunks(q), chunks(k), chunks(v)
    bc = jnp.cumsum(chunks(log_f), axis=3)
    tri = jnp.tril(jnp.ones((C_CHUNK, C_CHUNK), bool))[:, :, None]

    def step(s, inp):
        qi, ki, vi, bi = inp
        b_last = bi[:, :, -1:, :]
        s_new = jnp.exp(b_last[:, :, 0, :, None]) * s + jnp.einsum('bhsk,bhsv->bhkv', ki * jnp.exp(b_last - bi), vi)
        if not with_output:
            return s_new, None
        diff = bi[:, :, :, None, :] - bi[:, :, None, :, :]
        decay = jnp.where(tri, jnp.exp(jnp.where(tri, diff, 0.0)), 0.0)
        scores = jnp.einsum('bhtk,bhsk,bhtsk->bhts', qi, ki, decay)
        o = jnp.einsum('bhts,bhsv->bhtv', scores, vi) + jnp.einsum('bhtk,bhkv->bhtv', qi * jnp.exp(bi), s)
        return s_new, o

    s_fin, o = lax.scan(step, s0, (qc, kc, vc, bc))
    if with_output:
        o = o.transpose(1, 0, 3, 2, 4).reshape(b, t, h, v.shape[-1])
    return s_fin, o

def hgrn_bidir(z, zc, lb, ctx_out):
    q, v, kf, lf, kb, lbw = hgrn_inputs(z, lb)
    qc, vc, kfc, lfc, kbc, lbc = hgrn_inputs(zc, lb)
    s0 = jnp.zeros((z.shape[0], C_HEADS, HEAD_DIM, HEAD_DIM), jnp.float32)
    rev = lambda a: a[:, ::-1]
    sf, of_c = hgrn_scan(qc, kfc, vc, lfc, s0, ctx_out)
    _, of = hgrn_scan(q, kf, v, lf, sf, True)
    sb, ob_c = hgrn_scan(rev(qc), rev(kbc), rev(vc), rev(lbc), s0, ctx_out)
    _, ob = hgrn_scan(rev(q), rev(kb), rev(v), rev(lbw), sb, True)
    o = of + rev(ob)
    o_c = of_c + rev(ob_c) if ctx_out else None
    return o, o_c

def hgrn_out(o, g, w):
    b, t = g.shape[:2]
    return (_rms(o) * w).reshape(b, t, C_WIDTH).astype(g.dtype) * jax.nn.silu(g)

def hier_moe(h, w_grp, b_grp, w_exp, b_exp, w1, w3, w2):
    n_tok, d = h.shape
    g_logits = (h @ w_grp + b_grp).astype(jnp.float32)
    grp = jnp.argmax(g_logits, axis=-1)
    p_grp = jnp.take_along_axis(jax.nn.softmax(g_logits, axis=-1), grp[:, None], axis=-1)
    e_logits = (h @ w_exp + b_exp).astype(jnp.float32).reshape(n_tok, N_GROUPS, EXPERTS_PER_GROUP)
    e_in = jnp.take_along_axis(e_logits, grp[:, None, None], axis=1)[:, 0]
    top_val, top_idx = lax.top_k(e_in, TOP_K)
    gate = (jax.nn.softmax(top_val, axis=-1) * p_grp).reshape(-1)
    expert = (grp[:, None] * EXPERTS_PER_GROUP + top_idx).reshape(-1)
    tok = jnp.repeat(jnp.arange(n_tok), TOP_K)
    n_asg = n_tok * TOP_K
    order = jnp.argsort(expert)
    e_sorted, tok_sorted, gate_sorted = expert[order], tok[order], gate[order]
    counts = jax.ops.segment_sum(jnp.ones_like(expert), expert, num_segments=N_EXPERTS)
    padded = (counts + MOE_BLOCK - 1) // MOE_BLOCK * MOE_BLOCK
    starts = jnp.cumsum(counts) - counts
    pad_ends = jnp.cumsum(padded)
    pad_starts = pad_ends - padded
    dest = pad_starts[e_sorted] + jnp.arange(n_asg) - starts[e_sorted]
    n_blocks = -(-n_asg // MOE_BLOCK) + N_EXPERTS
    buf = jnp.zeros((n_blocks * MOE_BLOCK, d), h.dtype).at[dest].set(h[tok_sorted])
    blk_expert = jnp.minimum(jnp.searchsorted(pad_ends, jnp.arange(n_blocks) * MOE_BLOCK, side='right'), N_EXPERTS - 1)

    def expert_block(args):
        xb, e = args
        return (jax.nn.silu(xb @ w1[e]) * (xb @ w3[e])) @ w2[e]

    out = lax.map(expert_block, (buf.reshape(n_blocks, MOE_BLOCK, d), blk_expert)).reshape(-1, d)
    y = jax.ops.segment_sum(out[dest] * gate_sorted[:, None], tok_sorted, num_segments=n_tok)
    return y.astype(h.dtype)

def hybrid_layer(x, xc, c, c_ctx, cos, sin, lb, w_mod, b_mod, norm1_w, w_in, w_s, b_s, q_norm_w, k_norm_w,
                 hgrn_norm_w, w_out, norm2_w, w_grp, b_grp, w_exp, b_exp, w1, w3, w2, ctx_out):
    b, t, d = x.shape
    lc = xc.shape[1]
    sh1, sc1, g1, sh2, sc2, g2 = jnp.split((jax.nn.silu(c) @ w_mod + b_mod)[:, None, :], 6, axis=-1)
    n_mod = 6 if ctx_out else 2
    mod_c = jnp.split(jax.nn.silu(c_ctx) @ w_mod[:, :n_mod * d] + b_mod[:n_mod * d], n_mod)
    h = _rms(x) * norm1_w * (1.0 + sc1) + sh1
    hc = _rms(xc) * norm1_w * (1.0 + mod_c[1]) + mod_c[0]
    p = h @ w_in
    pc = hc @ w_in[:, OFF_KV:OFF_G]
    ya = chunk_mlp(p[..., :OFF_B], w_s, b_s)
    q = apply_rope(_rms(p[..., OFF_B:OFF_KV].reshape(b, t, B_HEADS, HEAD_DIM)) * q_norm_w, cos, sin)
    k, v = jnp.split(p[..., OFF_KV:OFF_C].reshape(b, t, 2 * B_KV_HEADS, HEAD_DIM), 2, axis=2)
    k = apply_rope(_rms(k) * k_norm_w, cos, sin)
    kc, vc = jnp.split(pc[..., :2 * B_KV_WIDTH].reshape(b, lc, 2 * B_KV_HEADS, HEAD_DIM), 2, axis=2)
    kc = _rms(kc) * k_norm_w
    yb = latent_attention(q, k, v, kc, vc)
    o, o_c = hgrn_bidir(p[..., OFF_C:OFF_G], pc[..., 2 * B_KV_WIDTH:], lb, ctx_out)
    yc = hgrn_out(o, p[..., OFF_G:], hgrn_norm_w)
    x = x + g1 * (jnp.concatenate([ya, yb, yc], axis=-1) @ w_out)
    h2 = _rms(x) * norm2_w * (1.0 + sc2) + sh2
    if ctx_out:
        pc_rest = hc @ w_in[:, :OFF_KV]
        pc_g = hc @ w_in[:, OFF_G:]
        ya_c = chunk_mlp(pc_rest[..., :OFF_B], w_s, b_s)
        qc = _rms(pc_rest[..., OFF_B:].reshape(b, lc, B_HEADS, HEAD_DIM)) * q_norm_w
        yb_c = _gqa(qc.reshape(b, lc, B_KV_HEADS, B_GROUP, HEAD_DIM), kc, vc).reshape(b, lc, B_WIDTH)
        yc_c = hgrn_out(o_c, pc_g, hgrn_norm_w)
        xc = xc + mod_c[2] * (jnp.concatenate([ya_c, yb_c, yc_c], axis=-1) @ w_out)
        h2c = _rms(xc) * norm2_w * (1.0 + mod_c[4]) + mod_c[3]
        tokens = jnp.concatenate([h2.reshape(-1, d), h2c.reshape(-1, d)], axis=0)
        m = hier_moe(tokens, w_grp, b_grp, w_exp, b_exp, w1, w3, w2)
        x = x + g2 * m[:b * t].reshape(b, t, d)
        xc = xc + mod_c[5] * m[b * t:].reshape(b, lc, d)
    else:
        x = x + g2 * hier_moe(h2.reshape(-1, d), w_grp, b_grp, w_exp, b_exp, w1, w3, w2).reshape(b, t, d)
    return x, xc

def second_inputs(seed: int = 0) -> dict:
    key = jax.random.key(seed)
    ks = jax.random.split(key, 24)
    nrm = lambda k, shape, scale: jax.random.normal(k, shape, jnp.float32) * scale
    return {
        'x': nrm(ks[0], (BATCH, SEQ, D_MODEL), 1.0),
        'c': nrm(ks[1], (BATCH, D_MODEL), 1.0),
        'ctx': nrm(ks[2], (BATCH, CTX_LEN, D_MODEL), 1.0),
        'c_ctx': nrm(ks[3], (D_MODEL,), 1.0),
        'w_mod': nrm(ks[4], (DEPTH_2, D_MODEL, 6 * D_MODEL), 0.5 * D_MODEL ** -0.5),
        'b_mod': nrm(ks[5], (DEPTH_2, 6 * D_MODEL), 0.02),
        'norm1_w': 1.0 + nrm(ks[6], (DEPTH_2, D_MODEL), 0.02),
        'w_in': nrm(ks[7], (DEPTH_2, D_MODEL, IN_WIDTH), D_MODEL ** -0.5),
        'w_s': nrm(ks[8], (DEPTH_2, A_HEADS, A_CHUNK, A_CHUNK), A_CHUNK ** -0.5),
        'b_s': 1.0 + nrm(ks[9], (DEPTH_2, A_HEADS, A_CHUNK), 0.02),
        'q_norm_w': 1.0 + nrm(ks[10], (DEPTH_2, HEAD_DIM), 0.02),
        'k_norm_w': 1.0 + nrm(ks[11], (DEPTH_2, HEAD_DIM), 0.02),
        'hgrn_lb_logits': nrm(ks[12], (DEPTH_2, 2, C_WIDTH), 1.0),
        'hgrn_norm_w': 1.0 + nrm(ks[13], (DEPTH_2, HEAD_DIM), 0.02),
        'w_out': nrm(ks[14], (DEPTH_2, MIX_WIDTH, D_MODEL), MIX_WIDTH ** -0.5),
        'norm2_w': 1.0 + nrm(ks[15], (DEPTH_2, D_MODEL), 0.02),
        'w_grp': nrm(ks[16], (DEPTH_2, D_MODEL, N_GROUPS), D_MODEL ** -0.5),
        'b_grp': nrm(ks[17], (DEPTH_2, N_GROUPS), 0.01),
        'w_exp': nrm(ks[18], (DEPTH_2, D_MODEL, N_EXPERTS), D_MODEL ** -0.5),
        'b_exp': nrm(ks[19], (DEPTH_2, N_EXPERTS), 0.01),
        'w1': nrm(ks[20], (DEPTH_2, N_EXPERTS, D_MODEL, D_FF_EXPERT), D_MODEL ** -0.5),
        'w3': nrm(ks[21], (DEPTH_2, N_EXPERTS, D_MODEL, D_FF_EXPERT), D_MODEL ** -0.5),
        'w2': nrm(ks[22], (DEPTH_2, N_EXPERTS, D_FF_EXPERT, D_MODEL), D_FF_EXPERT ** -0.5),
    }

def second_block(x, c, ctx, c_ctx, w_mod, b_mod, norm1_w, w_in, w_s, b_s, q_norm_w, k_norm_w, hgrn_lb_logits,
              hgrn_norm_w, w_out, norm2_w, w_grp, b_grp, w_exp, b_exp, w1, w3, w2):
    ROWS = x.shape[1] // GRID_W
    cos, sin = axial_rope_tables(ROWS)
    lb_sm = jax.nn.softmax(hgrn_lb_logits.astype(jnp.float32), axis=0)
    lb = jnp.cumsum(lb_sm, axis=0) - lb_sm[0]
    xc = ctx
    for l in range(DEPTH_2):
        x, xc = hybrid_layer(x, xc, c, c_ctx, cos, sin, lb[l], w_mod[l], b_mod[l], norm1_w[l], w_in[l], w_s[l],
                             b_s[l], q_norm_w[l], k_norm_w[l], hgrn_norm_w[l], w_out[l], norm2_w[l], w_grp[l],
                             b_grp[l], w_exp[l], b_exp[l], w1[l], w3[l], w2[l], ctx_out=(l < DEPTH_2 - 1))
    return x


def setup_inputs(seed=0):
    out = dict(first_inputs(seed))
    for name, value in second_inputs(seed + 1).items():
        if name != "x":
            out[name + "_2"] = value
    return out


def reference(
    x, meta_tokens, ffn1_norm, ffn1_w_gate, ffn1_w_up, ffn1_w_down, mix_norm, w_in, ret_gn_w,
    diff_subln_w, diff_lambda_q1, diff_lambda_k1, diff_lambda_q2, diff_lambda_k2, w_out,
    ffn2_norm, ffn2_w_gate, ffn2_w_up, ffn2_w_down, final_norm, c_2, ctx_2, c_ctx_2, w_mod_2,
    b_mod_2, norm1_w_2, w_in_2, w_s_2, b_s_2, q_norm_w_2, k_norm_w_2, hgrn_lb_logits_2,
    hgrn_norm_w_2, w_out_2, norm2_w_2, w_grp_2, b_grp_2, w_exp_2, b_exp_2, w1_2, w3_2, w2_2,
):
    x = first_block(
        x, meta_tokens, ffn1_norm, ffn1_w_gate, ffn1_w_up, ffn1_w_down, mix_norm, w_in,
        ret_gn_w, diff_subln_w, diff_lambda_q1, diff_lambda_k1, diff_lambda_q2, diff_lambda_k2,
        w_out, ffn2_norm, ffn2_w_gate, ffn2_w_up, ffn2_w_down, final_norm,
    )
    return second_block(
        x, c_2, ctx_2, c_ctx_2, w_mod_2, b_mod_2, norm1_w_2, w_in_2, w_s_2, b_s_2, q_norm_w_2,
        k_norm_w_2, hgrn_lb_logits_2, hgrn_norm_w_2, w_out_2, norm2_w_2, w_grp_2, b_grp_2,
        w_exp_2, b_exp_2, w1_2, w3_2, w2_2,
    )


_drawn_inputs = setup_inputs


def setup_inputs(seed=0):
    import zlib

    import numpy as np

    out = dict(_drawn_inputs(seed))
    spreads = {}
    factors = {'ctx_2': 3.681,
     'norm1_w_2': 8.0,
     'b_s_2': 8.0,
     'q_norm_w_2': 8.0,
     'k_norm_w_2': 8.0,
     'hgrn_norm_w_2': 8.0,
     'norm2_w_2': 6.037,
     'b_grp_2': 7.973,
     'b_exp_2': 26.775}
    for name, (base, spread) in spreads.items():
        noise = np.random.default_rng([zlib.crc32(name.encode()), seed]).standard_normal(out[name].shape)
        drawn = base * np.exp(spread * noise) if base else spread * noise
        out[name] = __import__('jax').numpy.asarray(drawn.astype(out[name].dtype))
    for name, factor in factors.items():
        out[name] = (out[name] * factor).astype(out[name].dtype)
    return out
```

```python
import math
from contextlib import ExitStack

import numpy as np

import concourse.bass as bass
from concourse import mybir

P = 128
D = 1024
C = D // P
META, SEQ = 16, 256
T = META + SEQ
DEPTH = 2
FF = 2816
F = FF // P
HEADS = 4
TT = [(0, 128), (128, 128), (256, 16)]
EPS = 1e-6
LAMBDA_INIT = [0.8 - 0.6 * math.exp(-0.3 * l) for l in range(DEPTH)]

SLOT = 2048
NS = 11
GU_SLOTS, DOWN_SLOTS = F, F // 2
IN_SLOTS, OUT_SLOTS = 14, 8
LAYER_SLOTS = 2 * (GU_SLOTS + DOWN_SLOTS) + IN_SLOTS + OUT_SLOTS
ROUNDS = LAYER_SLOTS // NS
assert LAYER_SLOTS % NS == 0 and (GU_SLOTS + DOWN_SLOTS) % NS == 0
MOD_SLOTS, IN2_SLOTS = 24, 11
TAIL_SLOTS = MOD_SLOTS + IN2_SLOTS + OUT_SLOTS

E, FE = 32, 512
GROUPS, PER_GROUP = 4, 8
BIG = 4096
BIG_SLOTS = 6
PAIRS = E // 2
CAP = P // 2
PASSES = 256 // CAP
CTX = 256
KEYS = SEQ + CTX
GRID = 64
LEVELS = [64, 32, 16, 8, 4, 2, 1]

VEC = {}


def _columns(table, items):
    at = 0
    for name, n in items:
        table[name] = (at, n)
        at += n
    return at


N_VEC = _columns(VEC, [
    ("norms", 6 * C), ("final", C), ("gn", DEPTH * HEADS), ("subln", DEPTH), ("lam", DEPTH * 4 * 64),
    ("norm1", C), ("norm2", C), ("b_mod", 48), ("c", 2 * C), ("qn", 1), ("kn", 1), ("hgn", 1),
    ("b_s", 2 * P), ("b_router", GROUPS + E)])

CON = {}
DEC = sum(T - t for t, _ in TT)
N_CON = _columns(CON, [
    ("ret_cos", T), ("ret_sin", T), ("diff_cos", T), ("diff_sin", T), ("decay", HEADS * DEC),
    ("causal", 3 * P), ("ret_swap", P), ("diff_swap", P), ("axial_swap", P), ("ident", P),
    ("ones", P), ("half_ones", P), ("axial_cos", SEQ), ("axial_sin", SEQ),
    ("levels", (2 * len(LEVELS) + 1) * P), ("earlier", P), ("iota", CAP), ("eps", 1), ("one", 1)])


def constants():
    f = np.float32
    con = np.zeros((P, N_CON), f)

    def put(name, a):
        at, n = CON[name]
        con[:, at:at + n] = np.asarray(a, f).reshape(P, n)

    pos = np.arange(T, dtype=f)
    p = np.arange(P)
    angle = (f(10000.0) ** (-np.linspace(0.0, 1.0, 64, dtype=f))).astype(f)
    freqs = (pos[:, None] * angle[None, :]).astype(f)
    put("ret_cos", np.cos(freqs).T[p // 2])
    put("ret_sin", np.sin(freqs).T[p // 2] * np.where(p % 2 == 0, -1, 1)[:, None])
    swap = np.zeros((P, P), f)
    swap[p ^ 1, p] = 1
    put("ret_swap", swap)
    inv = (f(500000.0) ** (-np.arange(0, 16, 2, dtype=f) / f(16))).astype(f)
    freqs = (pos[:, None] * inv[None, :]).astype(f)
    r = p % 64
    put("diff_cos", np.where((r < 16)[:, None], np.cos(freqs).T[r % 8], 1))
    put("diff_sin", np.where((r < 16)[:, None], np.sin(freqs).T[r % 8] * np.where(r < 8, -1, 1)[:, None], 0))
    swap = np.zeros((P, P), f)
    swap[np.where(r < 8, p + 8, np.where(r < 16, p - 8, p)), p] = 1
    put("diff_swap", swap)
    inv = (f(1.0) / (f(10000.0) ** (np.arange(0, 32, 2, dtype=f) / f(32)))).astype(f)
    t = np.arange(SEQ)
    axes = np.stack([t // GRID, t % GRID]).astype(f)
    ang = (axes[r // 32] * inv[r % 16][:, None]).astype(f)
    put("axial_cos", np.cos(ang))
    put("axial_sin", np.sin(ang) * np.where(r % 32 < 16, -1, 1)[:, None])
    swap = np.zeros((P, P), f)
    swap[np.where(r % 32 < 16, p + 16, p - 16), p] = 1
    put("axial_swap", swap)
    log_gamma = np.log(f(1.0) - f(2.0) ** (f(-5.0) - np.arange(HEADS, dtype=f))).astype(f)
    parts = []
    for h in range(HEADS):
        for t0, n in TT:
            rel = (np.arange(t0, T)[None, :] - (t0 + p)[:, None]).astype(f)
            parts.append(np.where(rel >= 0, np.exp(log_gamma[h] * np.maximum(rel, 0)), 0) * f(P ** -0.5))
    put("decay", np.concatenate(parts, 1))
    put("causal", np.where(np.arange(3 * P)[None, :] - 2 * P <= p[:, None], 0, -1e30))
    put("ident", np.eye(P))
    put("ones", np.ones((P, P)))
    put("half_ones", p[:, None] // 64 == p[None, :] // 64)
    s, q = p[:, None], p[None, :]
    masks = []
    for m in LEVELS:
        ahead = (s // (2 * m) == q // (2 * m)) & (s // m % 2 == 0) & (q // m % 2 == 1)
        masks += [ahead, ahead.T]
    put("levels", np.concatenate(masks + [s == q], 1))
    put("earlier", s < q)
    put("iota", np.broadcast_to(np.arange(CAP), (P, CAP)))
    put("eps", np.full((P, 1), EPS))
    put("one", np.ones((P, 1)))
    return con


def build(nc, stream_ffn, stream_in, stream_out, stream_mod, stream_in2, stream_out2, stream_expert,
          h_first, ctx_in, vectors, tables, w_router, w_spatial, out):
    fp32, u32 = mybir.dt.float32, mybir.dt.uint32
    ALU, ACT, AX = mybir.AluOpType, mybir.ActivationFunctionType, mybir.AxisListType

    with ExitStack() as ctx:
        def sb(name, shape, dt=fp32):
            return ctx.enter_context(nc.sbuf_tensor(name, shape, dt))

        def sem(name):
            return ctx.enter_context(nc.semaphore(name))

        ring = sb("ring", [P, 12 * SLOT])
        vec = sb("vec", [P, N_VEC])
        con = sb("con", [P, N_CON])
        arena = sb("arena", [P, 20300])
        small = sb("small", [P, 640])
        ps = ctx.enter_context(nc.psum_tensor("ps", [P, 8, 512], fp32))

        def cut(tensor, at, *shape):
            n = int(np.prod(shape))
            piece = tensor[:, at:at + n]
            if len(shape) == 1:
                return piece
            names = "abcd"[:len(shape)]
            sizes = dict(zip(names[1:], shape[1:]))
            return piece.rearrange(f"p ({' '.join(names)}) -> p {' '.join(names)}", **sizes)

        def layout(tensor, at, items):
            found = {}
            for name, *shape in items:
                found[name] = cut(tensor, at, *shape)
                at += int(np.prod(shape))
            assert at <= tensor.shape[1], (at, tensor.shape)
            return found

        def V(name, *shape):
            at, n = VEC[name]
            return cut(vec, at, *(shape or (n,)))

        def K(name, *shape):
            at, n = CON[name]
            return cut(con, at, *(shape or (n,)))

        def slot(s, *shape):
            return cut(ring, s * SLOT, *shape)

        m = layout(arena, 0, [("h", C, T), ("xn", C, T), ("rest", 1)])
        h, xn = m["h"], m["xn"]
        rest = 2 * C * T
        m = layout(arena, rest, [("hid", F, T), ("gate", 4, T), ("sq", C, T), ("std", T), ("rstd", T)])
        hid, gate_act, sq, std, rstd = m["hid"], m["gate"], m["sq"], m["std"], m["rstd"]
        m = layout(arena, rest, [
            ("rot", 16, T), ("raw", 4, T), ("rgate", HEADS, T), ("dv", 3, 512), ("rv", 3, 512),
            ("s", 2, 2, T), ("e", 2, 2, T), ("a", 2, T), ("aT", 2, 3, T), ("o", T), ("osq", T),
            ("ostd", T), ("orstd", T), ("oc", T), ("on", T)])
        rot, raw, rgate, dv, rv = m["rot"], m["raw"], m["rgate"], m["dv"], m["rv"]
        s_buf, e_buf, a_buf, aT_buf = m["s"], m["e"], m["a"], m["aT"]
        o_buf, osq, ostd, orstd, oc, on = m["o"], m["osq"], m["ostd"], m["orstd"], m["oc"], m["on"]
        t_cos, t_sin = s_buf[:, 0], s_buf[:, 1]
        sT = cut(arena, rest + 16 * T + 4 * T + HEADS * T + 6 * 512, 2, DEC)
        msq = cut(arena, rest + 16 * T + 8 * T, C, T)
        mstd = cut(arena, rest + 16 * T + 8 * T + C * T, T)
        mrstd = cut(arena, rest + 16 * T + 8 * T + C * T + T, T)
        y = xn

        lam_prod = cut(arena, rest, DEPTH, 4, 64)
        m = layout(small, 0, [("lam", DEPTH * 4), ("lam_dot", DEPTH * 2), ("neglam", DEPTH), ("sub", DEPTH),
                              ("max", 2, 2), ("negmax", 2, 2), ("sum", 2, 2), ("rsum", 2, 2), ("nr", 2)])
        lam_dot, neglam, sub_w = m["lam_dot"], m["neglam"], m["sub"]
        s_max, neg_max, e_sum, e_rsum, neg_r = m["max"], m["negmax"], m["sum"], m["rsum"], m["nr"]

        consts_loaded, h_loaded, out_stored = sem("consts_loaded"), sem("h_loaded"), sem("out_stored")
        slot_full = [sem(f"slot_full{s}") for s in range(NS)]
        slot_done = sem("slot_done")
        h_ready = sem("h_ready")
        sq_ready, sumsq_ready, std_ready, xn_ready = (sem(x) for x in ("sq_ready", "sumsq_ready", "std_ready", "xn_ready"))
        gate_ready, gate_act_ready, gate_up_used = sem("gate_ready"), sem("gate_act_ready"), sem("gate_up_used")
        y_ready = sem("y_ready")
        proj_evac, swap_ready, rot_ready, v_evac = (sem(x) for x in ("proj_evac", "swap_ready", "rot_ready", "v_evac"))
        scores_ready, masked_ready, max_ready, exp_ready, attn_ready, attn_turned, attnT_ready = (
            sem(x) for x in ("scores_ready", "masked_ready", "max_ready", "exp_ready", "attn_ready", "attn_turned", "attnT_ready"))
        diff_o_ready, diff_sq_ready, diff_sum_ready, diff_std_ready = (
            sem(x) for x in ("diff_o_ready", "diff_sq_ready", "diff_sum_ready", "diff_std_ready"))
        ret_scores_ready, ret_decayed, ret_o_ready, ret_o_evac, ret_mean_ready, ret_centred, ret_sq_ready, ret_var_ready, ret_std_ready = (
            sem(x) for x in ("ret_scores_ready", "ret_decayed", "ret_o_ready", "ret_o_evac", "ret_mean_ready", "ret_centred",
                             "ret_sq_ready", "ret_var_ready", "ret_std_ready"))
        lam_dots_ready, lam_exp_ready = sem("lam_dots_ready"), sem("lam_exp_ready")
        mixed_ready = sem("mixed_ready")

        b0 = 2 * C * T
        m = layout(arena, b0, [("raw2", C, KEYS), ("x2n", C, KEYS), ("z", 4, KEYS), ("k", 4, KEYS), ("t1", 4, KEYS),
                               ("q", 2, SEQ), ("u", 2, SEQ), ("g", 2, SEQ)])
        raw2, x2n, z, hk, log_f, hq, mlp_u, hg = (m[x] for x in ("raw2", "x2n", "z", "k", "t1", "q", "u", "g"))
        at_x2n, at_z = b0 + C * KEYS, b0 + 2 * C * KEYS
        at_k, at_t1 = at_z + 4 * KEYS, at_z + 8 * KEYS
        m = layout(arena, 0, [("B", 4, SEQ), ("G", 4, SEQ), ("zv", 4, SEQ), ("kraw", 2, KEYS), ("state", 4, 64)])
        decay_b, decay_g, zv, ak, state = m["B"], m["G"], m["zv"], m["kraw"], m["state"]
        m = layout(ring, NS * SLOT, [("qraw", 4, SEQ), ("vtok", 4, P), ("va", 2, SEQ)])
        aq, av, mlp_v = m["qraw"], m["vtok"], m["va"]
        sq2 = x2n[:, 0:4]
        m = layout(arena, at_k, [("std2", KEYS), ("rstd2", KEYS), ("norm2t", 2, KEYS)])
        std2, rstd2, scaled2 = m["std2"], m["rstd2"], m["norm2t"]
        y2 = cut(arena, at_z, C, SEQ)
        m = layout(arena, at_x2n, [("lev", 2, 4, SEQ), ("S", 8, P), ("SX", 2, 4, P)])
        lev, S_acc, S_cross = m["lev"], m["S"], m["SX"]
        m = layout(arena, at_t1, [("kdT", 8, P), ("qx", 4, SEQ)])
        kdT, qx = m["kdT"], m["qx"]
        m = layout(arena, at_x2n, [("oh", 2, SEQ), ("ohsq", 2, SEQ), ("ohstd", 2 * SEQ), ("ohr", 2 * SEQ), ("astd", 4, KEYS)])
        oh, oh_sq, oh_std, oh_rstd, a_std = m["oh"], m["ohsq"], m["ohstd"], m["ohr"], m["astd"]
        a_sq = cut(arena, at_k, 4, KEYS)
        a_cos, a_sin = cut(arena, at_k, 4, SEQ), cut(arena, at_k + 4 * SEQ, 4, SEQ)
        m = layout(arena, at_x2n, [("e", 2, KEYS), ("eT", 2, KEYS)])
        ae, aeT = m["e"], m["eT"]
        m = layout(arena, at_t1, [("vsq", 8, 64), ("mix", 2, 2, P)])
        v_sq, mlp_mix = m["vsq"], m["mix"]
        m = layout(arena, 0, [("x2", C, SEQ), ("h2", C, SEQ)])
        x2, h2 = m["x2"], m["h2"]
        m = layout(arena, b0, [("h2t", 2, D), ("xs", C, P), ("ye", D), ("selT", SEQ)])
        h2t, xs, ye, selT = m["h2t"], m["xs"], m["ye"], m["selT"]
        m = layout(arena, at_z, [("act", FE), ("hid", FE), ("hidT", 4, P), ("sel", 2, 2, CAP), ("selg", 2, 2, CAP), ("sq3", C, SEQ), ("std3", SEQ), ("rstd3", SEQ)])
        e_act, e_hid, hidT, sel, sel_gate, sq3, std3, rstd3 = (m[x] for x in ("act", "hid", "hidT", "sel", "selg", "sq3", "std3", "rstd3"))
        m = layout(arena, at_t1 + 4 * KEYS, [
            ("lg", 2, GROUPS + E), ("gmax", 2), ("ngmax", 2), ("gsum", 2), ("gexp", 2, GROUPS), ("p", 2), ("t4", 2, GROUPS),
            ("i4", 2), ("one4", 2, GROUPS), ("em", 2, E), ("v1", 2), ("v2", 2), ("t32", 2, E), ("i32", 2), ("oh1", 2, E), ("oh2", 2, E),
            ("d", 2), ("ex", 2), ("g1", 2), ("g2", 2), ("gate", 2, E), ("chosen", 2, E), ("rank", 2, E + 2), ("most", 1)])
        R = m
        most = ctx.enter_context(nc.sbuf_tensor("most", [P, 1], mybir.dt.int32))
        w_r = cut(con, CON["decay"][0], C, GROUPS + E)
        w_sp = cut(vec, VEC["lam"][0], HEADS, P)
        m = layout(small, 64, [("mod", 48, 2), ("a1", C, 2), ("a2", C), ("cc", C, 2), ("ss", 8), ("vstd", 8), ("vr", 8),
                               ("amax", 2), ("anm", 2), ("asum", 2), ("arsum", 2)])
        mod, a1, a2, cc, v_ss, v_std, v_rstd = (m[x] for x in ("mod", "a1", "a2", "cc", "ss", "vstd", "vr"))
        a_max, a_nmax, a_sum, a_rsum = (m[x] for x in ("amax", "anm", "asum", "arsum"))
        SH1, SC1, G1, SH2, SC2, G2 = (slice(C * i, C * i + C) for i in range(6))

        big_full = [sem(f"big_full{b}") for b in range(BIG_SLOTS)]
        ctx_loaded, router_loaded, spatial_loaded = sem("ctx_loaded"), sem("router_loaded"), sem("spatial_loaded")
        cc_ready, x_ready, sq2_ready, sq2_used, std2_ready, x2n_ready = (
            sem(x) for x in ("cc_ready", "x_ready", "sq2_ready", "sq2_used", "std2_ready", "x2n_ready"))
        proj2_evac, gates_ready, scans_ready, decays_ready, kd_ready, kd_turned, kdT_ready, states_summed, state_ready, qx_ready = (
            sem(x) for x in ("proj2_evac", "gates_ready", "scans_ready", "decays_ready", "kd_ready", "kd_turned", "kdT_ready",
                             "states_summed", "state_ready", "qx_ready"))
        diff_ready, level_exp_ready, level_ready, gram_ready, gram_used = (
            sem(x) for x in ("diff_ready", "level_exp_ready", "level_ready", "gram_ready", "gram_used"))
        o2_ready, o2_sq_ready, o2_sum_ready, o2_std_ready = (sem(x) for x in ("o2_ready", "o2_sq_ready", "o2_sum_ready", "o2_std_ready"))
        v_ss_ready, v_std_ready, v_normed, mlp_mixed = (sem(x) for x in ("v_ss_ready", "v_std_ready", "v_normed", "mlp_mixed"))
        qk_sq_ready, qk_sum_ready, qk_std_ready, qk_normed, qk_swapped, qk_ready = (
            sem(x) for x in ("qk_sq_ready", "qk_sum_ready", "qk_std_ready", "qk_normed", "qk_swapped", "qk_ready"))
        s2_ready, s2_max_ready, s2_exp_ready, p2_ready, p2_turned, p2T_ready, pv2_ready = (
            sem(x) for x in ("s2_ready", "s2_max_ready", "s2_exp_ready", "p2_ready", "p2_turned", "p2T_ready", "pv2_ready"))
        y2_ready, x2_ready, sq3_ready, sum3_ready, std3_ready, h2_ready = (
            sem(x) for x in ("y2_ready", "x2_ready", "sq3_ready", "sum3_ready", "std3_ready", "h2_ready"))
        logits_ready, gmax_ready, gexp_ready, top_ready, top_exp_ready, chosen_ready, ranks_ready, most_ready = (
            sem(x) for x in ("logits_ready", "gmax_ready", "gexp_ready", "top_ready", "top_exp_ready", "chosen_ready", "ranks_ready", "most_ready"))
        h2_turned, h2t_ready, sel_ready, sel_gate_ready, gathered, xs_ready, e_act_ready, e_hid_ready = (
            sem(x) for x in ("h2_turned", "h2t_ready", "sel_ready", "sel_gate_ready", "gathered", "xs_ready", "e_act_ready", "e_hid_ready"))
        hid_turned, hidT_ready, sel_turned, selT_ready, down_ready, ye_ready, big_done, experts_done, out_ready = (
            sem(x) for x in ("hid_turned", "hidT_ready", "sel_turned", "selT_ready", "down_ready", "ye_ready", "big_done", "experts_done", "out_ready"))
        TAIL = DEPTH * LAYER_SLOTS
        N_LEVELS = len(LEVELS) + 2
        UNITS = [(j, hh, i) for j in range(4) for i in range(2) for hh in range(2)]

        ident, ones, half_ones = K("ident"), K("ones"), K("half_ones")
        eps, one = K("eps"), K("one")

        def after(slots):
            return NS + slots

        block = ctx.enter_context(nc.Block())

        @block.sync
        def _(sp):
            sp.dma_start(con[:, :], tables).then_inc(consts_loaded, 16)
            sp.dma_start(vec[:, :], vectors).then_inc(consts_loaded, 16)
            sp.dma_start(h, h_first).then_inc(h_loaded, 16)

            def fill(n, s, src):
                sp.wait_ge(slot_done, n + 1)
                sp.dma_start(slot(s, SLOT)[:, :src.shape[-1]], src).then_inc(slot_full[s], 16)

            def ffn_fills(first, f):
                with sp.Fori(0, (GU_SLOTS + DOWN_SLOTS) // NS) as r:
                    for s in range(NS):
                        fill(first + r * NS + s, s, stream_ffn[f, r * NS + s, :, :])

            with sp.Fori(0, DEPTH) as l:
                first = l * LAYER_SLOTS
                ffn_fills(first, 2 * l)
                at = GU_SLOTS + DOWN_SLOTS
                for q in range(IN_SLOTS):
                    fill(first + at + q, (at + q) % NS, stream_in[l, q, :, :])
                at += IN_SLOTS
                for q in range(OUT_SLOTS):
                    fill(first + at + q, (at + q) % NS, stream_out[l, q, :, :])
                ffn_fills(first + at + OUT_SLOTS, 2 * l + 1)


            def tail_fill(q, src):
                fill(TAIL + q, q % NS, src)

            for q in range(MOD_SLOTS):
                tail_fill(q, stream_mod[q, :, :])
                if q == 2:
                    sp.wait_ge(lam_exp_ready, 1)
                    sp.dma_start(w_sp, w_spatial).then_inc(spatial_loaded, 16)
                    sp.wait_ge(h_ready, 7 * C)
                    sp.dma_start(raw2[:, :, SEQ:KEYS], ctx_in).then_inc(ctx_loaded, 16)
                    sp.dma_start(w_r, w_router).then_inc(router_loaded, 16)
            for q in range(IN2_SLOTS):
                tail_fill(MOD_SLOTS + q, stream_in2[q, :, :])
            for q in range(OUT_SLOTS):
                tail_fill(MOD_SLOTS + IN2_SLOTS + q, stream_out2[q, :, :])
            sp.wait_ge(slot_done, after(TAIL + TAIL_SLOTS))
            def experts(pass_):
                with sp.Fori(0, PAIRS) as pair:
                    for b in range(BIG_SLOTS):
                        sp.wait_ge(big_done, (pass_ * PAIRS + pair) * BIG_SLOTS + b + 1)
                        sp.dma_start(cut(ring, b * BIG, BIG), stream_expert[pair, b, :, :]).then_inc(big_full[b], 16)

            experts(0)
            sp.wait_ge(most_ready, 1)
            with sp.If(sp.value_load(most[0:1, 0:1], min_val=0, max_val=SEQ) > CAP):
                with sp.Fori(1, PASSES) as pass_:
                    experts(pass_)
            for o in range(C):
                sp.wait_ge(out_ready, o + 1)
                sp.dma_start(out[:, o, :], x2[:, o]).then_inc(out_stored, 16)
            sp.wait_ge(out_stored, C * 16)

        @block.tensor
        def _(pe):
            pe.sem_inc(slot_done, NS)
            pe.sem_inc(big_done, BIG_SLOTS)
            pe.wait_ge(consts_loaded, 32)

            def slot_loaded(s, round_):
                pe.wait_ge(slot_full[s], round_ * 16 + 16)

            def norm_sum(n, squares):
                for c in range(C):
                    pe.wait_ge(sq_ready, n * C + c + 1)
                    last = pe.matmul(ps[:, 0, 0:T], ones, squares[:, c], start=c == 0, stop=c == C - 1)
                last.then_inc(sumsq_ready, 1)

            def ffn(l, f, n, round_):
                norm_sum(n, sq)
                with pe.Fori(0, GU_SLOTS // NS) as it:
                    for j in range(NS):
                        slot_loaded(j, round_ + it)
                        if j == 0:
                            pe.wait_ge(xn_ready, n * C + C)
                        w = slot(j, 2, C, P)
                        pe.wait_ge(gate_up_used, f * F + it * NS + j + 1)
                        pair = 2 * (j % 4)
                        for c in range(C):
                            last = pe.matmul(ps[:, pair, 0:T], w[:, 0, c], xn[:, c], start=c == 0, stop=c == C - 1)
                        last.then_inc(gate_ready, 1)
                        for c in range(C):
                            last = pe.matmul(ps[:, pair + 1, 0:T], w[:, 1, c], xn[:, c], start=c == 0, stop=c == C - 1)
                        last.then_inc(slot_done, 1)
                pe.wait_ge(gate_up_used, f * F + F + 3)
                for j in range(DOWN_SLOTS):
                    slot_loaded(j, round_ + 2)
                    w = slot(j, 2, C, P)
                    if j < DOWN_SLOTS - 1:
                        for k in range(2):
                            for o in range(C):
                                last = pe.matmul(ps[:, o, 0:T], w[:, k, o], hid[:, 2 * j + k], start=j + k == 0, stop=False)
                        last.then_inc(slot_done, 1)
                    else:
                        for o in range(C):
                            for k in range(2):
                                last = pe.matmul(ps[:, o, 0:T], w[:, k, o], hid[:, 2 * j + k], start=False, stop=k == 1)
                            last.then_inc(y_ready if o < C - 1 else slot_done, 1)

            def mixer(l, n, round_):
                norm_sum(n, msq)
                pe.wait_ge(xn_ready, n * C + C)
                done = []

                def features(q, tile):
                    slot_loaded(q % NS, round_ + q // NS)
                    w = slot(q % NS, 2, C, P)
                    if tile >= 4:
                        pe.wait_ge(proj_evac, l * 20 + tile - 2)
                    for i in range(2):
                        for c in range(C):
                            last = pe.matmul(ps[:, (tile + i) % 4, 0:T], w[:, i, c], xn[:, c], start=c == 0, stop=c == C - 1)
                    last.then_inc(slot_done, 1)

                def swaps(tile):
                    for i in range(tile, tile + 2):
                        pe.wait_ge(proj_evac, l * 20 + i + 1)
                        if i >= 2:
                            pe.wait_ge(rot_ready, l * 16 + i - 1)
                        pe.matmul(ps[:, 4 if i % 2 == 0 else 7, 0:T], K("diff_swap" if i < 8 else "ret_swap"), raw[:, i % 4],
                                  start=True, stop=True).then_inc(swap_ready, 1)

                def values(q, which):
                    if which == 1:
                        pe.wait_ge(v_evac, l * 6 + 3)
                    for half in range(2):
                        s = (q + half) % NS
                        slot_loaded(s, round_ + (q + half) // NS)
                        w = slot(s, 4, 512)
                        for c in range(4):
                            for t, (t0, nt) in enumerate(TT):
                                k = 4 * half + c
                                bank = (5, 6, 4)[t]
                                last = pe.matmul(ps[0:nt, bank, 0:512], xn[:, k, t0:t0 + nt], w[:, c], start=k == 0, stop=k == C - 1)
                        last.then_inc(slot_done, 1)

                features(0, 0)
                features(1, 2)
                swaps(0)
                features(2, 4)
                swaps(2)
                features(3, 6)
                swaps(4)
                swaps(6)
                pe.wait_ge(rot_ready, l * 16 + 8)
                values(4, 0)
                features(6, 8)
                features(7, 10)
                pe.wait_ge(v_evac, l * 6 + 3)
                swaps(8)
                features(8, 12)
                swaps(10)
                features(9, 14)
                swaps(12)
                swaps(14)
                pe.wait_ge(rot_ready, l * 16 + 16)
                values(10, 1)
                features(12, 16)
                features(13, 18)
                pe.wait_ge(proj_evac, l * 20 + 20)
                pe.wait_ge(v_evac, l * 6 + 6)

                def scores(u):
                    hd, t = divmod(u, 3)
                    t0, nt = TT[t]
                    for g in range(2):
                        rows = slice(64 * g, 64 * g + 64)
                        last = pe.matmul(ps[0:nt, 2 * (u % 2) + g, 0:t0 + nt], rot[rows, hd, t0:t0 + nt],
                                         rot[rows, 4 + hd, 0:t0 + nt], start=True, stop=True)
                    last.then_inc(scores_ready, 1)

                def turn(u):
                    t0, nt = TT[u % 3]
                    pe.wait_ge(attn_ready, l * 12 + u + 1)
                    if u >= 2:
                        pe.wait_ge(attnT_ready, l * 12 + u - 1)
                    for b in range(u % 3 + 1):
                        b0, nb = TT[b]
                        last = pe.matmul(ps[0:nb, 4 + u % 2, b * P:b * P + nt], a_buf[0:nt, u % 2, b0:b0 + nb],
                                         ident[0:nt, 0:nt], start=True, stop=True)
                    last.then_inc(attn_turned, 1)

                def diff_out(hd):
                    pe.wait_ge(attnT_ready, l * 12 + 3 * hd + 3)
                    if hd >= 1:
                        pe.wait_ge(diff_sq_ready, l * 4 + hd)
                    for b, (b0, nb) in enumerate(TT):
                        last = pe.matmul(ps[:, 6, b0:T], dv[0:nb, b, hd * P:hd * P + P], aT_buf[0:nb, hd % 2, b, b0:T],
                                         start=b == 0, stop=b == 2)
                    last.then_inc(diff_o_ready, 1)

                def diff_sum(hd):
                    pe.wait_ge(diff_sq_ready, l * 4 + hd + 1)
                    if hd >= 1:
                        pe.wait_ge(diff_std_ready, l * 4 + hd)
                    pe.matmul(ps[:, 7, 0:T], ones, osq, start=True, stop=True).then_inc(diff_sum_ready, 1)

                for u in range(12):
                    scores(u)
                    if u >= 1:
                        turn(u - 1)
                    if u >= 3 and u % 3 == 0:
                        diff_out(u // 3 - 1)
                    if u >= 3 and u % 3 == 1:
                        diff_sum(u // 3 - 1)
                turn(11)
                diff_out(3)
                diff_sum(3)

                pe.wait_ge(masked_ready, l * 12 + 12)

                def ret_scores(hd):
                    if hd >= 2:
                        pe.wait_ge(ret_decayed, l * 8 + 2 * hd - 2)
                    at = 0
                    for t0, nt in TT:
                        last = pe.matmul(ps[0:nt, hd % 2, at:at + T - t0], rot[:, 12 + hd, t0:t0 + nt], rot[:, 8 + hd, t0:T],
                                         start=True, stop=True)
                        at += T - t0
                    last.then_inc(ret_scores_ready, 1)

                ret_scores(0)
                for hd in range(HEADS):
                    if hd < HEADS - 1:
                        ret_scores(hd + 1)
                    pe.wait_ge(ret_decayed, l * 8 + 2 * hd + 2)
                    if hd >= 1:
                        pe.wait_ge(ret_centred, l * 4 + hd)
                    at = 0
                    for b, (b0, nb) in enumerate(TT):
                        last = pe.matmul(ps[:, 2, b0:T], rv[0:nb, b, hd * P:hd * P + P], sT[0:nb, hd % 2, at:at + T - b0],
                                         start=b == 0, stop=b == 2)
                        at += T - b0
                    last.then_inc(ret_o_ready, 1)
                    pe.wait_ge(ret_o_evac, l * 4 + hd + 1)
                    pe.matmul(ps[:, 3, 0:T], ones, o_buf, start=True, stop=True).then_inc(ret_mean_ready, 1)
                    pe.wait_ge(ret_sq_ready, l * 4 + hd + 1)
                    pe.matmul(ps[:, 7, 0:T], ones, osq, start=True, stop=True).then_inc(ret_var_ready, 1)

                pe.wait_ge(mixed_ready, l * 8 + 8)
                for o in range(C):
                    q = IN_SLOTS + o
                    slot_loaded(q % NS, round_ + q // NS)
                    w = slot(q % NS, C, P)
                    for c in range(C):
                        last = pe.matmul(ps[:, o, 0:T], w[:, c], y[:, c], start=c == 0, stop=c == C - 1)
                    last.then_inc(slot_done, 1)

            with pe.Fori(0, DEPTH) as l:
                ffn(l, 2 * l, 3 * l, l * ROUNDS)
                mixer(l, 3 * l + 1, l * ROUNDS + 3)
                ffn(l, 2 * l + 1, 3 * l + 2, l * ROUNDS + 5)

            norm_sum(3 * DEPTH, sq)
            pe.wait_ge(cc_ready, 1)
            pe.wait_ge(h_ready, 7 * C)

            def tail_slot(q, *shape):
                slot_loaded(q % NS, DEPTH * ROUNDS + q // NS)
                return slot(q % NS, *shape)

            for q in range(MOD_SLOTS):
                w = tail_slot(q, 2, C, P)
                for i in range(2):
                    at = 2 * (2 * q + i)
                    for c in range(C):
                        last = pe.matmul(ps[:, 1, at:at + 2], w[:, i, c], cc[:, c], start=c == 0, stop=c == C - 1)
                last.then_inc(slot_done, 1)
            for c in range(C):
                pe.wait_ge(sq2_ready, c + 1)
                pe.matmul(ps[:, 2, 0:KEYS], ones, sq2[:, c % 4], start=c == 0, stop=c == C - 1).then_inc(sq2_used, 1)

            pe.wait_ge(x2n_ready, 1)
            job = 0

            def bank():
                nonlocal job
                if job >= 8:
                    pe.wait_ge(proj2_evac, job - 7)
                job += 1
                return (job - 1) % 8

            def features(q, n, together):
                w = tail_slot(MOD_SLOTS + q, 2, C, P)
                for i in range(2):
                    if i == 0 or not together:
                        b = bank()
                    at = i * n if together else 0
                    for c in range(C):
                        last = pe.matmul(ps[:, b, at:at + n], w[:, i, c], x2n[:, c, 0:n], start=c == 0, stop=c == C - 1)
                last.then_inc(slot_done, 1)

            def tokens(q, n, tiles_):
                w = tail_slot(MOD_SLOTS + q, SLOT)[:, 0:C * n].rearrange("p (c n) -> p c n", c=C)
                for t in range(tiles_):
                    if t * n % 512 == 0:
                        b = bank()
                    at = t * n % 512
                    for c in range(C):
                        last = pe.matmul(ps[:, b, at:at + n], x2n[:, c, t * P:t * P + P], w[:, c], start=c == 0, stop=c == C - 1)
                last.then_inc(slot_done, 1)

            features(0, KEYS, False)
            features(1, KEYS, False)
            tokens(2, 256, 4)
            features(3, SEQ, True)
            features(4, KEYS, False)
            tokens(5, P, 4)
            features(6, SEQ, True)
            features(7, SEQ, True)
            features(8, SEQ, True)
            tokens(9, 256, 2)
            features(10, SEQ, True)
            pe.wait_ge(proj2_evac, 15)

            pe.wait_ge(kd_ready, 1)
            for i in range(8):
                last = pe.matmul(ps[:, i // 4, (i % 4) * P:(i % 4) * P + P], decay_g[:, i // 2, (i % 2) * P:(i % 2) * P + P], ident,
                                 start=True, stop=True)
            last.then_inc(kd_turned, 1)
            pe.wait_ge(kdT_ready, 1)
            for i in range(4):
                for hh in range(2):
                    head = (i % 2) * 2 + hh
                    for t in range(2):
                        last = pe.matmul(ps[64 * hh:64 * hh + 64, 2, i * 64:i * 64 + 64], kdT[:, 2 * i + t, 64 * hh:64 * hh + 64],
                                         zv[:, 2 + t, head * 64:head * 64 + 64], start=t == 0, stop=t == 1)
            last.then_inc(states_summed, 1)
            pe.wait_ge(state_ready, 1)

            for n in range(N_LEVELS):
                pe.wait_ge(level_ready, n + 1)
                if n >= 2:
                    pe.wait_ge(gram_used, n - 1)
                banks = 4 * (n % 2)
                for d in range(2):
                    for i in range(2):
                        for c in range(2):
                            for hh in range(2):
                                rows = slice(64 * hh, 64 * hh + 64)
                                y_ = lev[rows, n % 2, 2 * d + i]
                                b = banks + 2 * d + hh
                                if n < len(LEVELS):
                                    left = right = y_[:, c * P:c * P + P]
                                    at = (2 * i + c) * P
                                elif n == len(LEVELS):
                                    if c == 1:
                                        continue
                                    left, right = (y_[:, 0:P], y_[:, P:2 * P]) if d == 0 else (y_[:, P:2 * P], y_[:, 0:P])
                                    at = i * P
                                else:
                                    if d == 1:
                                        continue
                                    left, right = y_[:, c * P:c * P + P], hq[rows, i, c * P:c * P + P]
                                    at = (2 * i + c) * P
                                last = pe.matmul(ps[:, b, at:at + P], left, right, start=True, stop=True)
                last.then_inc(gram_ready, 1)
            pe.wait_ge(gram_used, N_LEVELS)
            pe.wait_ge(qx_ready, 1)
            for i in range(2):
                for hh in range(2):
                    rows = slice(64 * hh, 64 * hh + 64)
                    cols = slice((2 * i + hh) * 64, (2 * i + hh) * 64 + 64)
                    b = 4 + 2 * i + hh
                    pe.matmul(ps[rows, b, 0:SEQ], state[rows, i], qx[rows, i], start=True, stop=False)
                    pe.matmul(ps[rows, b, 0:SEQ], state[rows, 2 + i], qx[rows, 2 + i], start=False, stop=False)
                    for c in range(2):
                        pe.matmul(ps[rows, b, c * P:c * P + P], zv[:, c, cols], S_acc[:, hh * 4 + 2 * i + c], start=False, stop=False)
                    pe.matmul(ps[rows, b, P:2 * P], zv[:, 0, cols], S_cross[:, 0, hh * 2 + i], start=False, stop=False)
                    last = pe.matmul(ps[rows, b, 0:P], zv[:, 1, cols], S_cross[:, 1, hh * 2 + i], start=False, stop=True)
            last.then_inc(o2_ready, 1)
            pe.wait_ge(o2_sq_ready, 1)
            pe.matmul(ps[:, 0, 0:512], half_ones, oh_sq, start=True, stop=True).then_inc(o2_sum_ready, 1)

            pe.wait_ge(spatial_loaded, 16)
            pe.wait_ge(v_normed, 1)
            for i in range(2):
                for t in range(2):
                    for hh in range(2):
                        head = 2 * i + hh
                        at = (2 * i + t) * P
                        last = pe.matmul(ps[64 * hh:64 * hh + 64, 1, at:at + P], mlp_v[:, t, head * 64:head * 64 + 64], w_sp[:, head],
                                         start=True, stop=True)
            last.then_inc(mlp_mixed, 1)

            pe.wait_ge(qk_sq_ready, 1)
            for i in range(4):
                last = pe.matmul(ps[:, 2 + i, 0:KEYS], half_ones, a_sq[:, i], start=True, stop=True)
            last.then_inc(qk_sum_ready, 1)
            pe.wait_ge(qk_normed, 1)
            pe.matmul(ps[:, 6, 0:512], K("axial_swap"), aq[:, 0:2], start=True, stop=True)
            pe.matmul(ps[:, 7, 0:512], K("axial_swap"), aq[:, 2:4], start=True, stop=True)
            pe.matmul(ps[:, 0, 0:512], K("axial_swap"), ak[:, :, 0:SEQ], start=True, stop=True).then_inc(qk_swapped, 1)
            pe.wait_ge(qk_ready, 1)

            def scores2(n):
                j, hh, i = UNITS[n]
                rows = slice(64 * hh, 64 * hh + 64)
                if n >= 2:
                    pe.wait_ge(s2_exp_ready, n - 1)
                pe.matmul(ps[:, 2 + n % 2, 0:KEYS], aq[rows, j, i * P:i * P + P], ak[rows, j // 2, 0:KEYS], start=True, stop=True).then_inc(s2_ready, 1)

            def turn2(n):
                pe.wait_ge(p2_ready, n + 1)
                if n >= 2:
                    pe.wait_ge(p2T_ready, n - 1)
                for t in range(4):
                    last = pe.matmul(ps[:, 4 + n % 2, t * P:t * P + P], ae[:, n % 2, t * P:t * P + P], ident, start=True, stop=True)
                last.then_inc(p2_turned, 1)

            def values2(n):
                j, hh, i = UNITS[n]
                pe.wait_ge(p2T_ready, n + 1)
                if n >= 2:
                    pe.wait_ge(y2_ready, 2 + n - 1)
                kv = j // 2
                for t in range(4):
                    last = pe.matmul(ps[64 * hh:64 * hh + 64, 6 + n % 2, 0:P], av[:, t, kv * 64:kv * 64 + 64], aeT[:, n % 2, t * P:t * P + P],
                                     start=t == 0, stop=t == 3)
                last.then_inc(pv2_ready, 1)

            scores2(0)
            for n in range(len(UNITS)):
                if n + 1 < len(UNITS):
                    scores2(n + 1)
                turn2(n)
                if n >= 1:
                    values2(n - 1)
            values2(len(UNITS) - 1)

            pe.wait_ge(y2_ready, 2 + len(UNITS))
            for o in range(C):
                w = tail_slot(MOD_SLOTS + IN2_SLOTS + o, C, P)
                for c in range(C):
                    last = pe.matmul(ps[:, o, 0:SEQ], w[:, c], y2[:, c], start=c == 0, stop=c == C - 1)
                last.then_inc(slot_done, 1)
            for c in range(C):
                pe.wait_ge(sq3_ready, c + 1)
                last = pe.matmul(ps[:, 0, 0:SEQ], ones, sq3[:, c], start=c == 0, stop=c == C - 1)
            last.then_inc(sum3_ready, 1)
            pe.wait_ge(h2_ready, 1)
            pe.wait_ge(router_loaded, 16)
            for t in range(2):
                for c in range(C):
                    last = pe.matmul(ps[:, 1, t * 36:t * 36 + 36], h2[:, c, t * P:t * P + P], w_r[:, c], start=c == 0, stop=c == C - 1)
            last.then_inc(logits_ready, 1)
            for t in range(2):
                for c in range(C):
                    last = pe.matmul(ps[:, 4 + 2 * t + c // 4, (c % 4) * P:(c % 4) * P + P], h2[:, c, t * P:t * P + P], ident, start=True, stop=True)
            last.then_inc(h2_turned, 1)
            pe.wait_ge(chosen_ready, 1)
            pe.matmul(ps[:, 2, 0:E], K("earlier"), R["chosen"][:, 0], start=True, stop=True)
            pe.matmul(ps[:, 2, E:2 * E], ones, R["chosen"][:, 0], start=True, stop=False)
            pe.matmul(ps[:, 2, E:2 * E], K("earlier"), R["chosen"][:, 1], start=False, stop=True)
            pe.matmul(ps[:, 2, 2 * E:3 * E], ones, R["chosen"][:, 0], start=True, stop=False)
            pe.matmul(ps[:, 2, 2 * E:3 * E], ones, R["chosen"][:, 1], start=False, stop=True).then_inc(ranks_ready, 1)

            pe.wait_ge(h2t_ready, 1)
            pe.wait_ge(most_ready, 1)
            for b in range(4):
                pe.matmul(ps[:, b, 0:512], ident, ye[:, 0:512], start=True, stop=False)

            def gather(n):
                pe.wait_ge(sel_ready, n + 1)
                for c in range(C):
                    for t in range(2):
                        last = pe.matmul(ps[:, 6 + c // 4, (c % 4) * P:(c % 4) * P + P], h2t[:, t, c * P:c * P + P], sel[:, t],
                                         start=t == 0, stop=t == 1)
                    if c % 4 == 3:
                        last.then_inc(gathered, 1)

            def scatter(last_pair):
                for o in range(C):
                    last = pe.matmul(ps[:, o // 2, (o % 2) * SEQ:(o % 2) * SEQ + SEQ], ye[:, o * P:o * P + P], selT, start=False,
                                     stop=last_pair and o % 2 == 1)
                return last

            def experts(pass_):
                gather(pass_ * (PAIRS + 1))
                with pe.Fori(0, PAIRS) as pair:
                    n = pass_ * PAIRS + pair
                    g = pass_ * (PAIRS + 1) + pair
                    pe.wait_ge(xs_ready, 2 * g + 2)
                    for e in range(2):
                        rows = slice(CAP * e, CAP * e + CAP)
                        for part in range(2):
                            b = 2 * e + part
                            w = cut(ring, b * BIG, C, FE)
                            pe.wait_ge(big_full[b], n * 16 + 16)
                            if e == 0:
                                pe.wait_ge((hidT_ready, selT_ready)[part], n + 1)
                            for c in range(C):
                                last = pe.matmul(ps[rows, 4 + part, 0:FE], xs[:, c, rows], w[:, c], start=c == 0, stop=c == C - 1)
                            last.then_inc(big_done, 1)
                        if e == 0:
                            pe.wait_ge(ye_ready, 2 * n + 2)
                            scatter(False)
                    gather(g + 1)
                    pe.wait_ge(e_hid_ready, n + 1)
                    for f in range(FE // P):
                        last = pe.matmul(ps[:, 4, f * P:f * P + P], e_hid[:, f * P:f * P + P], ident, start=True, stop=True)
                    last.then_inc(hid_turned, 1)
                    pe.wait_ge(sel_gate_ready, n + 1)
                    for t in range(2):
                        last = pe.matmul(ps[:, 5, t * P:t * P + P], sel_gate[:, t], ident, start=True, stop=True)
                    last.then_inc(sel_turned, 1)
                    pe.wait_ge(hidT_ready, n + 2)
                    for half in range(2):
                        pe.wait_ge(xs_ready, 2 * g + 3 + half)
                        for e in range(2):
                            rows = slice(CAP * e, CAP * e + CAP)
                            w = cut(ring, (4 + e) * BIG, FE // P, D)
                            if half == 0:
                                pe.wait_ge(big_full[4 + e], n * 16 + 16)
                            for f in range(FE // P):
                                last = pe.matmul(ps[rows, 6 + half, 0:512], hidT[:, f, rows], w[:, f, half * 512:half * 512 + 512],
                                                 start=f == 0, stop=f == FE // P - 1)
                            if half == 1:
                                last.then_inc(big_done, 1)
                            elif e == 1:
                                last.then_inc(down_ready, 1)
                pe.wait_ge(ye_ready, (pass_ + 1) * PAIRS * 2 + 2)
                pe.wait_ge(selT_ready, (pass_ + 1) * PAIRS + 1)

            experts(0)
            with pe.If(pe.value_load(most[0:1, 0:1], min_val=0, max_val=SEQ) > CAP):
                with pe.Fori(1, PASSES) as pass_:
                    experts(pass_)
            scatter(True).then_inc(experts_done, 1)

        @block.scalar
        def _(act):
            act.wait_ge(consts_loaded, 32)
            act.wait_ge(lam_dots_ready, 1)
            nc.scalar.activation(lam_dot, lam_dot, ACT.Exp).then_inc(lam_exp_ready, 1)
            nc.scalar.activation(cc, V("c", C, 2), ACT.Silu).then_inc(cc_ready, 1)

            def norm(n, squares, std_to):
                for c in range(C):
                    act.wait_ge(h_ready, n * C + c + 1)
                    nc.scalar.activation(squares[:, c], h[:, c], ACT.Square).then_inc(sq_ready, 1)
                act.wait_ge(sumsq_ready, n + 1)
                nc.scalar.activation(std_to, ps[:, 0, 0:T], ACT.Sqrt, bias=eps, scale=1.0 / D).then_inc(std_ready, 1)

            def ffn(f, n):
                norm(n, sq, std)
                with act.Fori(0, GU_SLOTS // NS) as it:
                    for j in range(NS):
                        act.wait_ge(gate_ready, f * F + it * NS + j + 1)
                        nc.scalar.activation(gate_act[:, j % 4], ps[:, 2 * (j % 4), 0:T], ACT.Silu).then_inc(gate_act_ready, 1)

            def mixer(l, n, slots):
                norm(n, msq, mstd)

                def features(q, tile):
                    act.wait_ge(slot_done, after(slots + q + 1))
                    for i in range(tile, tile + 2):
                        if i < 16:
                            if i >= 4:
                                act.wait_ge(rot_ready, l * 16 + i - 3)
                            nc.scalar.activation(raw[:, i % 4], ps[:, i % 4, 0:T], ACT.Copy).then_inc(proj_evac, 1)
                        else:
                            nc.scalar.activation(rgate[:, i - 16], ps[:, i % 4, 0:T], ACT.Silu).then_inc(proj_evac, 1)

                def values(q, to):
                    act.wait_ge(slot_done, after(slots + q + 2))
                    for t, (_, nt) in enumerate(TT):
                        nc.scalar.activation(to[0:nt, t], ps[0:nt, (5, 6, 4)[t], 0:512], ACT.Copy).then_inc(v_evac, 1)

                for q in range(4):
                    features(q, 2 * q)
                values(4, dv)
                for q in range(6, 10):
                    features(q, 2 * q - 4)
                values(10, rv)
                for q in range(12, 14):
                    features(q, 2 * q - 8)

                def turned(u):
                    hd, t = divmod(u, 3)
                    t0, nt = TT[t]
                    act.wait_ge(attn_turned, l * 12 + u + 1)
                    if t == 0 and hd >= 2:
                        act.wait_ge(diff_o_ready, l * 4 + hd - 1)
                    full = min(t + 1, 2)
                    copy = nc.scalar.activation(aT_buf[:, hd % 2, 0:full, t0:t0 + nt],
                                                ps[:, 4 + u % 2, 0:full * P].rearrange("p (b i) -> p b i", b=full)[:, :, 0:nt], ACT.Copy)
                    if t == 2:
                        copy = nc.scalar.activation(aT_buf[0:META, hd % 2, 2, t0:t0 + nt], ps[0:META, 4 + u % 2, 2 * P:2 * P + nt], ACT.Copy)
                    copy.then_inc(attnT_ready, 1)

                def diff_evac(hd):
                    act.wait_ge(diff_o_ready, l * 4 + hd + 1)
                    if hd >= 1:
                        act.wait_ge(mixed_ready, l * 8 + hd)
                    nc.scalar.activation(o_buf, ps[:, 6, 0:T], ACT.Copy)
                    nc.scalar.activation(osq, ps[:, 6, 0:T], ACT.Square).then_inc(diff_sq_ready, 1)
                    act.wait_ge(diff_sum_ready, l * 4 + hd + 1)
                    nc.scalar.activation(ostd, ps[:, 7, 0:T], ACT.Sqrt, bias=eps, scale=1.0 / P).then_inc(diff_std_ready, 1)

                for u in range(12):
                    nt = TT[u % 3][1]
                    n_keys = TT[u % 3][0] + nt
                    act.wait_ge(max_ready, l * 12 + u + 1)
                    for g in range(2):
                        last = nc.scalar.activation(e_buf[0:nt, u % 2, g, 0:n_keys], s_buf[0:nt, u % 2, g, 0:n_keys], ACT.Exp,
                                                    bias=neg_max[0:nt, u % 2, g:g + 1], accum_out=e_sum[0:nt, u % 2, g:g + 1])
                    last.then_inc(exp_ready, 1)
                    if u >= 1:
                        turned(u - 1)
                    if u >= 3 and u % 3 == 0:
                        diff_evac(u // 3 - 1)
                turned(11)
                diff_evac(3)

                for hd in range(HEADS):
                    act.wait_ge(ret_o_ready, l * 4 + hd + 1)
                    act.wait_ge(mixed_ready, l * 8 + 4 + hd)
                    nc.scalar.activation(o_buf, ps[:, 2, 0:T], ACT.Copy).then_inc(ret_o_evac, 1)
                    act.wait_ge(ret_centred, l * 4 + hd + 1)
                    nc.scalar.activation(osq, oc, ACT.Square).then_inc(ret_sq_ready, 1)
                    act.wait_ge(ret_var_ready, l * 4 + hd + 1)
                    nc.scalar.activation(ostd, ps[:, 7, 0:T], ACT.Sqrt, bias=eps, scale=1.0 / P).then_inc(ret_std_ready, 1)

            with act.Fori(0, DEPTH) as l:
                ffn(2 * l, 3 * l)
                mixer(l, 3 * l + 1, l * LAYER_SLOTS + GU_SLOTS + DOWN_SLOTS)
                ffn(2 * l + 1, 3 * l + 2)

            norm(3 * DEPTH, sq, std)
            act.wait_ge(ctx_loaded, 16)
            for c in range(C):
                act.wait_ge(x_ready, c + 1)
                if c >= 4:
                    act.wait_ge(sq2_used, c - 3)
                nc.scalar.activation(sq2[:, c % 4], raw2[:, c], ACT.Square).then_inc(sq2_ready, 1)
            act.wait_ge(sq2_used, C)
            nc.scalar.activation(std2, ps[:, 2, 0:KEYS], ACT.Sqrt, bias=eps, scale=1.0 / D).then_inc(std2_ready, 1)

            job = 0

            def evac(q, *copies):
                nonlocal job
                act.wait_ge(slot_done, after(TAIL + MOD_SLOTS + q + 1))
                for to, n, func in copies:
                    nc.scalar.activation(to, ps[:, job % 8, 0:n], func).then_inc(proj2_evac, 1)
                    job += 1

            def flat(a):
                return a.rearrange("p a b -> p (a b)")

            evac(0, (z[:, 0], KEYS, ACT.Copy), (z[:, 1], KEYS, ACT.Copy))
            evac(1, (z[:, 2], KEYS, ACT.Copy), (z[:, 3], KEYS, ACT.Copy))
            evac(2, (flat(zv[:, 0:2]), 512, ACT.Copy), (flat(zv[:, 2:4]), 512, ACT.Copy))
            evac(3, (flat(hq), 512, ACT.Silu))
            act.drain()
            nc.scalar.activation(hk, z, ACT.Sigmoid, scale=-1.0)
            nc.scalar.activation(log_f, z, ACT.Abs)
            act.drain()
            nc.scalar.activation(log_f, log_f, ACT.Exp, scale=-1.0)
            act.drain()
            nc.scalar.activation(log_f, log_f, ACT.Ln, bias=one).then_inc(gates_ready, 1)
            evac(4, (ak[:, 0], KEYS, ACT.Copy), (ak[:, 1], KEYS, ACT.Copy))
            evac(5, (flat(av), 512, ACT.Copy))
            evac(6, (flat(aq[:, 0:2]), 512, ACT.Copy))
            evac(7, (flat(aq[:, 2:4]), 512, ACT.Copy))
            evac(8, (flat(mlp_u), 512, ACT.Gelu_apprx_tanh))
            evac(9, (flat(mlp_v), 512, ACT.Gelu_apprx_tanh))
            evac(10, (flat(hg), 512, ACT.Silu))

            act.wait_ge(scans_ready, 1)
            nc.scalar.activation(decay_g, decay_g, ACT.Exp).then_inc(decays_ready, 1)
            nc.scalar.activation(qx[:, 0:2], decay_b[:, 0:2], ACT.Exp)
            nc.scalar.activation(qx[:, 2:4], decay_b[:, 2:4], ACT.Exp, scale=-1.0).then_inc(decays_ready, 1)
            act.wait_ge(kd_turned, 1)
            for i in range(2):
                last = nc.scalar.activation(flat(kdT[:, 4 * i:4 * i + 4]), ps[:, i, 0:512], ACT.Copy)
            last.then_inc(kdT_ready, 1)
            act.wait_ge(states_summed, 1)
            nc.scalar.activation(flat(state), ps[:, 2, 0:SEQ], ACT.Copy).then_inc(state_ready, 1)
            for n in range(N_LEVELS - 1):
                act.wait_ge(diff_ready, n + 1)
                width = 2 * LEVELS[n] if n < len(LEVELS) else SEQ
                pairs = flat(lev[:, n % 2]).rearrange("p (b s m) -> p b s m", s=2, m=width // 2)
                nc.scalar.activation(pairs[:, :, 0], pairs[:, :, 0], ACT.Exp, scale=-1.0)
                nc.scalar.activation(pairs[:, :, 1], pairs[:, :, 1], ACT.Exp).then_inc(level_exp_ready, 1)
            act.wait_ge(o2_ready, 1)
            for i in range(2):
                for hh in range(2):
                    rows = slice(64 * hh, 64 * hh + 64)
                    nc.scalar.activation(oh[rows, i], ps[rows, 4 + 2 * i + hh, 0:SEQ], ACT.Copy)
            act.drain()
            nc.scalar.activation(oh_sq, oh, ACT.Square).then_inc(o2_sq_ready, 1)
            act.wait_ge(o2_sum_ready, 1)
            nc.scalar.activation(oh_std, ps[:, 0, 0:512], ACT.Sqrt, bias=eps, scale=1.0 / 64).then_inc(o2_std_ready, 1)

            act.wait_ge(v_ss_ready, 1)
            nc.scalar.activation(v_std, v_ss, ACT.Sqrt, bias=eps, scale=1.0 / 64).then_inc(v_std_ready, 1)

            nc.scalar.activation(a_sq[:, 0:2], aq, ACT.Square)
            nc.scalar.activation(a_sq[:, 2:4], ak, ACT.Square).then_inc(qk_sq_ready, 1)
            act.wait_ge(qk_sum_ready, 1)
            for i in range(4):
                last = nc.scalar.activation(a_std[:, i], ps[:, 2 + i, 0:KEYS], ACT.Sqrt, bias=eps, scale=1.0 / 64)
            last.then_inc(qk_std_ready, 1)

            def exp2(n):
                act.wait_ge(s2_max_ready, n + 1)
                nc.scalar.activation(ae[:, n % 2], ps[:, 2 + n % 2, 0:KEYS], ACT.Exp, bias=a_nmax[:, n % 2:n % 2 + 1], scale=0.125,
                                     accum_out=a_sum[:, n % 2:n % 2 + 1]).then_inc(s2_exp_ready, 1)

            for n in range(len(UNITS)):
                if n == 0:
                    exp2(0)
                if n + 1 < len(UNITS):
                    exp2(n + 1)
                act.wait_ge(p2_turned, n + 1)
                if n >= 2:
                    act.wait_ge(pv2_ready, n - 1)
                nc.scalar.activation(aeT[:, n % 2], ps[:, 4 + n % 2, 0:512], ACT.Copy).then_inc(p2T_ready, 1)

            for c in range(C):
                act.wait_ge(x2_ready, c + 1)
                nc.scalar.activation(sq3[:, c], x2[:, c], ACT.Square).then_inc(sq3_ready, 1)
            act.wait_ge(sum3_ready, 1)
            nc.scalar.activation(std3, ps[:, 0, 0:SEQ], ACT.Sqrt, bias=eps, scale=1.0 / D).then_inc(std3_ready, 1)

            act.wait_ge(gmax_ready, 1)
            for t in range(2):
                last = nc.scalar.activation(R["gexp"][:, t], R["lg"][:, t, 0:GROUPS], ACT.Exp, bias=R["ngmax"][:, t:t + 1],
                                            accum_out=R["gsum"][:, t:t + 1])
            last.then_inc(gexp_ready, 1)
            act.wait_ge(top_ready, 1)
            nc.scalar.activation(R["ex"], R["d"], ACT.Exp).then_inc(top_exp_ready, 1)
            act.wait_ge(h2_turned, 1)
            nc.scalar.activation(h2t.rearrange("p t d -> p (t d)"), ps[:, 4:8, :].rearrange("p b n -> p (b n)"), ACT.Copy).then_inc(h2t_ready, 1)

            def gathered_tokens(n):
                for half in range(2):
                    act.wait_ge(gathered, 2 * n + half + 1)
                    nc.scalar.activation(xs[:, 4 * half:4 * half + 4], ps[:, 6 + half, 0:512].rearrange("p (c s) -> p c s", s=P), ACT.Copy).then_inc(xs_ready, 1)

            def experts(pass_):
                gathered_tokens(pass_ * (PAIRS + 1))
                with act.Fori(0, PAIRS) as pair:
                    n = pass_ * PAIRS + pair
                    act.wait_ge(big_done, n * BIG_SLOTS + BIG_SLOTS + 3)
                    nc.scalar.activation(e_act, ps[:, 4, 0:FE], ACT.Silu).then_inc(e_act_ready, 1)
                    gathered_tokens(pass_ * (PAIRS + 1) + pair + 1)
                    act.wait_ge(hid_turned, n + 1)
                    nc.scalar.activation(hidT, ps[:, 4, 0:FE].rearrange("p (f s) -> p f s", s=P), ACT.Copy).then_inc(hidT_ready, 1)
                    act.wait_ge(sel_turned, n + 1)
                    nc.scalar.activation(selT, ps[:, 5, 0:SEQ], ACT.Copy).then_inc(selT_ready, 1)
                    act.wait_ge(down_ready, n + 1)
                    nc.scalar.activation(ye[:, 0:512], ps[:, 6, 0:512], ACT.Copy).then_inc(ye_ready, 1)
                    act.wait_ge(big_done, n * BIG_SLOTS + 2 * BIG_SLOTS)
                    nc.scalar.activation(ye[:, 512:D], ps[:, 7, 0:512], ACT.Copy).then_inc(ye_ready, 1)

            experts(0)
            act.wait_ge(most_ready, 1)
            with act.If(act.value_load(most[0:1, 0:1], min_val=0, max_val=SEQ) > CAP):
                with act.Fori(1, PASSES) as pass_:
                    experts(pass_)

        @block.vector
        def _(dve):
            dve.wait_ge(consts_loaded, 32)
            pairs = V("lam", DEPTH * 2, 2, 64)
            prod = cut(arena, rest, DEPTH * 2, 64)
            nc.vector.tensor_tensor(prod, pairs[:, :, 0], pairs[:, :, 1], ALU.mult)
            dve.drain()
            nc.vector.tensor_reduce(lam_dot, prod, AX.X, ALU.add).then_inc(lam_dots_ready, 1)
            dve.wait_ge(lam_exp_ready, 1)
            for l in range(DEPTH):
                nc.vector.tensor_tensor(neglam[:, l:l + 1], lam_dot[:, 2 * l + 1:2 * l + 2], lam_dot[:, 2 * l:2 * l + 1], ALU.subtract)
                nc.vector.tensor_scalar(sub_w[:, l:l + 1], V("subln")[:, l:l + 1], 1.0 - LAMBDA_INIT[l], None, ALU.mult)
            dve.drain()
            for l in range(DEPTH):
                nc.vector.tensor_scalar(neglam[:, l:l + 1], neglam[:, l:l + 1], -LAMBDA_INIT[l], None, ALU.add)
            dve.sem_inc(gate_up_used, 3)
            dve.wait_ge(h_loaded, 16)
            dve.sem_inc(h_ready, C)

            def norm(n, std_from, rstd_to):
                dve.wait_ge(std_ready, n + 1)
                nc.vector.reciprocal(rstd_to, std_from)
                dve.drain()
                for c in range(C):
                    nc.vector.scalar_tensor_tensor(xn[:, c], h[:, c], V("norms")[:, bass.ds(n * C + c, 1)], rstd_to, ALU.mult, ALU.mult).then_inc(xn_ready, 1)

            def residual(ready, scale):
                for o in range(C):
                    ready(o)
                    nc.vector.scalar_tensor_tensor(h[:, o], ps[:, o, 0:T], scale, h[:, o], ALU.mult, ALU.add).then_inc(h_ready, 1)

            def ffn(f, n, slots):
                norm(n, std, rstd)
                with dve.Fori(0, GU_SLOTS // NS) as it:
                    for j in range(NS):
                        dve.wait_ge(gate_act_ready, f * F + it * NS + j + 1)
                        dve.wait_ge(slot_done, after(slots + it * NS + j + 1))
                        to = cut(arena, rest, F * T)[:, bass.ds(it * (NS * T) + j * T, T)]
                        nc.vector.tensor_tensor(to, gate_act[:, j % 4], ps[:, 2 * (j % 4) + 1, 0:T], ALU.mult).then_inc(gate_up_used, 1)

                def ready(o):
                    if o < C - 1:
                        dve.wait_ge(y_ready, f * (C - 1) + o + 1)
                    else:
                        dve.wait_ge(slot_done, after(slots + GU_SLOTS + DOWN_SLOTS))

                residual(ready, 0.5)

            def mixer(l, n, slots):
                norm(n, mstd, mrstd)

                for i in range(16):
                    table = "diff" if i < 8 else "ret"
                    dve.wait_ge(proj_evac, l * 20 + i + 1)
                    nc.vector.tensor_tensor(t_cos[:, i % 2], raw[:, i % 4], K(table + "_cos"), ALU.mult)
                    dve.wait_ge(swap_ready, l * 16 + i + 1)
                    nc.vector.tensor_tensor(t_sin[:, i % 2], ps[:, 4 if i % 2 == 0 else 7, 0:T], K(table + "_sin"), ALU.mult)
                    dve.drain()
                    nc.vector.tensor_tensor(rot[:, i], t_cos[:, i % 2], t_sin[:, i % 2], ALU.add).then_inc(rot_ready, 1)

                def masked(u):
                    t0, nt = TT[u % 3]
                    n_keys = t0 + nt
                    dve.wait_ge(scores_ready, l * 12 + u + 1)
                    mask = K("causal")[0:nt, 2 * P - t0:2 * P - t0 + n_keys].unsqueeze(1).to_broadcast([nt, 2, n_keys])
                    at = 2 * (u % 2)
                    nc.vector.scalar_tensor_tensor(s_buf[0:nt, u % 2, :, 0:n_keys], ps[0:nt, at:at + 2, 0:n_keys], 64.0 ** -0.5,
                                                   mask, ALU.mult, ALU.add).then_inc(masked_ready, 1)
                    dve.drain()
                    nc.vector.tensor_reduce(s_max[0:nt, u % 2], s_buf[0:nt, u % 2, :, 0:n_keys], AX.X, ALU.max)
                    dve.drain()
                    nc.vector.tensor_scalar(neg_max[0:nt, u % 2], s_max[0:nt, u % 2], -1.0, None, ALU.mult).then_inc(max_ready, 1)

                def combine(u):
                    t0, nt = TT[u % 3]
                    n_keys = t0 + nt
                    dve.wait_ge(exp_ready, l * 12 + u + 1)
                    nc.vector.reciprocal(e_rsum[0:nt, u % 2], e_sum[0:nt, u % 2])
                    dve.drain()
                    nc.vector.tensor_scalar(neg_r[0:nt, u % 2:u % 2 + 1], e_rsum[0:nt, u % 2, 1:2], neglam[0:nt, bass.ds(l, 1)], None, ALU.mult)
                    if u >= 2:
                        dve.wait_ge(attn_turned, l * 12 + u - 1)
                    nc.vector.tensor_scalar(a_buf[0:nt, u % 2, 0:n_keys], e_buf[0:nt, u % 2, 0, 0:n_keys], e_rsum[0:nt, u % 2, 0:1], None, ALU.mult)
                    dve.drain()
                    nc.vector.scalar_tensor_tensor(a_buf[0:nt, u % 2, 0:n_keys], e_buf[0:nt, u % 2, 1, 0:n_keys], neg_r[0:nt, u % 2:u % 2 + 1],
                                                   a_buf[0:nt, u % 2, 0:n_keys], ALU.mult, ALU.add).then_inc(attn_ready, 1)

                def diff_norm(hd):
                    dve.wait_ge(diff_std_ready, l * 4 + hd + 1)
                    nc.vector.reciprocal(orstd, ostd)
                    dve.drain()
                    nc.vector.scalar_tensor_tensor(y[:, 4 + hd], o_buf, sub_w[:, bass.ds(l, 1)], orstd, ALU.mult, ALU.mult).then_inc(mixed_ready, 1)

                for u in range(12):
                    masked(u)
                    if u >= 1:
                        combine(u - 1)
                    if u >= 4 and u % 3 == 1:
                        diff_norm(u // 3 - 1)
                combine(11)
                diff_norm(3)

                def decayed(hd):
                    dve.wait_ge(ret_scores_ready, l * 4 + hd + 1)
                    if hd >= 2:
                        dve.wait_ge(ret_o_ready, l * 4 + hd - 1)
                    decay = K("decay", HEADS, DEC)[:, hd]
                    wide = DEC - META
                    nc.vector.tensor_tensor(sT[:, hd % 2, 0:wide], ps[:, hd % 2, 0:wide], decay[:, 0:wide], ALU.mult).then_inc(ret_decayed, 1)
                    nc.vector.tensor_tensor(sT[0:META, hd % 2, wide:DEC], ps[0:META, hd % 2, wide:DEC], decay[0:META, wide:DEC], ALU.mult).then_inc(ret_decayed, 1)

                decayed(0)
                for hd in range(HEADS):
                    if hd < HEADS - 1:
                        decayed(hd + 1)
                    dve.wait_ge(ret_mean_ready, l * 4 + hd + 1)
                    nc.vector.scalar_tensor_tensor(oc, ps[:, 3, 0:T], -1.0 / P, o_buf, ALU.mult, ALU.add).then_inc(ret_centred, 1)
                    dve.wait_ge(ret_std_ready, l * 4 + hd + 1)
                    nc.vector.reciprocal(orstd, ostd)
                    dve.drain()
                    nc.vector.scalar_tensor_tensor(on, oc, V("gn")[:, bass.ds(l * HEADS + hd, 1)], orstd, ALU.mult, ALU.mult)
                    dve.drain()
                    nc.vector.tensor_tensor(y[:, hd], on, rgate[:, hd], ALU.mult).then_inc(mixed_ready, 1)

                residual(lambda o: dve.wait_ge(slot_done, after(slots + IN_SLOTS + o + 1)), 1.0)

            with dve.Fori(0, DEPTH) as l:
                first = l * LAYER_SLOTS
                ffn(2 * l, 3 * l, first)
                mixer(l, 3 * l + 1, first + GU_SLOTS + DOWN_SLOTS)
                ffn(2 * l + 1, 3 * l + 2, first + GU_SLOTS + DOWN_SLOTS + IN_SLOTS + OUT_SLOTS)

            def wide(a, n, m):
                return a.unsqueeze(2).to_broadcast([P, n, m])

            def flat(a):
                return a.rearrange("p a b -> p (a b)")

            dve.wait_ge(std_ready, 3 * DEPTH + 1)
            nc.vector.reciprocal(rstd, std)
            dve.drain()
            for c in range(C):
                nc.vector.scalar_tensor_tensor(raw2[:, c, 0:SEQ], h[:, c, META:T], V("final")[:, c:c + 1], rstd[:, META:T], ALU.mult, ALU.mult).then_inc(x_ready, 1)
            dve.wait_ge(slot_done, after(TAIL + MOD_SLOTS))
            nc.vector.tensor_tensor(mod, ps[:, 1, 0:96].rearrange("p (o n) -> p o n", n=2), wide(V("b_mod"), 48, 2), ALU.add)
            dve.drain()
            nc.vector.scalar_tensor_tensor(a1, mod[:, SC1], 1.0, wide(V("norm1"), C, 2), ALU.add, ALU.mult)
            nc.vector.scalar_tensor_tensor(a2, mod[:, SC2, 0], 1.0, V("norm2"), ALU.add, ALU.mult)
            dve.wait_ge(std2_ready, 1)
            nc.vector.reciprocal(rstd2, std2)
            dve.drain()
            for c in range(C):
                nc.vector.tensor_tensor(scaled2[:, c % 2], raw2[:, c], rstd2, ALU.mult)
                dve.drain()
                for i in range(2):
                    half = slice(i * SEQ, i * SEQ + SEQ)
                    last = nc.vector.tensor_scalar(x2n[:, c, half], scaled2[:, c % 2, half], a1[:, c, i:i + 1], mod[:, c, i:i + 1], ALU.mult, ALU.add)
            last.then_inc(x2n_ready, 1)

            dve.wait_ge(gates_ready, 1)
            nc.vector.scalar_tensor_tensor(log_f, z, 0.0, log_f, ALU.min, ALU.subtract)
            nc.vector.memset(decay_g[:, 0:2, SEQ - 1:SEQ], 0.0)
            nc.vector.memset(decay_g[:, 2:4, 0:1], 0.0)
            dve.drain()
            unit = one.to_broadcast([P, SEQ])
            for i in range(2):
                nc.vector.tensor_tensor_scan(decay_b[:, i], unit, log_f[:, i, 0:SEQ], 0.0, ALU.mult, ALU.add)
                nc.vector.tensor_tensor_scan(decay_b[:, 2 + i, ::-1], unit, log_f[:, 2 + i, 0:SEQ][:, ::-1], 0.0, ALU.mult, ALU.subtract)
                nc.vector.tensor_tensor_scan(decay_g[:, i, 0:SEQ - 1][:, ::-1], unit[:, 1:], log_f[:, i, SEQ + 1:KEYS][:, ::-1], 0.0, ALU.mult, ALU.add)
                last = nc.vector.tensor_tensor_scan(decay_g[:, 2 + i, 1:SEQ], unit[:, 1:], log_f[:, 2 + i, SEQ:KEYS - 1], 0.0, ALU.mult, ALU.add)
            last.then_inc(scans_ready, 1)
            dve.wait_ge(decays_ready, 1)
            nc.vector.tensor_tensor(decay_g, decay_g, hk[:, :, SEQ:KEYS], ALU.mult).then_inc(kd_ready, 1)
            dve.wait_ge(decays_ready, 2)
            for d in range(2):
                last = nc.vector.tensor_tensor(qx[:, 2 * d:2 * d + 2], qx[:, 2 * d:2 * d + 2], hq, ALU.mult)
            last.then_inc(qx_ready, 1)

            dve.wait_ge(slot_done, after(TAIL + MOD_SLOTS + IN2_SLOTS))
            nc.vector.memset(S_acc, 0.0)

            def difference(n):
                if n >= 2:
                    dve.wait_ge(gram_ready, n - 1)
                half = LEVELS[n] if n < len(LEVELS) else P
                for d in range(2):
                    b = flat(decay_b[:, 2 * d:2 * d + 2]).rearrange("p (b m) -> p b m", m=2 * half)
                    to = flat(lev[:, n % 2, 2 * d:2 * d + 2]).rearrange("p (b m) -> p b m", m=2 * half)
                    at = half - 1 + d
                    last = nc.vector.tensor_tensor(to, b, b[:, :, at:at + 1].to_broadcast([P, SEQ // half, 2 * half]), ALU.subtract)
                last.then_inc(diff_ready, 1)

            def level(n):
                dve.wait_ge(level_exp_ready, n + 1)
                half = LEVELS[n] if n < len(LEVELS) else P
                for d in range(2):
                    to = lev[:, n % 2, 2 * d:2 * d + 2].rearrange("p i (b s m) -> p i b s m", s=2, m=half)
                    for side in range(2):
                        by = (hk[:, 2 * d:2 * d + 2, 0:SEQ] if side == d else hq).rearrange("p i (b s m) -> p i b s m", s=2, m=half)
                        last = nc.vector.tensor_tensor(to[:, :, :, side], to[:, :, :, side], by[:, :, :, side], ALU.mult)
                last.then_inc(level_ready, 1)

            def merge(n):
                dve.wait_ge(gram_ready, n + 1)
                banks = 4 * (n % 2)
                if n < len(LEVELS):
                    for d in range(2):
                        dve.drain()
                        mask = K("levels", 2 * len(LEVELS) + 1, P)[:, 2 * n + d].bitcast(u32).unsqueeze(1).to_broadcast([P, 8, P])
                        last = nc.vector.copy_predicated(S_acc, mask, ps[:, banks + 2 * d:banks + 2 * d + 2, :].rearrange("p b (c t) -> p (b c) t", t=P))
                elif n == len(LEVELS):
                    for d in range(2):
                        last = nc.vector.tensor_copy(S_cross[:, d].rearrange("p (b c) t -> p b (c t)", b=2), ps[:, banks + 2 * d:banks + 2 * d + 2, 0:256])
                else:
                    dve.drain()
                    mask = K("levels", 2 * len(LEVELS) + 1, P)[:, 2 * len(LEVELS)].bitcast(u32).unsqueeze(1).to_broadcast([P, 8, P])
                    last = nc.vector.copy_predicated(S_acc, mask, ps[:, banks:banks + 2, :].rearrange("p b (c t) -> p (b c) t", t=P))
                last.then_inc(gram_used, 1)

            difference(0)
            for n in range(N_LEVELS):
                if n + 1 < N_LEVELS - 1:
                    difference(n + 1)
                if n < N_LEVELS - 1:
                    level(n)
                else:
                    dve.wait_ge(gram_ready, n - 1)
                    nc.vector.tensor_tensor(lev[:, n % 2, 0:2], hk[:, 0:2, 0:SEQ], hk[:, 2:4, 0:SEQ], ALU.add).then_inc(level_ready, 1)
                if n >= 1:
                    merge(n - 1)
            merge(N_LEVELS - 1)

            dve.wait_ge(o2_std_ready, 1)
            nc.vector.reciprocal(oh_rstd, oh_std)
            dve.drain()
            nc.vector.scalar_tensor_tensor(flat(oh), flat(oh), V("hgn"), oh_rstd, ALU.mult, ALU.mult)
            dve.drain()
            nc.vector.tensor_tensor(y2[:, 6:8], oh, hg, ALU.mult).then_inc(y2_ready, 1)

            vh = flat(mlp_v).rearrange("p (h d) -> p h d", d=64)
            nc.vector.tensor_tensor(v_sq, vh, vh, ALU.mult)
            dve.drain()
            nc.vector.tensor_reduce(v_ss, v_sq, AX.X, ALU.add).then_inc(v_ss_ready, 1)
            dve.wait_ge(v_std_ready, 1)
            nc.vector.reciprocal(v_rstd, v_std)
            dve.drain()
            nc.vector.tensor_tensor(vh, vh, wide(v_rstd, 8, 64), ALU.mult).then_inc(v_normed, 1)
            dve.wait_ge(mlp_mixed, 1)
            nc.vector.tensor_tensor(mlp_mix, ps[:, 1, 0:512].rearrange("p (i t n) -> p i t n", i=2, t=2),
                                    V("b_s", 2, P).unsqueeze(2).to_broadcast([P, 2, 2, P]), ALU.add)
            dve.drain()
            nc.vector.tensor_tensor(flat(y2[:, 0:2]), flat(mlp_u), mlp_mix.rearrange("p a b c -> p (a b c)"), ALU.mult).then_inc(y2_ready, 1)

            dve.wait_ge(qk_std_ready, 1)
            nc.vector.reciprocal(a_std, a_std)
            dve.drain()
            nc.vector.scalar_tensor_tensor(flat(aq), flat(aq), V("qn"), flat(a_std[:, 0:2]), ALU.mult, ALU.mult)
            nc.vector.scalar_tensor_tensor(flat(ak), flat(ak), V("kn"), flat(a_std[:, 2:4]), ALU.mult, ALU.mult).then_inc(qk_normed, 1)
            dve.wait_ge(qk_swapped, 1)

            def rotate(x, swapped, n):
                cos = K("axial_cos").unsqueeze(1).to_broadcast([P, n, SEQ])
                sin = K("axial_sin").unsqueeze(1).to_broadcast([P, n, SEQ])
                nc.vector.tensor_tensor(a_cos[:, 0:n], x, cos, ALU.mult)
                nc.vector.tensor_tensor(a_sin[:, 0:n], swapped, sin, ALU.mult)
                dve.drain()
                return nc.vector.tensor_tensor(x, a_cos[:, 0:n], a_sin[:, 0:n], ALU.add)

            rotate(aq, ps[:, 6:8, :].rearrange("p b (c t) -> p (b c) t", t=SEQ), 4)
            dve.drain()
            rotate(ak[:, :, 0:SEQ], ps[:, 0, :].rearrange("p (c t) -> p c t", t=SEQ), 2).then_inc(qk_ready, 1)

            def max2(n):
                dve.wait_ge(s2_ready, n + 1)
                k = slice(n % 2, n % 2 + 1)
                nc.vector.tensor_reduce(a_max[:, k], ps[:, 2 + n % 2, 0:KEYS], AX.X, ALU.max)
                dve.drain()
                nc.vector.tensor_scalar(a_nmax[:, k], a_max[:, k], -0.125, None, ALU.mult).then_inc(s2_max_ready, 1)

            def out2(n):
                j, hh, i = UNITS[n]
                rows = slice(64 * hh, 64 * hh + 64)
                dve.wait_ge(pv2_ready, n + 1)
                nc.vector.tensor_copy(y2[rows, 2 + j, i * P:i * P + P], ps[rows, 6 + n % 2, 0:P]).then_inc(y2_ready, 1)

            max2(0)
            for n in range(len(UNITS)):
                if n + 1 < len(UNITS):
                    if n >= 1:
                        dve.wait_ge(p2_turned, n)
                    max2(n + 1)
                k = slice(n % 2, n % 2 + 1)
                dve.wait_ge(s2_exp_ready, n + 1)
                nc.vector.reciprocal(a_rsum[:, k], a_sum[:, k])
                dve.drain()
                nc.vector.tensor_scalar(ae[:, n % 2], ae[:, n % 2], a_rsum[:, k], None, ALU.mult).then_inc(p2_ready, 1)
                if n >= 1:
                    out2(n - 1)
            out2(len(UNITS) - 1)

            for o in range(C):
                dve.wait_ge(slot_done, after(TAIL + MOD_SLOTS + IN2_SLOTS + o + 1))
                nc.vector.scalar_tensor_tensor(x2[:, o], ps[:, o, 0:SEQ], mod[:, G1, 0][:, o:o + 1], raw2[:, o, 0:SEQ], ALU.mult, ALU.add).then_inc(x2_ready, 1)
            dve.wait_ge(std3_ready, 1)
            nc.vector.reciprocal(rstd3, std3)
            dve.drain()
            for c in range(C):
                nc.vector.scalar_tensor_tensor(h2[:, c], x2[:, c], a2[:, c:c + 1], rstd3, ALU.mult, ALU.mult)
            dve.drain()
            for c in range(C):
                last = nc.vector.tensor_scalar(h2[:, c], h2[:, c], mod[:, SH2, 0][:, c:c + 1], None, ALU.add)
            last.then_inc(h2_ready, 1)

            dve.wait_ge(logits_ready, 1)
            nc.vector.tensor_tensor(R["lg"], ps[:, 1, 0:72].rearrange("p (t e) -> p t e", t=2), V("b_router").unsqueeze(1).to_broadcast([P, 2, 36]), ALU.add)
            dve.drain()
            groups = R["lg"][:, :, 0:GROUPS]
            nc.vector.tensor_reduce(R["gmax"], groups, AX.X, ALU.max)
            dve.drain()
            nc.vector.tensor_scalar(R["ngmax"], R["gmax"], -1.0, None, ALU.mult).then_inc(gmax_ready, 1)

            def first_greatest(x, top, n, index, scratch, onehot):
                iota = K("iota")[:, 0:n].unsqueeze(1).to_broadcast([P, 2, n])
                nc.vector.tensor_tensor(scratch, x, wide(top, 2, n), ALU.is_lt)
                dve.drain()
                nc.vector.scalar_tensor_tensor(scratch, scratch, 64.0, iota, ALU.mult, ALU.add)
                dve.drain()
                nc.vector.tensor_reduce(index, scratch, AX.X, ALU.min)
                dve.drain()
                nc.vector.tensor_tensor(onehot, iota, wide(index, 2, n), ALU.is_equal)
                dve.drain()

            first_greatest(groups, R["gmax"], GROUPS, R["i4"], R["t4"], R["one4"])
            nc.vector.tensor_scalar(R["t4"], R["one4"], -1.0, 1e30, ALU.add, ALU.mult)
            dve.drain()
            nc.vector.tensor_tensor(R["em"].rearrange("p t (g e) -> p t g e", g=GROUPS), R["lg"][:, :, GROUPS:].rearrange("p t (g e) -> p t g e", g=GROUPS),
                                    R["t4"].unsqueeze(3).to_broadcast([P, 2, GROUPS, PER_GROUP]), ALU.add)
            dve.drain()
            nc.vector.tensor_reduce(R["v1"], R["em"], AX.X, ALU.max)
            dve.drain()
            first_greatest(R["em"], R["v1"], E, R["i32"], R["t32"], R["oh1"])
            nc.vector.scalar_tensor_tensor(R["em"], R["oh1"], -3e30, R["em"], ALU.mult, ALU.add)
            dve.drain()
            nc.vector.tensor_reduce(R["v2"], R["em"], AX.X, ALU.max)
            dve.drain()
            nc.vector.tensor_tensor(R["d"], R["v2"], R["v1"], ALU.subtract).then_inc(top_ready, 1)
            first_greatest(R["em"], R["v2"], E, R["i32"], R["t32"], R["oh2"])
            nc.vector.tensor_tensor(R["chosen"], R["oh1"], R["oh2"], ALU.add).then_inc(chosen_ready, 1)
            dve.wait_ge(gexp_ready, 1)
            dve.wait_ge(top_exp_ready, 1)
            nc.vector.tensor_scalar(R["g1"], R["ex"], 1.0, None, ALU.add)
            dve.drain()
            nc.vector.tensor_tensor(R["g1"], R["g1"], R["gsum"], ALU.mult)
            dve.drain()
            nc.vector.reciprocal(R["g1"], R["g1"])
            dve.drain()
            nc.vector.tensor_tensor(R["g2"], R["g1"], R["ex"], ALU.mult)
            nc.vector.tensor_tensor(R["oh1"], R["oh1"], wide(R["g1"], 2, E), ALU.mult)
            dve.drain()
            nc.vector.tensor_tensor(R["oh2"], R["oh2"], wide(R["g2"], 2, E), ALU.mult)
            dve.drain()
            nc.vector.tensor_tensor(R["gate"], R["oh1"], R["oh2"], ALU.add)
            dve.drain()
            nc.vector.memset(ye, 0.0)
            nc.vector.memset(selT, 0.0)
            nc.vector.memset(R["rank"], -1.0)
            dve.wait_ge(ranks_ready, 1)
            nc.vector.tensor_reduce(R["gmax"][:, 0:1], ps[:, 2, 2 * E:3 * E], AX.X, ALU.max)
            dve.drain()
            ranks = R["rank"][:, :, 0:E]
            nc.vector.scalar_tensor_tensor(ranks, ps[:, 2, 0:2 * E].rearrange("p (t e) -> p t e", t=2), 1.0, R["chosen"], ALU.add, ALU.mult)
            nc.vector.tensor_copy(most[:, :], R["gmax"][:, 0:1])
            dve.drain()
            nc.vector.tensor_scalar(ranks, ranks, -1.0, None, ALU.add).then_inc(most_ready, 1)
            dve.drain()

            dve.sem_inc(ye_ready, 2)
            dve.sem_inc(hidT_ready, 1)
            dve.sem_inc(selT_ready, 1)
            iota = K("iota").unsqueeze(1).unsqueeze(1).to_broadcast([P, 2, 2, CAP])

            def by_slot(a, pair):
                return a[:, :, bass.ds(pair * 2, 2)].unsqueeze(3).to_broadcast([P, 2, 2, CAP])

            def select(pair):
                nc.vector.tensor_tensor(sel, iota, by_slot(R["rank"], pair), ALU.is_equal).then_inc(sel_ready, 1)

            def experts(pass_):
                select(0)
                with dve.Fori(0, PAIRS) as pair:
                    n = pass_ * PAIRS + pair
                    dve.drain()
                    dve.wait_ge(sel_turned, n)
                    nc.vector.tensor_tensor(sel_gate, sel, by_slot(R["gate"], pair), ALU.mult).then_inc(sel_gate_ready, 1)
                    dve.drain()
                    dve.wait_ge(gathered, (pass_ * (PAIRS + 1) + pair) * 2 + 2)
                    select(pair + 1)
                    dve.wait_ge(e_act_ready, n + 1)
                    dve.wait_ge(big_done, n * BIG_SLOTS + BIG_SLOTS + 4)
                    nc.vector.tensor_tensor(e_hid, e_act, ps[:, 5, 0:FE], ALU.mult).then_inc(e_hid_ready, 1)

            experts(0)
            with dve.If(dve.value_load(most[0:1, 0:1], min_val=0, max_val=SEQ) > CAP):
                with dve.Fori(1, PASSES) as pass_:
                    dve.drain()
                    nc.vector.tensor_scalar(R["rank"], R["rank"], -float(CAP), None, ALU.add)
                    dve.drain()
                    dve.wait_ge(gathered, pass_ * (PAIRS + 1) * 2)
                    experts(pass_)
            dve.wait_ge(experts_done, 1)
            for o in range(C):
                nc.vector.scalar_tensor_tensor(x2[:, o], ps[:, o // 2, (o % 2) * SEQ:(o % 2) * SEQ + SEQ], mod[:, G2, 0][:, o:o + 1], x2[:, o],
                                               ALU.mult, ALU.add).then_inc(out_ready, 1)


def tiles(w, rows, cols):
    lead = w.shape[:-2]
    w = w.reshape(*lead, rows, P, cols, P)
    n = len(lead)
    return w.transpose(*range(n), n + 2, n + 1, n, n + 3)


def by_feature(a):
    return a.reshape(-1, P).T


def lay_out(x, meta_tokens, ffn1_norm, ffn1_w_gate, ffn1_w_up, ffn1_w_down, mix_norm, w_in, ret_gn_w, diff_subln_w,
            diff_lambda_q1, diff_lambda_k1, diff_lambda_q2, diff_lambda_k2, w_out, ffn2_norm, ffn2_w_gate, ffn2_w_up,
            ffn2_w_down, final_norm, c_2, ctx_2, c_ctx_2, w_mod_2, b_mod_2, norm1_w_2, w_in_2, w_s_2, b_s_2, q_norm_w_2,
            k_norm_w_2, hgrn_lb_logits_2, hgrn_norm_w_2, w_out_2, norm2_w_2, w_grp_2, b_grp_2, w_exp_2, b_exp_2, w1_2,
            w3_2, w2_2):
    f = np.float32
    ffn = np.empty((2 * DEPTH, GU_SLOTS + DOWN_SLOTS, P, SLOT), f)
    for l in range(DEPTH):
        for i, (g, u, d) in enumerate(((ffn1_w_gate, ffn1_w_up, ffn1_w_down), (ffn2_w_gate, ffn2_w_up, ffn2_w_down))):
            to = ffn[2 * l + i]
            both = to[:GU_SLOTS].reshape(F, P, 2, C, P)
            both[:, :, 0] = tiles(g[l], C, F)
            both[:, :, 1] = tiles(u[l], C, F)
            to[GU_SLOTS:] = d[l].reshape(DOWN_SLOTS, 2, P, D).transpose(0, 2, 1, 3).reshape(DOWN_SLOTS, P, SLOT)

    def features(w, first):
        w = w[:, first * P:(first + 2) * P]
        return tiles(w, C, 2).transpose(1, 0, 2, 3).reshape(P, -1)

    def rows(w, first, n):
        return w[:, first:first + n].reshape(C, P, n).transpose(1, 0, 2).reshape(P, -1)

    win = np.empty((DEPTH, IN_SLOTS, P, SLOT), f)
    for l in range(DEPTH):
        w = w_in[l]
        q = 0
        for first in (16, 18, 20, 22, "dv", 0, 2, 4, 6, "rv", 12, 14):
            if isinstance(first, str):
                v = rows(w, (24 if first == "dv" else 8) * P, 512)
                win[l, q], win[l, q + 1] = v[:, :SLOT], v[:, SLOT:]
                q += 2
            else:
                win[l, q] = features(w, first)
                q += 1
    wout = np.ascontiguousarray(tiles(w_out, C, C).reshape(DEPTH, OUT_SLOTS, P, D))

    mod = np.ascontiguousarray(tiles(w_mod_2[0], C, 48).reshape(MOD_SLOTS, 2, P, D).transpose(0, 2, 1, 3).reshape(MOD_SLOTS, P, SLOT))
    w = w_in_2[0]
    in2 = np.zeros((IN2_SLOTS, P, SLOT), f)
    key = w[:, 1024:1152].reshape(D, 2, 1, 64)
    twice = np.concatenate([key, key], 2).reshape(D, 256)
    for q, a in enumerate((features(w, 12), features(w, 14), rows(w, 2048, 256), features(w, 10), features(twice, 0),
                           rows(w, 1152, 128), features(w, 4), features(w, 6), features(w, 0), rows(w, 256, 256), features(w, 18))):
        in2[q, :, :a.shape[1]] = a
    out2 = np.ascontiguousarray(tiles(w_out_2[0], C, C).reshape(OUT_SLOTS, P, D))
    expert = np.empty((PAIRS, BIG_SLOTS, P, BIG), f)
    up = expert[:, 0:4].reshape(PAIRS, 2, 2, P, C, FE)
    up[:, :, 0] = w1_2[0].reshape(PAIRS, 2, C, P, FE).transpose(0, 1, 3, 2, 4)
    up[:, :, 1] = w3_2[0].reshape(PAIRS, 2, C, P, FE).transpose(0, 1, 3, 2, 4)
    expert[:, 4:6] = w2_2[0].reshape(PAIRS, 2, FE // P, P, D).transpose(0, 1, 3, 2, 4).reshape(PAIRS, 2, P, BIG)

    vec = np.empty((P, N_VEC), f)

    def put(name, a):
        at, n = VEC[name]
        vec[:, at:at + n] = np.asarray(a).reshape(-1, n)

    norms = np.stack([np.stack([ffn1_norm[l], mix_norm[l], ffn2_norm[l]]) for l in range(DEPTH)])
    put("norms", by_feature(norms))
    put("final", by_feature(final_norm))
    put("gn", by_feature(ret_gn_w))
    put("subln", by_feature(diff_subln_w))
    put("lam", np.stack([diff_lambda_q1, diff_lambda_k1, diff_lambda_q2, diff_lambda_k2], 1))
    put("norm1", by_feature(norm1_w_2))
    put("norm2", by_feature(norm2_w_2))
    put("b_mod", by_feature(b_mod_2))
    put("c", np.stack([c_2.reshape(C, P).T, c_ctx_2.reshape(C, P).T], 2).reshape(P, -1))
    for name, a in (("qn", q_norm_w_2), ("kn", k_norm_w_2), ("hgn", hgrn_norm_w_2)):
        put(name, np.concatenate([a[0], a[0]])[:, None])
    put("b_s", np.repeat(b_s_2[0].reshape(2, 2, P).transpose(1, 0, 2).reshape(2, 2 * P), 64, axis=0))
    put("b_router", np.concatenate([b_grp_2, b_exp_2], 1))

    first = np.concatenate([meta_tokens, x[0]], 0)
    return {
        "stream_ffn": ffn, "stream_in": win, "stream_out": wout, "stream_mod": mod, "stream_in2": in2, "stream_out2": out2,
        "stream_expert": expert,
        "h_first": np.ascontiguousarray(first.T.reshape(C, P, T).transpose(1, 0, 2)),
        "ctx_in": np.ascontiguousarray(ctx_2[0].T.reshape(C, P, CTX).transpose(1, 0, 2)),
        "vectors": vec, "tables": constants(),
        "w_router": np.ascontiguousarray(np.concatenate([w_grp_2[0], w_exp_2[0]], 1).reshape(C, P, GROUPS + E).transpose(1, 0, 2)),
        "w_spatial": np.ascontiguousarray(w_s_2[0].transpose(2, 0, 1)),
    }


def kernel(**inputs):
    import concourse.bacc as bacc
    from concourse.bass_utils import run_bass_kernel_spmd

    arrays = lay_out(**{k: np.asarray(v) for k, v in inputs.items()})
    nc = bacc.Bacc("TRN2", target_bir_lowering=False, num_devices=1)
    aps = {name: nc.dram_tensor(name, a.shape, mybir.dt.from_np(a.dtype), kind="ExternalInput").ap() for name, a in arrays.items()}
    out = nc.dram_tensor("out", (P, C, SEQ), mybir.dt.float32, kind="ExternalOutput").ap()
    build(nc, out=out, **aps)
    result = run_bass_kernel_spmd(nc, [arrays], core_ids=[0]).results[0]["out"]
    return np.ascontiguousarray(np.asarray(result).transpose(2, 1, 0)).reshape(1, SEQ, D)
```

```python
import math
from contextlib import ExitStack

import numpy as np

import concourse.bass as bass
from concourse import mybir

P = 128
D = 1024
C = D // P
META, SEQ = 16, 256
T = META + SEQ
DEPTH = 2
FF = 2816
F = FF // P
HEADS = 4
TT = [(0, 128), (128, 128), (256, 16)]
EPS = 1e-6
LAMBDA_INIT = [0.8 - 0.6 * math.exp(-0.3 * l) for l in range(DEPTH)]

SLOT = 2048
NS = 11
GU_SLOTS, DOWN_SLOTS = F, F // 2
IN_SLOTS, OUT_SLOTS = 14, 8
MOD_SLOTS, MOD_MIX = 24, 11
MOD_COLS = SLOT // C
LAYER_SLOTS = 2 * (GU_SLOTS + DOWN_SLOTS) + IN_SLOTS + MOD_MIX + OUT_SLOTS
FFN_SLOTS = GU_SLOTS + DOWN_SLOTS
MIX_SLOTS = IN_SLOTS + MOD_MIX + OUT_SLOTS
HALF = SLOT // 2
PER_ROUND = 2 * NS
HALVES = 2 * FFN_SLOTS
ARENA = 20304
SPLITS = 4
ROUNDS = LAYER_SLOTS // NS
assert LAYER_SLOTS % NS == 0 and (GU_SLOTS + DOWN_SLOTS) % NS == 0
IN2_SLOTS = 11
MOD_TAIL = MOD_SLOTS - DEPTH * MOD_MIX
TAIL_SLOTS = MOD_TAIL + IN2_SLOTS + OUT_SLOTS

E, FE = 32, 512
GROUPS, PER_GROUP = 4, 8
BIG = 4096
BIG_SLOTS = 6
PAIRS = E // 2
CAP = P // 2
PASSES = 256 // CAP
CTX = 256
KEYS = SEQ + CTX
GRID = 64
AHEAD = 3
LEVELS = [64, 32, 16, 8, 4, 2, 1]

VEC = {}


def _columns(table, items):
    at = 0
    for name, n in items:
        table[name] = (at, n)
        at += n
    return at


N_VEC = _columns(VEC, [
    ("norms", 6 * C), ("final", C), ("gn", DEPTH * HEADS), ("subln", DEPTH), ("lam", DEPTH * 4 * 64),
    ("norm1", C), ("norm2", C), ("b_mod", 48), ("c", 2 * C), ("qn", 1), ("kn", 1), ("hgn", 1),
    ("b_s", 2 * P), ("b_router", GROUPS + E)])

CON = {}
DEC = sum(T - t for t, _ in TT)
N_CON = _columns(CON, [
    ("ret_cos", T), ("ret_sin", T), ("diff_cos", T), ("diff_sin", T), ("decay", HEADS * DEC),
    ("causal", 3 * P), ("ret_swap", P), ("diff_swap", P), ("axial_swap", P), ("ident", P),
    ("ones", P), ("half_ones", P), ("axial_cos", SEQ), ("axial_sin", SEQ),
    ("levels", (2 * len(LEVELS) + 1) * P), ("earlier", P), ("iota", CAP), ("eps", 1), ("one", 1)])


def constants():
    f = np.float32
    con = np.zeros((P, N_CON), f)

    def put(name, a):
        at, n = CON[name]
        con[:, at:at + n] = np.asarray(a, f).reshape(P, n)

    pos = np.arange(T, dtype=f)
    p = np.arange(P)
    angle = (f(10000.0) ** (-np.linspace(0.0, 1.0, 64, dtype=f))).astype(f)
    freqs = (pos[:, None] * angle[None, :]).astype(f)
    put("ret_cos", np.cos(freqs).T[p // 2])
    put("ret_sin", np.sin(freqs).T[p // 2] * np.where(p % 2 == 0, -1, 1)[:, None])
    swap = np.zeros((P, P), f)
    swap[p ^ 1, p] = 1
    put("ret_swap", swap)
    inv = (f(500000.0) ** (-np.arange(0, 16, 2, dtype=f) / f(16))).astype(f)
    freqs = (pos[:, None] * inv[None, :]).astype(f)
    r = p % 64
    put("diff_cos", np.where((r < 16)[:, None], np.cos(freqs).T[r % 8], 1))
    put("diff_sin", np.where((r < 16)[:, None], np.sin(freqs).T[r % 8] * np.where(r < 8, -1, 1)[:, None], 0))
    swap = np.zeros((P, P), f)
    swap[np.where(r < 8, p + 8, np.where(r < 16, p - 8, p)), p] = 1
    put("diff_swap", swap)
    inv = (f(1.0) / (f(10000.0) ** (np.arange(0, 32, 2, dtype=f) / f(32)))).astype(f)
    t = np.arange(SEQ)
    axes = np.stack([t // GRID, t % GRID]).astype(f)
    ang = (axes[r // 32] * inv[r % 16][:, None]).astype(f)
    put("axial_cos", np.cos(ang))
    put("axial_sin", np.sin(ang) * np.where(r % 32 < 16, -1, 1)[:, None])
    swap = np.zeros((P, P), f)
    swap[np.where(r % 32 < 16, p + 16, p - 16), p] = 1
    put("axial_swap", swap)
    log_gamma = np.log(f(1.0) - f(2.0) ** (f(-5.0) - np.arange(HEADS, dtype=f))).astype(f)
    parts = []
    for h in range(HEADS):
        for t0, n in TT:
            rel = (np.arange(t0, T)[None, :] - (t0 + p)[:, None]).astype(f)
            parts.append(np.where(rel >= 0, np.exp(log_gamma[h] * np.maximum(rel, 0)), 0) * f(P ** -0.5))
    put("decay", np.concatenate(parts, 1))
    put("causal", np.where(np.arange(3 * P)[None, :] - 2 * P <= p[:, None], 0, -1e30))
    put("ident", np.eye(P))
    put("ones", np.ones((P, P)))
    put("half_ones", p[:, None] // 64 == p[None, :] // 64)
    s, q = p[:, None], p[None, :]
    masks = []
    for m in LEVELS:
        ahead = (s // (2 * m) == q // (2 * m)) & (s // m % 2 == 0) & (q // m % 2 == 1)
        masks += [ahead, ahead.T]
    put("levels", np.concatenate(masks + [s == q], 1))
    put("earlier", s < q)
    put("iota", np.broadcast_to(np.arange(CAP), (P, CAP)))
    put("eps", np.full((P, 1), EPS))
    put("one", np.ones((P, 1)))
    return con


def build(nc, stream_ffn, stream_in, stream_out, stream_mod, stream_in2, stream_out2, stream_expert,
          h_first, ctx_in, vectors, tables, w_router, w_spatial, out):
    fp32, u32, f32r = mybir.dt.float32, mybir.dt.uint32, mybir.dt.float32r
    ALU, ACT, AX = mybir.AluOpType, mybir.ActivationFunctionType, mybir.AxisListType

    with ExitStack() as ctx:
        def sb(name, shape, dt=fp32):
            return ctx.enter_context(nc.sbuf_tensor(name, shape, dt))

        def sem(name):
            return ctx.enter_context(nc.semaphore(name))

        ring = sb("ring", [P, 12 * SLOT])
        ring_at = nc.sbuf_base - 4 * 12 * SLOT
        arena = sb("arena", [P, ARENA])
        arena_at = nc.sbuf_base - 4 * ARENA
        vec = sb("vec", [P, N_VEC])
        con = sb("con", [P, N_CON])
        small = sb("small", [P, 640])
        ps = ctx.enter_context(nc.psum_tensor("ps", [P, 8, 512], fp32))

        def cut(tensor, at, *shape):
            n = int(np.prod(shape))
            piece = tensor[:, at:at + n]
            if len(shape) == 1:
                return piece
            names = "abcd"[:len(shape)]
            sizes = dict(zip(names[1:], shape[1:]))
            return piece.rearrange(f"p ({' '.join(names)}) -> p {' '.join(names)}", **sizes)

        def layout(tensor, at, items):
            found = {}
            for name, *shape in items:
                found[name] = cut(tensor, at, *shape)
                at += int(np.prod(shape))
            assert at <= tensor.shape[1], (at, tensor.shape)
            return found

        def V(name, *shape):
            at, n = VEC[name]
            return cut(vec, at, *(shape or (n,)))

        def K(name, *shape):
            at, n = CON[name]
            return cut(con, at, *(shape or (n,)))

        def slot(s, *shape):
            return cut(ring, s * SLOT, *shape)

        def parts(name, byte, *shape):
            n = int(np.prod(shape))
            return cut(nc.alloc_sbuf_tensor_at(name, [P, n], f32r, offset=byte), 0, *shape)

        m = layout(arena, 0, [("h", C, T), ("xn", C, T), ("rest", 1)])
        h, xn = m["h"], m["xn"]
        rest = 2 * C * T
        m = layout(arena, rest, [("hid", F, T), ("gate", 4, T), ("sq", C, T), ("std", T), ("rstd", T)])
        hid, gate_act, sq, std, rstd = m["hid"], m["gate"], m["sq"], m["std"], m["rstd"]
        xn_hi = parts("xn_hi", arena_at + 4 * C * T, C, T)
        xn_lo = parts("xn_lo", arena_at + 4 * (rest + F * T + 4 * T), C, T)
        w_split = [parts(f"w_split{b}", ring_at + 4 * NS * SLOT if b == 0 else arena_at + 4 * (ARENA - b * SLOT), 2, C, P)
                   for b in range(SPLITS)]
        assert rest + F * T + 4 * T + C * T + 2 * T <= ARENA - (SPLITS - 1) * SLOT
        xn32 = cut(arena, rest + (F - C) * T, C, T)
        m = layout(arena, rest, [
            ("rot", 16, T), ("raw", 4, T), ("rgate", HEADS, T), ("dv", 3, 512), ("rv", 3, 512),
            ("s", 2, 2, T), ("e", 2, 2, T), ("a", 2, T), ("aT", 2, 3, T), ("o", T), ("osq", T),
            ("ostd", T), ("orstd", T), ("oc", T), ("on", T)])
        rot, raw, rgate, dv, rv = m["rot"], m["raw"], m["rgate"], m["dv"], m["rv"]
        s_buf, e_buf, a_buf, aT_buf = m["s"], m["e"], m["a"], m["aT"]
        o_buf, osq, ostd, orstd, oc, on = m["o"], m["osq"], m["ostd"], m["orstd"], m["oc"], m["on"]
        m = layout(arena, rest + 28 * T + 6 * 512, [("o", T), ("osq", T), ("ostd", T), ("orstd", T), ("oc", T), ("on", T)])
        RET = [(o_buf, osq, ostd, orstd, oc, on), tuple(m[x] for x in ("o", "osq", "ostd", "orstd", "oc", "on"))]
        t_cos, t_sin = s_buf[:, 0], s_buf[:, 1]
        sT = cut(arena, rest + 16 * T + 4 * T + HEADS * T + 6 * 512, 2, DEC)
        msq = cut(arena, rest + 16 * T + 8 * T, C, T)
        mstd = cut(arena, rest + 16 * T + 8 * T + C * T, T)
        mrstd = cut(arena, rest + 16 * T + 8 * T + C * T + T, T)
        y = xn

        lam_prod = cut(arena, rest, DEPTH, 4, 64)
        m = layout(small, 0, [("lam", DEPTH * 4), ("lam_dot", DEPTH * 2), ("neglam", DEPTH), ("sub", DEPTH),
                              ("max", 2, 2), ("negmax", 2, 2), ("sum", 2, 2), ("rsum", 2, 2), ("nr", 2)])
        lam_dot, neglam, sub_w = m["lam_dot"], m["neglam"], m["sub"]
        s_max, neg_max, e_sum, e_rsum, neg_r = m["max"], m["negmax"], m["sum"], m["rsum"], m["nr"]

        consts_loaded, h_loaded, out_stored = sem("consts_loaded"), sem("h_loaded"), sem("out_stored")
        slot_full = [sem(f"slot_full{s}") for s in range(NS)]
        slot_done = sem("slot_done")
        hi_ready, split_ready, split_used = sem("hi_ready"), sem("split_ready"), sem("split_used")
        hid_hi_ready, hid_split_ready = sem("hid_hi_ready"), sem("hid_split_ready")
        xn32_ready, xn_hi_ready = sem("xn32_ready"), sem("xn_hi_ready")
        h_ready = sem("h_ready")
        sq_ready, sumsq_ready, std_ready, xn_ready, mix_in_ready = (
            sem(x) for x in ("sq_ready", "sumsq_ready", "std_ready", "xn_ready", "mix_in_ready"))
        gate_act_ready, gate_up_used = sem("gate_act_ready"), sem("gate_up_used")
        y_ready = sem("y_ready")
        proj_evac, swap_ready, rot_ready, v_evac = (sem(x) for x in ("proj_evac", "swap_ready", "rot_ready", "v_evac"))
        scores_ready, masked_ready, max_ready, exp_ready, attn_ready, attn_turned, attnT_ready = (
            sem(x) for x in ("scores_ready", "masked_ready", "max_ready", "exp_ready", "attn_ready", "attn_turned", "attnT_ready"))
        diff_o_ready, diff_sq_ready, diff_sum_ready, diff_std_ready = (
            sem(x) for x in ("diff_o_ready", "diff_sq_ready", "diff_sum_ready", "diff_std_ready"))
        ret_scores_ready, ret_decayed, ret_o_ready, ret_o_evac, ret_mean_ready, ret_centred, ret_sq_ready, ret_var_ready, ret_std_ready = (
            sem(x) for x in ("ret_scores_ready", "ret_decayed", "ret_o_ready", "ret_o_evac", "ret_mean_ready", "ret_centred",
                             "ret_sq_ready", "ret_var_ready", "ret_std_ready"))
        lam_dots_ready, lam_exp_ready = sem("lam_dots_ready"), sem("lam_exp_ready")
        mixed_ready = sem("mixed_ready")

        b0 = 2 * C * T
        m = layout(arena, b0, [("raw2", C, KEYS), ("x2n", C, KEYS), ("z", 4, KEYS), ("k", 4, KEYS), ("t1", 4, KEYS),
                               ("q", 2, SEQ), ("u", 2, SEQ), ("g", 2, SEQ)])
        raw2, x2n, z, hk, log_f, hq, mlp_u, hg = (m[x] for x in ("raw2", "x2n", "z", "k", "t1", "q", "u", "g"))
        at_x2n, at_z = b0 + C * KEYS, b0 + 2 * C * KEYS
        at_k, at_t1 = at_z + 4 * KEYS, at_z + 8 * KEYS
        m = layout(arena, 0, [("B", 4, SEQ), ("G", 4, SEQ), ("zv", 4, SEQ), ("kraw", 2, KEYS), ("state", 4, 64)])
        decay_b, decay_g, zv, ak, state = m["B"], m["G"], m["zv"], m["kraw"], m["state"]
        m = layout(ring, NS * SLOT, [("qraw", 4, SEQ), ("vtok", 4, P), ("va", 2, SEQ)])
        aq, av, mlp_v = m["qraw"], m["vtok"], m["va"]
        sq2 = x2n[:, 0:4]
        m = layout(arena, at_k, [("std2", KEYS), ("rstd2", KEYS), ("norm2t", 2, KEYS)])
        std2, rstd2, scaled2 = m["std2"], m["rstd2"], m["norm2t"]
        y2 = cut(arena, at_z, C, SEQ)
        m = layout(arena, at_x2n, [("lev", 2, 4, SEQ), ("S", 8, P), ("SX", 2, 4, P)])
        lev, S_acc, S_cross = m["lev"], m["S"], m["SX"]
        m = layout(arena, at_t1, [("kdT", 8, P), ("qx", 4, SEQ)])
        kdT, qx = m["kdT"], m["qx"]
        m = layout(arena, at_x2n, [("oh", 2, SEQ), ("ohsq", 2, SEQ), ("ohstd", 2 * SEQ), ("ohr", 2 * SEQ)])
        oh, oh_sq, oh_std, oh_rstd = m["oh"], m["ohsq"], m["ohstd"], m["ohr"]
        a_sq, a_std = cut(arena, at_k, 4, KEYS), cut(arena, at_t1, 4, KEYS)
        m = layout(arena, 0, [("cos", 4, SEQ), ("sin", 4, SEQ)])
        a_cos, a_sin = m["cos"], m["sin"]
        v_sq = cut(arena, 0, 8, 64)
        m = layout(arena, at_k, [("mix", 2, 2, P), ("kswap", 2, SEQ)])
        mlp_mix, k_swapped = m["mix"], m["kswap"]
        m = layout(arena, at_x2n, [("e", AHEAD, KEYS), ("eT", 2, KEYS)])
        ae, aeT = m["e"], m["eT"]
        m = layout(arena, 0, [("x2", C, SEQ), ("h2", C, SEQ)])
        x2, h2 = m["x2"], m["h2"]
        m = layout(arena, b0, [("h2t", 2, D), ("xs", C, P), ("ye", D), ("selT", SEQ)])
        h2t, xs, ye, selT = m["h2t"], m["xs"], m["ye"], m["selT"]
        m = layout(arena, at_z, [("act", FE), ("hid", FE), ("hidT", 4, P), ("sel", 2, 2, CAP), ("selg", 2, 2, CAP), ("sq3", C, SEQ), ("std3", SEQ), ("rstd3", SEQ)])
        e_act, e_hid, hidT, sel, sel_gate, sq3, std3, rstd3 = (m[x] for x in ("act", "hid", "hidT", "sel", "selg", "sq3", "std3", "rstd3"))
        m = layout(arena, at_t1 + 4 * KEYS, [
            ("lg", 2, GROUPS + E), ("gmax", 2), ("ngmax", 2), ("gsum", 2), ("gexp", 2, GROUPS), ("p", 2), ("t4", 2, GROUPS),
            ("i4", 2), ("one4", 2, GROUPS), ("em", 2, E), ("v1", 2), ("v2", 2), ("t32", 2, E), ("i32", 2), ("oh1", 2, E), ("oh2", 2, E),
            ("d", 2), ("ex", 2), ("g1", 2), ("g2", 2), ("gate", 2, E), ("chosen", 2, E), ("rank", 2, E + 2), ("most", 1)])
        R = m
        most = ctx.enter_context(nc.sbuf_tensor("most", [P, 1], mybir.dt.int32))
        w_r = cut(con, CON["decay"][0], C, GROUPS + E)
        w_sp = cut(vec, VEC["lam"][0], HEADS, P)
        MOD_AT = 64
        m = layout(small, MOD_AT, [("mod", 48, 2), ("a1", C, 2), ("a2", C), ("cc", C, 2), ("ss", 8), ("vstd", 8), ("vr", 8),
                               ("amax", AHEAD), ("anm", AHEAD), ("asum", AHEAD), ("arsum", AHEAD), ("modrow", MOD_COLS)])
        mod_row = m["modrow"][0:2]
        mod, a1, a2, cc, v_ss, v_std, v_rstd = (m[x] for x in ("mod", "a1", "a2", "cc", "ss", "vstd", "vr"))
        a_max, a_nmax, a_sum, a_rsum = (m[x] for x in ("amax", "anm", "asum", "arsum"))
        SH1, SC1, G1, SH2, SC2, G2 = (slice(C * i, C * i + C) for i in range(6))

        big_full = [sem(f"big_full{b}") for b in range(BIG_SLOTS)]
        mod_row_ready, mod_turned, mod_ready = sem("mod_row_ready"), sem("mod_turned"), sem("mod_ready")
        ctx_loaded, router_loaded, spatial_loaded = sem("ctx_loaded"), sem("router_loaded"), sem("spatial_loaded")
        cc_ready, x_ready, sq2_ready, sq2_used, std2_ready, x2n_ready = (
            sem(x) for x in ("cc_ready", "x_ready", "sq2_ready", "sq2_used", "std2_ready", "x2n_ready"))
        proj2_evac, gates_ready, scans_ready, decays_ready, kd_ready, kd_turned, kdT_ready, states_summed, state_ready, qx_ready = (
            sem(x) for x in ("proj2_evac", "gates_ready", "scans_ready", "decays_ready", "kd_ready", "kd_turned", "kdT_ready",
                             "states_summed", "state_ready", "qx_ready"))
        diff_ready, level_exp_ready, level_ready, gram_ready, gram_used = (
            sem(x) for x in ("diff_ready", "level_exp_ready", "level_ready", "gram_ready", "gram_used"))
        o2_ready, o2_sq_ready, o2_sum_ready, o2_std_ready = (sem(x) for x in ("o2_ready", "o2_sq_ready", "o2_sum_ready", "o2_std_ready"))
        v_ss_ready, v_std_ready, v_normed, mlp_mixed = (sem(x) for x in ("v_ss_ready", "v_std_ready", "v_normed", "mlp_mixed"))
        qk_sq_ready, qk_sum_ready, qk_std_ready, qk_normed, qk_swapped, qk_ready = (
            sem(x) for x in ("qk_sq_ready", "qk_sum_ready", "qk_std_ready", "qk_normed", "qk_swapped", "qk_ready"))
        s2_ready, s2_max_ready, s2_exp_ready, p2_ready, p2_turned, p2T_ready, pv2_ready = (
            sem(x) for x in ("s2_ready", "s2_max_ready", "s2_exp_ready", "p2_ready", "p2_turned", "p2T_ready", "pv2_ready"))
        y2_ready, x2_ready, sq3_ready, sum3_ready, std3_ready, h2_ready = (
            sem(x) for x in ("y2_ready", "x2_ready", "sq3_ready", "sum3_ready", "std3_ready", "h2_ready"))
        logits_ready, gmax_ready, gexp_ready, top_ready, top_exp_ready, chosen_ready, ranks_ready, most_ready = (
            sem(x) for x in ("logits_ready", "gmax_ready", "gexp_ready", "top_ready", "top_exp_ready", "chosen_ready", "ranks_ready", "most_ready"))
        h2_turned, h2t_ready, sel_ready, sel_gate_ready, gathered, xs_ready, e_act_ready, e_hid_ready = (
            sem(x) for x in ("h2_turned", "h2t_ready", "sel_ready", "sel_gate_ready", "gathered", "xs_ready", "e_act_ready", "e_hid_ready"))
        hid_turned, hidT_ready, sel_turned, selT_ready, down_ready, ye_ready, big_done, experts_done, out_ready = (
            sem(x) for x in ("hid_turned", "hidT_ready", "sel_turned", "selT_ready", "down_ready", "ye_ready", "big_done", "experts_done", "out_ready"))
        TAIL = DEPTH * MIX_SLOTS
        N_LEVELS = len(LEVELS) + 2
        UNITS = [(j, hh, i) for j in range(4) for i in range(2) for hh in range(2)]

        ident, ones, half_ones = K("ident"), K("ones"), K("half_ones")
        eps, one = K("eps"), K("one")

        def split_of(i):
            if i >= PER_ROUND - PER_ROUND % SPLITS or i >= SPLITS:
                return i % SPLITS, SPLITS
            return i, (PER_ROUND % SPLITS if i < PER_ROUND % SPLITS else SPLITS + PER_ROUND % SPLITS)

        USED_CREDITS = SPLITS + PER_ROUND % SPLITS
        SPLIT_CREDITS = PER_ROUND

        def half_of(j, k):
            return cut(ring, j * SLOT + k * HALF, C, P)

        def hid_part(f):
            return (f + 2) % C

        block = ctx.enter_context(nc.Block())

        @block.sync
        def _(sp):
            sp.dma_start(con[:, :], tables).then_inc(consts_loaded, 16)
            sp.dma_start(vec[:, :], vectors).then_inc(consts_loaded, 16)
            sp.dma_start(h, h_first).then_inc(h_loaded, 16)

            def fill(s, src):
                sp.dma_start(slot(s, SLOT)[:, :src.shape[-1]], src).then_inc(slot_full[s], 16)

            def split_away(n):
                sp.wait_ge(split_ready, 2 * n + 2)

            with sp.Fori(0, DEPTH) as l:
                used = l * MIX_SLOTS
                for i in range(2):
                    first = (2 * l + i) * FFN_SLOTS
                    for s in range(NS):
                        if i == 0:
                            split_away(first + s)
                        else:
                            sp.wait_ge(slot_done, used + MIX_SLOTS - NS + s + 1)
                        fill(s, stream_ffn[2 * l + i, s, :, :])
                    with sp.Fori(1, FFN_SLOTS // NS) as r:
                        for s in range(NS):
                            split_away(first + r * NS + s)
                            fill(s, stream_ffn[2 * l + i, r * NS + s, :, :])
                    if i == 1:
                        continue
                    for q in range(MIX_SLOTS):
                        if q < NS:
                            split_away(first + FFN_SLOTS + q)
                        else:
                            sp.wait_ge(slot_done, used + q - NS + 1)
                        if q < IN_SLOTS:
                            fill(q % NS, stream_in[l, q, :, :])
                        elif q < IN_SLOTS + MOD_MIX:
                            fill(q % NS, stream_mod[l * MOD_MIX + (q - IN_SLOTS), :, :])
                        else:
                            fill(q % NS, stream_out[l, q - IN_SLOTS - MOD_MIX, :, :])

            def tail_fill(q, src):
                if q < NS:
                    split_away(2 * DEPTH * FFN_SLOTS + q)
                else:
                    sp.wait_ge(slot_done, TAIL + q - NS + 1)
                fill(q % NS, src)

            for q in range(MOD_TAIL):
                tail_fill(q, stream_mod[DEPTH * MOD_MIX + q, :, :])
            for q in range(IN2_SLOTS):
                if q == NS - MOD_TAIL:
                    sp.wait_ge(lam_exp_ready, 1)
                    sp.dma_start(w_sp, w_spatial).then_inc(spatial_loaded, 16)
                    sp.wait_ge(h_ready, 7 * C)
                    sp.dma_start(raw2[:, :, SEQ:KEYS], ctx_in).then_inc(ctx_loaded, 16)
                    sp.dma_start(w_r, w_router).then_inc(router_loaded, 16)
                tail_fill(MOD_TAIL + q, stream_in2[q, :, :])
            for q in range(OUT_SLOTS):
                tail_fill(MOD_TAIL + IN2_SLOTS + q, stream_out2[q, :, :])
            sp.wait_ge(slot_done, TAIL + TAIL_SLOTS)
            def experts(pass_):
                with sp.Fori(0, PAIRS) as pair:
                    for b in range(BIG_SLOTS):
                        sp.wait_ge(big_done, (pass_ * PAIRS + pair) * BIG_SLOTS + b + 1)
                        sp.dma_start(cut(ring, b * BIG, BIG), stream_expert[pair, b, :, :]).then_inc(big_full[b], 16)

            experts(0)
            sp.wait_ge(most_ready, 1)
            with sp.If(sp.value_load(most[0:1, 0:1], min_val=0, max_val=SEQ) > CAP):
                with sp.Fori(1, PASSES) as pass_:
                    experts(pass_)
            for o in range(C):
                sp.wait_ge(out_ready, o + 1)
                sp.dma_start(out[:, o, :], x2[:, o]).then_inc(out_stored, 16)
            sp.wait_ge(out_stored, C * 16)

        @block.tensor
        def _(pe):
            pe.sem_inc(split_used, USED_CREDITS)
            pe.sem_inc(big_done, BIG_SLOTS)
            pe.wait_ge(consts_loaded, 32)

            def slot_loaded(s, round_):
                pe.wait_ge(slot_full[s], round_ * 16 + 16)

            def norm_sum(n, squares):
                for c in range(C):
                    pe.wait_ge(sq_ready, n * C + c + 1)
                    last = pe.matmul(ps[:, 0, 0:T], ones, squares[:, c], start=c == 0, stop=c == C - 1)
                last.then_inc(sumsq_ready, 1)

            def product(to, w, k, hi, lo, first, last_):
                pe.matmul(to, w[:, 0, k], hi, start=first, stop=False)
                pe.matmul(to, w[:, 0, k], lo, start=False, stop=False)
                return pe.matmul(to, w[:, 1, k], hi, start=False, stop=last_)

            def ffn(f, n):
                norm_sum(n, sq)
                with pe.Fori(0, GU_SLOTS // NS) as it:
                    for j in range(NS):
                        pe.wait_ge(gate_up_used, f * F + it * NS + j + 1)
                        for k in range(2):
                            i = 2 * j + k
                            pe.wait_ge(split_ready, f * HALVES + it * PER_ROUND + i + 1 + SPLIT_CREDITS)
                            w = w_split[split_of(i)[0]]
                            for c in range(C):
                                if i == 0:
                                    pe.wait_ge(xn_ready, f * C + c + 1)
                                last = product(ps[:, 2 * (j % 4) + k, 0:T], w, c, xn_hi[:, c], xn_lo[:, c], c == 0, c == C - 1)
                            last.then_inc(split_used, 1)
                at = f * HALVES + 2 * GU_SLOTS
                for i in range(F):
                    pe.wait_ge(split_ready, at + i + 1 + SPLIT_CREDITS)
                    pe.wait_ge(hid_split_ready, f * F + i + 1)
                    w = w_split[split_of(i)[0]]
                    hid_at = hid_part(i)
                    if i == 0:
                        pe.wait_ge(gate_up_used, f * F + F + 2)
                    last_pair = 2 * ((NS - 1) % 4)
                    others = [o for o in range(C) if o not in (last_pair, last_pair + 1)]
                    for o in others + [last_pair, last_pair + 1] if i == 0 else range(C):
                        if i == 0 and o == last_pair:
                            pe.wait_ge(gate_up_used, f * F + F + 3)
                        last = product(ps[:, o, 0:T], w, o, xn_hi[:, hid_at], xn_lo[:, hid_at], i == 0, i == F - 1)
                        if i == F - 1 and o < C - 1:
                            last.then_inc(y_ready, 1)
                    last.then_inc(split_used, 1)

            def mod_rows(at, q, s, loaded):
                slot_loaded(s, loaded)
                if at == 0:
                    pe.wait_ge(cc_ready, 1)
                pe.wait_ge(mod_ready, q + 1)
                w = slot(s, C, MOD_COLS)
                for c in range(C):
                    last = pe.matmul(ps[0:2, 5, 0:MOD_COLS], cc[:, c], w[:, c], start=c == 0, stop=c == C - 1)
                last.then_inc(slot_done, 1)

            def mod_turn(q):
                pe.wait_ge(mod_row_ready, q + 1)
                for i in range(2):
                    last = pe.matmul(ps[:, 5, MOD_COLS + 2 * i:MOD_COLS + 2 * i + 2], mod_row[:, i * P:i * P + P], ident[0:2, 0:2], start=True, stop=True)
                last.then_inc(mod_turned, 1)

            def mixer(l, n, round_):
                norm_sum(n, msq)
                done = []

                def features(q, tile):
                    slot_loaded(q % NS, round_ + q // NS)
                    w = slot(q % NS, 2, C, P)
                    if tile >= 4:
                        pe.wait_ge(proj_evac, l * 20 + tile - 2)
                    for i in range(2):
                        for c in range(C):
                            if tile + i == 0:
                                pe.wait_ge(mix_in_ready, l * C + c + 1)
                            last = pe.matmul(ps[:, (tile + i) % 4, 0:T], w[:, i, c], xn[:, c], start=c == 0, stop=c == C - 1)
                    last.then_inc(slot_done, 1)

                def swaps(tile):
                    for i in range(tile, tile + 2):
                        pe.wait_ge(proj_evac, l * 20 + i + 1)
                        if i >= 2:
                            pe.wait_ge(rot_ready, l * 16 + i - 1)
                        pe.matmul(ps[:, 4 if i % 2 == 0 else 7, 0:T], K("diff_swap" if i < 8 else "ret_swap"), raw[:, i % 4],
                                  start=True, stop=True).then_inc(swap_ready, 1)

                def values(q, which):
                    if which == 1:
                        pe.wait_ge(v_evac, l * 6 + 3)
                    for half in range(2):
                        s = (q + half) % NS
                        slot_loaded(s, round_ + (q + half) // NS)
                        w = slot(s, 4, 512)
                        for c in range(4):
                            for t, (t0, nt) in enumerate(TT):
                                k = 4 * half + c
                                bank = (5, 6, 4)[t]
                                last = pe.matmul(ps[0:nt, bank, 0:512], xn[:, k, t0:t0 + nt], w[:, c], start=k == 0, stop=k == C - 1)
                        last.then_inc(slot_done, 1)

                features(0, 0)
                features(1, 2)
                swaps(0)
                features(2, 4)
                swaps(2)
                features(3, 6)
                swaps(4)
                swaps(6)
                pe.wait_ge(rot_ready, l * 16 + 8)
                values(4, 0)
                features(6, 8)
                features(7, 10)
                pe.wait_ge(v_evac, l * 6 + 3)
                swaps(8)
                features(8, 12)
                swaps(10)
                features(9, 14)
                swaps(12)
                swaps(14)
                pe.wait_ge(rot_ready, l * 16 + 16)
                values(10, 1)
                features(12, 16)
                features(13, 18)
                pe.wait_ge(proj_evac, l * 20 + 20)
                pe.wait_ge(v_evac, l * 6 + 6)

                def scores(u):
                    hd, t = divmod(u, 3)
                    t0, nt = TT[t]
                    for g in range(2):
                        rows = slice(64 * g, 64 * g + 64)
                        last = pe.matmul(ps[0:nt, 2 * (u % 2) + g, 0:t0 + nt], rot[rows, hd, t0:t0 + nt],
                                         rot[rows, 4 + hd, 0:t0 + nt], start=True, stop=True)
                    last.then_inc(scores_ready, 1)

                def turn(u):
                    t0, nt = TT[u % 3]
                    pe.wait_ge(attn_ready, l * 12 + u + 1)
                    if u >= 1:
                        pe.wait_ge(attnT_ready, l * 12 + u)
                    for b in range(u % 3 + 1):
                        b0, nb = TT[b]
                        last = pe.matmul(ps[0:nb, 4, b * P:b * P + nt], a_buf[0:nt, u % 2, b0:b0 + nb],
                                         ident[0:nt, 0:nt], start=True, stop=True)
                    last.then_inc(attn_turned, 1)

                def diff_out(hd):
                    pe.wait_ge(attnT_ready, l * 12 + 3 * hd + 3)
                    if hd >= 1:
                        pe.wait_ge(diff_sq_ready, l * 4 + hd)
                    for b, (b0, nb) in enumerate(TT):
                        last = pe.matmul(ps[:, 6, b0:T], dv[0:nb, b, hd * P:hd * P + P], aT_buf[0:nb, hd % 2, b, b0:T],
                                         start=b == 0, stop=b == 2)
                    last.then_inc(diff_o_ready, 1)

                def diff_sum(hd):
                    pe.wait_ge(diff_sq_ready, l * 4 + hd + 1)
                    if hd >= 1:
                        pe.wait_ge(diff_std_ready, l * 4 + hd)
                    pe.matmul(ps[:, 7, 0:T], ones, osq, start=True, stop=True).then_inc(diff_sum_ready, 1)

                for u in range(12):
                    scores(u)
                    if u < MOD_MIX:
                        q = IN_SLOTS + u
                        mod_rows(u, l * MOD_MIX + u, q % NS, round_ + q // NS)
                    if u >= 1:
                        turn(u - 1)
                    if u >= 3 and u % 3 == 0:
                        diff_out(u // 3 - 1)
                    if u >= 3 and u % 3 == 1:
                        diff_sum(u // 3 - 1)
                    if u < MOD_MIX:
                        mod_turn(l * MOD_MIX + u)
                turn(11)
                diff_out(3)
                diff_sum(3)

                pe.wait_ge(masked_ready, l * 12 + 12)

                def ret_scores(hd):
                    if hd >= 2:
                        pe.wait_ge(ret_decayed, l * 8 + 2 * hd - 2)
                    at = 0
                    for t0, nt in TT:
                        last = pe.matmul(ps[0:nt, hd % 2, at:at + T - t0], rot[:, 12 + hd, t0:t0 + nt], rot[:, 8 + hd, t0:T],
                                         start=True, stop=True)
                        at += T - t0
                    last.then_inc(ret_scores_ready, 1)

                ret_scores(0)
                ret_scores(1)
                for first in range(0, HEADS, 2):
                    for hd in range(first, first + 2):
                        pe.wait_ge(ret_decayed, l * 8 + 2 * hd + 2)
                        at = 0
                        for b, (b0, nb) in enumerate(TT):
                            last = pe.matmul(ps[:, (2, 6)[hd % 2], b0:T], rv[0:nb, b, hd * P:hd * P + P], sT[0:nb, hd % 2, at:at + T - b0],
                                             start=b == 0, stop=b == 2)
                            at += T - b0
                        last.then_inc(ret_o_ready, 1)
                    if first + 2 < HEADS:
                        ret_scores(first + 2)
                        ret_scores(first + 3)
                    for hd in range(first, first + 2):
                        pe.wait_ge(ret_o_evac, l * 4 + hd + 1)
                        pe.matmul(ps[:, (3, 4)[hd % 2], 0:T], ones, RET[hd % 2][0], start=True, stop=True).then_inc(ret_mean_ready, 1)
                    for hd in range(first, first + 2):
                        pe.wait_ge(ret_sq_ready, l * 4 + hd + 1)
                        pe.matmul(ps[:, (7, 5)[hd % 2], 0:T], ones, RET[hd % 2][1], start=True, stop=True).then_inc(ret_var_ready, 1)

                pe.wait_ge(mixed_ready, l * 8 + 8)
                for o in range(C):
                    q = IN_SLOTS + MOD_MIX + o
                    slot_loaded(q % NS, round_ + q // NS)
                    w = slot(q % NS, C, P)
                    for c in range(C):
                        last = pe.matmul(ps[:, o, 0:T], w[:, c], y[:, c], start=c == 0, stop=c == C - 1)
                    last.then_inc(slot_done, 1)

            with pe.Fori(0, DEPTH) as l:
                ffn(2 * l, 3 * l)
                mixer(l, 3 * l + 1, l * ROUNDS + FFN_SLOTS // NS)
                ffn(2 * l + 1, 3 * l + 2)

            norm_sum(3 * DEPTH, sq)
            pe.wait_ge(h_ready, 7 * C)

            def tail_slot(q, *shape):
                slot_loaded(q % NS, DEPTH * ROUNDS + q // NS)
                return slot(q % NS, *shape)

            for q in range(MOD_TAIL):
                mod_rows(1, DEPTH * MOD_MIX + q, q, DEPTH * ROUNDS)
                mod_turn(DEPTH * MOD_MIX + q)
            for c in range(C):
                pe.wait_ge(sq2_ready, c + 1)
                pe.matmul(ps[:, 2, 0:KEYS], ones, sq2[:, c % 4], start=c == 0, stop=c == C - 1).then_inc(sq2_used, 1)

            pe.wait_ge(x2n_ready, 1)
            job = 0

            def bank():
                nonlocal job
                if job >= 8:
                    pe.wait_ge(proj2_evac, job - 7)
                job += 1
                return (job - 1) % 8

            def features(q, n, together):
                w = tail_slot(MOD_TAIL + q, 2, C, P)
                for i in range(2):
                    if i == 0 or not together:
                        b = bank()
                    at = i * n if together else 0
                    for c in range(C):
                        last = pe.matmul(ps[:, b, at:at + n], w[:, i, c], x2n[:, c, 0:n], start=c == 0, stop=c == C - 1)
                last.then_inc(slot_done, 1)

            def tokens(q, n, tiles_):
                w = tail_slot(MOD_TAIL + q, SLOT)[:, 0:C * n].rearrange("p (c n) -> p c n", c=C)
                for t in range(tiles_):
                    if t * n % 512 == 0:
                        b = bank()
                    at = t * n % 512
                    for c in range(C):
                        last = pe.matmul(ps[:, b, at:at + n], x2n[:, c, t * P:t * P + P], w[:, c], start=c == 0, stop=c == C - 1)
                last.then_inc(slot_done, 1)

            features(0, KEYS, False)
            features(1, SEQ, True)
            features(2, SEQ, True)
            tokens(3, 256, 2)
            features(4, SEQ, True)
            pe.wait_ge(qk_sq_ready, 1)
            for i in range(4):
                pe.matmul(ps[:, bank(), 0:KEYS], half_ones, a_sq[:, i], start=True, stop=True).then_inc(qk_sum_ready, 1)
            features(5, KEYS, False)
            pe.wait_ge(spatial_loaded, 16)
            pe.wait_ge(v_normed, 1)
            b = bank()
            for i in range(2):
                for t in range(2):
                    for hh in range(2):
                        head = 2 * i + hh
                        at = (2 * i + t) * P
                        last = pe.matmul(ps[64 * hh:64 * hh + 64, b, at:at + P], mlp_v[:, t, head * 64:head * 64 + 64], w_sp[:, head],
                                         start=True, stop=True)
            last.then_inc(mlp_mixed, 1)
            features(6, KEYS, False)
            pe.wait_ge(qk_normed, 1)
            for x in (aq[:, 0:2], aq[:, 2:4], ak[:, :, 0:SEQ]):
                pe.matmul(ps[:, bank(), 0:512], K("axial_swap"), x, start=True, stop=True).then_inc(qk_swapped, 1)
            tokens(7, 256, 4)
            features(8, SEQ, True)
            tokens(9, P, 4)
            features(10, SEQ, True)
            pe.wait_ge(proj2_evac, 23)

            pe.wait_ge(kd_ready, 1)
            for i in range(8):
                last = pe.matmul(ps[:, i // 4, (i % 4) * P:(i % 4) * P + P], decay_g[:, i // 2, (i % 2) * P:(i % 2) * P + P], ident,
                                 start=True, stop=True)
            last.then_inc(kd_turned, 1)
            pe.wait_ge(kdT_ready, 1)
            for i in range(4):
                for hh in range(2):
                    head = (i % 2) * 2 + hh
                    for t in range(2):
                        last = pe.matmul(ps[64 * hh:64 * hh + 64, 2, i * 64:i * 64 + 64], kdT[:, 2 * i + t, 64 * hh:64 * hh + 64],
                                         zv[:, 2 + t, head * 64:head * 64 + 64], start=t == 0, stop=t == 1)
            last.then_inc(states_summed, 1)
            pe.wait_ge(state_ready, 1)

            for n in range(N_LEVELS):
                pe.wait_ge(level_ready, n + 1)
                if n >= 2:
                    pe.wait_ge(gram_used, n - 1)
                banks = 4 * (n % 2)
                for d in range(2):
                    for i in range(2):
                        for c in range(2):
                            for hh in range(2):
                                rows = slice(64 * hh, 64 * hh + 64)
                                y_ = lev[rows, n % 2, 2 * d + i]
                                b = banks + 2 * d + hh
                                if n < len(LEVELS):
                                    left = right = y_[:, c * P:c * P + P]
                                    at = (2 * i + c) * P
                                elif n == len(LEVELS):
                                    if c == 1:
                                        continue
                                    left, right = (y_[:, 0:P], y_[:, P:2 * P]) if d == 0 else (y_[:, P:2 * P], y_[:, 0:P])
                                    at = i * P
                                else:
                                    if d == 1:
                                        continue
                                    left, right = y_[:, c * P:c * P + P], hq[rows, i, c * P:c * P + P]
                                    at = (2 * i + c) * P
                                last = pe.matmul(ps[:, b, at:at + P], left, right, start=True, stop=True)
                last.then_inc(gram_ready, 1)
            pe.wait_ge(gram_used, N_LEVELS)
            pe.wait_ge(qx_ready, 1)
            for i in range(2):
                for hh in range(2):
                    rows = slice(64 * hh, 64 * hh + 64)
                    cols = slice((2 * i + hh) * 64, (2 * i + hh) * 64 + 64)
                    b = 4 + 2 * i + hh
                    pe.matmul(ps[rows, b, 0:SEQ], state[rows, i], qx[rows, i], start=True, stop=False)
                    pe.matmul(ps[rows, b, 0:SEQ], state[rows, 2 + i], qx[rows, 2 + i], start=False, stop=False)
                    for c in range(2):
                        pe.matmul(ps[rows, b, c * P:c * P + P], zv[:, c, cols], S_acc[:, hh * 4 + 2 * i + c], start=False, stop=False)
                    pe.matmul(ps[rows, b, P:2 * P], zv[:, 0, cols], S_cross[:, 0, hh * 2 + i], start=False, stop=False)
                    last = pe.matmul(ps[rows, b, 0:P], zv[:, 1, cols], S_cross[:, 1, hh * 2 + i], start=False, stop=True)
            last.then_inc(o2_ready, 1)
            pe.wait_ge(o2_sq_ready, 1)
            pe.matmul(ps[:, 0, 0:512], half_ones, oh_sq, start=True, stop=True).then_inc(o2_sum_ready, 1)

            pe.wait_ge(qk_ready, 1)

            def scores2(n):
                j, hh, i = UNITS[n]
                rows = slice(64 * hh, 64 * hh + 64)
                if n >= AHEAD:
                    pe.wait_ge(s2_exp_ready, n - AHEAD + 1)
                pe.matmul(ps[:, 1 + n % AHEAD, 0:KEYS], aq[rows, j, i * P:i * P + P], ak[rows, j // 2, 0:KEYS], start=True, stop=True).then_inc(s2_ready, 1)

            def turn2(n):
                pe.wait_ge(p2_ready, n + 1)
                if n >= 2:
                    pe.wait_ge(p2T_ready, n - 1)
                for t in range(4):
                    last = pe.matmul(ps[:, 4 + n % 2, t * P:t * P + P], ae[:, n % AHEAD, t * P:t * P + P], ident, start=True, stop=True)
                last.then_inc(p2_turned, 1)

            def values2(n):
                j, hh, i = UNITS[n]
                pe.wait_ge(p2T_ready, n + 1)
                if n >= 2:
                    pe.wait_ge(y2_ready, 2 + n - 1)
                kv = j // 2
                for t in range(4):
                    last = pe.matmul(ps[64 * hh:64 * hh + 64, 6 + n % 2, 0:P], av[:, t, kv * 64:kv * 64 + 64], aeT[:, n % 2, t * P:t * P + P],
                                     start=t == 0, stop=t == 3)
                last.then_inc(pv2_ready, 1)

            for n in range(AHEAD - 1):
                scores2(n)
            for n in range(len(UNITS)):
                if n + AHEAD - 1 < len(UNITS):
                    scores2(n + AHEAD - 1)
                turn2(n)
                if n >= 1:
                    values2(n - 1)
            values2(len(UNITS) - 1)

            pe.wait_ge(y2_ready, 2 + len(UNITS))
            for o in range(C):
                w = tail_slot(MOD_TAIL + IN2_SLOTS + o, C, P)
                for c in range(C):
                    last = pe.matmul(ps[:, o, 0:SEQ], w[:, c], y2[:, c], start=c == 0, stop=c == C - 1)
                last.then_inc(slot_done, 1)
            for c in range(C):
                pe.wait_ge(sq3_ready, c + 1)
                last = pe.matmul(ps[:, 0, 0:SEQ], ones, sq3[:, c], start=c == 0, stop=c == C - 1)
            last.then_inc(sum3_ready, 1)
            pe.wait_ge(h2_ready, 1)
            pe.wait_ge(router_loaded, 16)
            for t in range(2):
                for c in range(C):
                    last = pe.matmul(ps[:, 1, t * 36:t * 36 + 36], h2[:, c, t * P:t * P + P], w_r[:, c], start=c == 0, stop=c == C - 1)
            last.then_inc(logits_ready, 1)
            for t in range(2):
                for c in range(C):
                    last = pe.matmul(ps[:, 4 + 2 * t + c // 4, (c % 4) * P:(c % 4) * P + P], h2[:, c, t * P:t * P + P], ident, start=True, stop=True)
            last.then_inc(h2_turned, 1)
            pe.wait_ge(chosen_ready, 1)
            pe.matmul(ps[:, 2, 0:E], K("earlier"), R["chosen"][:, 0], start=True, stop=True)
            pe.matmul(ps[:, 2, E:2 * E], ones, R["chosen"][:, 0], start=True, stop=False)
            pe.matmul(ps[:, 2, E:2 * E], K("earlier"), R["chosen"][:, 1], start=False, stop=True)
            pe.matmul(ps[:, 2, 2 * E:3 * E], ones, R["chosen"][:, 0], start=True, stop=False)
            pe.matmul(ps[:, 2, 2 * E:3 * E], ones, R["chosen"][:, 1], start=False, stop=True).then_inc(ranks_ready, 1)

            pe.wait_ge(h2t_ready, 1)
            pe.wait_ge(most_ready, 1)
            for b in range(4):
                pe.matmul(ps[:, b, 0:512], ident, ye[:, 0:512], start=True, stop=False)

            def gather(n):
                pe.wait_ge(sel_ready, n + 1)
                for c in range(C):
                    for t in range(2):
                        last = pe.matmul(ps[:, 6 + c // 4, (c % 4) * P:(c % 4) * P + P], h2t[:, t, c * P:c * P + P], sel[:, t],
                                         start=t == 0, stop=t == 1)
                    if c % 4 == 3:
                        last.then_inc(gathered, 1)

            def scatter(last_pair):
                for o in range(C):
                    last = pe.matmul(ps[:, o // 2, (o % 2) * SEQ:(o % 2) * SEQ + SEQ], ye[:, o * P:o * P + P], selT, start=False,
                                     stop=last_pair and o % 2 == 1)
                return last

            def experts(pass_):
                gather(pass_ * (PAIRS + 1))
                with pe.Fori(0, PAIRS) as pair:
                    n = pass_ * PAIRS + pair
                    g = pass_ * (PAIRS + 1) + pair
                    pe.wait_ge(xs_ready, 2 * g + 2)
                    for part in range(2):
                        pe.wait_ge((hidT_ready, selT_ready)[part], n + 1)
                        for e in range(2):
                            pe.wait_ge(big_full[2 * part + e], n * 16 + 16)
                        for c in range(C):
                            for e in range(2):
                                rows = slice(CAP * e, CAP * e + CAP)
                                last = pe.matmul(ps[rows, 4 + part, 0:FE], xs[:, c, rows], cut(ring, (2 * part + e) * BIG, C, FE)[:, c],
                                                 start=c == 0, stop=c == C - 1)
                                if c == C - 1:
                                    last.then_inc(big_done, 1)
                        if part == 0:
                            pe.wait_ge(selT_ready, n + 1)
                            pe.wait_ge(ye_ready, 2 * n + 2)
                            scatter(False)
                    gather(g + 1)
                    pe.wait_ge(e_hid_ready, n + 1)
                    for f in range(FE // P):
                        last = pe.matmul(ps[:, 4, f * P:f * P + P], e_hid[:, f * P:f * P + P], ident, start=True, stop=True)
                    last.then_inc(hid_turned, 1)
                    pe.wait_ge(sel_gate_ready, n + 1)
                    for t in range(2):
                        last = pe.matmul(ps[:, 5, t * P:t * P + P], sel_gate[:, t], ident, start=True, stop=True)
                    last.then_inc(sel_turned, 1)
                    pe.wait_ge(hidT_ready, n + 2)
                    for half in range(2):
                        pe.wait_ge(xs_ready, 2 * g + 3 + half)
                        if half == 0:
                            for e in range(2):
                                pe.wait_ge(big_full[4 + e], n * 16 + 16)
                        for f in range(FE // P):
                            for e in range(2):
                                rows = slice(CAP * e, CAP * e + CAP)
                                w = cut(ring, (4 + e) * BIG, FE // P, D)
                                last = pe.matmul(ps[rows, 6 + half, 0:512], hidT[:, f, rows], w[:, f, half * 512:half * 512 + 512],
                                                 start=f == 0, stop=f == FE // P - 1)
                                if half == 1 and f == FE // P - 1:
                                    last.then_inc(big_done, 1)
                        if half == 0:
                            last.then_inc(down_ready, 1)
                pe.wait_ge(ye_ready, (pass_ + 1) * PAIRS * 2 + 2)
                pe.wait_ge(selT_ready, (pass_ + 1) * PAIRS + 1)

            experts(0)
            with pe.If(pe.value_load(most[0:1, 0:1], min_val=0, max_val=SEQ) > CAP):
                with pe.Fori(1, PASSES) as pass_:
                    experts(pass_)
            scatter(True).then_inc(experts_done, 1)

        @block.scalar
        def _(act):
            act.wait_ge(consts_loaded, 32)
            act.wait_ge(lam_dots_ready, 1)
            nc.scalar.activation(lam_dot, lam_dot, ACT.Exp).then_inc(lam_exp_ready, 1)
            nc.scalar.activation(cc, V("c", C, 2), ACT.Silu).then_inc(cc_ready, 1)

            def norm(n, squares, std_to):
                for c in range(C):
                    act.wait_ge(h_ready, n * C + c + 1)
                    nc.scalar.activation(squares[:, c], h[:, c], ACT.Square).then_inc(sq_ready, 1)
                act.wait_ge(sumsq_ready, n + 1)
                nc.scalar.activation(std_to, ps[:, 0, 0:T], ACT.Sqrt, bias=eps, scale=1.0 / D).then_inc(std_ready, 1)

            def weights_hi(f, round_, j, loaded):
                act.wait_ge(slot_full[j], loaded * 16 + 16)
                for k in range(2):
                    b, ago = split_of(2 * j + k)
                    act.wait_ge(split_used, f * HALVES + round_ * PER_ROUND + 2 * j + k + 1 - ago + USED_CREDITS)
                    nc.scalar.activation(w_split[b][:, 0], half_of(j, k), ACT.Copy).then_inc(hi_ready, 1)

            def ffn(f, n, loaded):
                norm(n, sq, std)
                weights_hi(f, 0, 0, loaded)
                for c in range(C):
                    act.wait_ge(xn32_ready, f * C + c + 1)
                    nc.scalar.activation(xn_hi[:, c], xn32[:, c], ACT.Copy).then_inc(xn_hi_ready, 1)
                with act.Fori(0, GU_SLOTS // NS) as it:
                    for j in range(NS):
                        nxt = (j + 1) % NS
                        weights_hi(f, it + (j + 1) // NS, nxt, loaded + it + (j + 1) // NS)
                        act.wait_ge(split_used, f * HALVES + it * PER_ROUND + 2 * j + 1 + USED_CREDITS)
                        nc.scalar.activation(gate_act[:, j % 4], ps[:, 2 * (j % 4), 0:T], ACT.Silu).then_inc(gate_act_ready, 1)

                def hidden_hi(i):
                    act.wait_ge(gate_up_used, f * F + i + 1 + 3)
                    act.wait_ge(split_used, f * HALVES + 2 * GU_SLOTS + max(0, i + 1 - C) + USED_CREDITS)
                    nc.scalar.activation(xn_hi[:, hid_part(i)], hid[:, i], ACT.Copy).then_inc(hid_hi_ready, 1)

                for j in range(DOWN_SLOTS):
                    for k in range(2):
                        hidden_hi(2 * j + k)
                    if j + 1 < DOWN_SLOTS:
                        weights_hi(f, 2, j + 1, loaded + 2)

            def mod_evac(slots):
                act.wait_ge(slot_done, slots)
                nc.scalar.activation(mod_row, ps[0:2, 5, 0:MOD_COLS], ACT.Copy).then_inc(mod_row_ready, 1)

            def mixer(l, n, slots):
                norm(n, msq, mstd)

                def features(q, tile):
                    act.wait_ge(slot_done, slots + q + 1)
                    for i in range(tile, tile + 2):
                        if i < 16:
                            if i >= 4:
                                act.wait_ge(rot_ready, l * 16 + i - 3)
                            nc.scalar.activation(raw[:, i % 4], ps[:, i % 4, 0:T], ACT.Copy).then_inc(proj_evac, 1)
                        else:
                            nc.scalar.activation(rgate[:, i - 16], ps[:, i % 4, 0:T], ACT.Silu).then_inc(proj_evac, 1)

                def values(q, to):
                    act.wait_ge(slot_done, slots + q + 2)
                    for t, (_, nt) in enumerate(TT):
                        nc.scalar.activation(to[0:nt, t], ps[0:nt, (5, 6, 4)[t], 0:512], ACT.Copy).then_inc(v_evac, 1)

                for q in range(4):
                    features(q, 2 * q)
                values(4, dv)
                for q in range(6, 10):
                    features(q, 2 * q - 4)
                values(10, rv)
                for q in range(12, 14):
                    features(q, 2 * q - 8)

                def turned(u):
                    hd, t = divmod(u, 3)
                    t0, nt = TT[t]
                    act.wait_ge(attn_turned, l * 12 + u + 1)
                    if t == 0 and hd >= 2:
                        act.wait_ge(diff_o_ready, l * 4 + hd - 1)
                    full = min(t + 1, 2)
                    copy = nc.scalar.activation(aT_buf[:, hd % 2, 0:full, t0:t0 + nt],
                                                ps[:, 4, 0:full * P].rearrange("p (b i) -> p b i", b=full)[:, :, 0:nt], ACT.Copy)
                    if t == 2:
                        copy = nc.scalar.activation(aT_buf[0:META, hd % 2, 2, t0:t0 + nt], ps[0:META, 4, 2 * P:2 * P + nt], ACT.Copy)
                    copy.then_inc(attnT_ready, 1)

                def diff_evac(hd):
                    act.wait_ge(diff_o_ready, l * 4 + hd + 1)
                    if hd >= 1:
                        act.wait_ge(mixed_ready, l * 8 + hd)
                    nc.scalar.activation(o_buf, ps[:, 6, 0:T], ACT.Copy)
                    nc.scalar.activation(osq, ps[:, 6, 0:T], ACT.Square).then_inc(diff_sq_ready, 1)
                    act.wait_ge(diff_sum_ready, l * 4 + hd + 1)
                    nc.scalar.activation(ostd, ps[:, 7, 0:T], ACT.Sqrt, bias=eps, scale=1.0 / P).then_inc(diff_std_ready, 1)

                for u in range(12):
                    nt = TT[u % 3][1]
                    n_keys = TT[u % 3][0] + nt
                    act.wait_ge(max_ready, l * 12 + u + 1)
                    for g in range(2):
                        last = nc.scalar.activation(e_buf[0:nt, u % 2, g, 0:n_keys], s_buf[0:nt, u % 2, g, 0:n_keys], ACT.Exp,
                                                    bias=neg_max[0:nt, u % 2, g:g + 1], accum_out=e_sum[0:nt, u % 2, g:g + 1])
                    last.then_inc(exp_ready, 1)
                    if u < MOD_MIX:
                        mod_evac(slots + IN_SLOTS + u + 1)
                    if u >= 1:
                        turned(u - 1)
                    if u >= 3 and u % 3 == 0:
                        diff_evac(u // 3 - 1)
                turned(11)
                diff_evac(3)

                for first in range(0, HEADS, 2):
                    both = [(hd, RET[hd % 2]) for hd in range(first, first + 2)]
                    for hd, (o_, _, _, _, _, _) in both:
                        act.wait_ge(ret_o_ready, l * 4 + hd + 1)
                        act.wait_ge(mixed_ready, l * 8 + 4 + (hd - 1 if first else 0))
                        nc.scalar.activation(o_, ps[:, (2, 6)[hd % 2], 0:T], ACT.Copy).then_inc(ret_o_evac, 1)
                    for hd, (_, sq_, _, _, centred, _) in both:
                        act.wait_ge(ret_centred, l * 4 + hd + 1)
                        nc.scalar.activation(sq_, centred, ACT.Square).then_inc(ret_sq_ready, 1)
                    for hd, (_, _, std_, _, _, _) in both:
                        act.wait_ge(ret_var_ready, l * 4 + hd + 1)
                        nc.scalar.activation(std_, ps[:, (7, 5)[hd % 2], 0:T], ACT.Sqrt, bias=eps, scale=1.0 / P).then_inc(ret_std_ready, 1)

            with act.Fori(0, DEPTH) as l:
                ffn(2 * l, 3 * l, l * ROUNDS)
                mixer(l, 3 * l + 1, l * MIX_SLOTS)
                ffn(2 * l + 1, 3 * l + 2, l * ROUNDS + (FFN_SLOTS + MIX_SLOTS) // NS)

            norm(3 * DEPTH, sq, std)
            for q in range(MOD_TAIL):
                mod_evac(TAIL + q + 1)
            act.wait_ge(ctx_loaded, 16)
            for c in range(C):
                act.wait_ge(x_ready, c + 1)
                if c >= 4:
                    act.wait_ge(sq2_used, c - 3)
                nc.scalar.activation(sq2[:, c % 4], raw2[:, c], ACT.Square).then_inc(sq2_ready, 1)
            act.wait_ge(sq2_used, C)
            nc.scalar.activation(std2, ps[:, 2, 0:KEYS], ACT.Sqrt, bias=eps, scale=1.0 / D).then_inc(std2_ready, 1)

            job = 0

            def evac(q, *copies):
                nonlocal job
                act.wait_ge(slot_done, TAIL + MOD_TAIL + q + 1)
                for to, n, func in copies:
                    nc.scalar.activation(to, ps[:, job % 8, 0:n], func).then_inc(proj2_evac, 1)
                    job += 1

            def flat(a):
                return a.rearrange("p a b -> p (a b)")

            evac(0, (ak[:, 0], KEYS, ACT.Copy), (ak[:, 1], KEYS, ACT.Copy))
            evac(1, (flat(aq[:, 0:2]), 512, ACT.Copy))
            evac(2, (flat(aq[:, 2:4]), 512, ACT.Copy))
            act.drain()
            nc.scalar.activation(a_sq[:, 0:2], aq, ACT.Square)
            nc.scalar.activation(a_sq[:, 2:4], ak, ACT.Square).then_inc(qk_sq_ready, 1)
            evac(3, (flat(mlp_v), 512, ACT.Gelu_apprx_tanh))
            evac(4, (flat(mlp_u), 512, ACT.Gelu_apprx_tanh))
            act.wait_ge(v_ss_ready, 1)
            nc.scalar.activation(v_std, v_ss, ACT.Sqrt, bias=eps, scale=1.0 / 64).then_inc(v_std_ready, 1)
            for i in range(4):
                act.wait_ge(qk_sum_ready, i + 1)
                nc.scalar.activation(a_std[:, i], ps[:, job % 8, 0:KEYS], ACT.Sqrt, bias=eps, scale=1.0 / 64).then_inc(proj2_evac, 1)
                job += 1
            evac(5, (z[:, 0], KEYS, ACT.Copy), (z[:, 1], KEYS, ACT.Copy))
            act.wait_ge(mlp_mixed, 1)
            nc.scalar.activation(mlp_mix.rearrange("p a b c -> p (a b c)"), ps[:, job % 8, 0:512], ACT.Copy).then_inc(proj2_evac, 1)
            job += 1
            evac(6, (z[:, 2], KEYS, ACT.Copy), (z[:, 3], KEYS, ACT.Copy))
            for i, to in enumerate((a_sin[:, 0:2], a_sin[:, 2:4], k_swapped)):
                act.wait_ge(qk_swapped, i + 1)
                nc.scalar.activation(flat(to), ps[:, job % 8, 0:512], ACT.Copy).then_inc(proj2_evac, 1)
                job += 1
            act.wait_ge(qk_ready, 1)
            nc.scalar.activation(hk, z, ACT.Sigmoid, scale=-1.0)
            nc.scalar.activation(log_f, z, ACT.Abs)
            act.drain()
            nc.scalar.activation(log_f, log_f, ACT.Exp, scale=-1.0)
            act.drain()
            nc.scalar.activation(log_f, log_f, ACT.Ln, bias=one).then_inc(gates_ready, 1)
            evac(7, (flat(zv[:, 0:2]), 512, ACT.Copy), (flat(zv[:, 2:4]), 512, ACT.Copy))
            evac(8, (flat(hq), 512, ACT.Silu))
            evac(9, (flat(av), 512, ACT.Copy))
            evac(10, (flat(hg), 512, ACT.Silu))

            act.wait_ge(scans_ready, 1)
            nc.scalar.activation(decay_g, decay_g, ACT.Exp).then_inc(decays_ready, 1)
            nc.scalar.activation(qx[:, 0:2], decay_b[:, 0:2], ACT.Exp)
            nc.scalar.activation(qx[:, 2:4], decay_b[:, 2:4], ACT.Exp, scale=-1.0).then_inc(decays_ready, 1)
            act.wait_ge(kd_turned, 1)
            for i in range(2):
                last = nc.scalar.activation(flat(kdT[:, 4 * i:4 * i + 4]), ps[:, i, 0:512], ACT.Copy)
            last.then_inc(kdT_ready, 1)
            act.wait_ge(states_summed, 1)
            nc.scalar.activation(flat(state), ps[:, 2, 0:SEQ], ACT.Copy).then_inc(state_ready, 1)
            for n in range(N_LEVELS - 1):
                act.wait_ge(diff_ready, n + 1)
                width = 2 * LEVELS[n] if n < len(LEVELS) else SEQ
                pairs = flat(lev[:, n % 2]).rearrange("p (b s m) -> p b s m", s=2, m=width // 2)
                nc.scalar.activation(pairs[:, :, 0], pairs[:, :, 0], ACT.Exp, scale=-1.0)
                nc.scalar.activation(pairs[:, :, 1], pairs[:, :, 1], ACT.Exp).then_inc(level_exp_ready, 1)
            act.wait_ge(o2_ready, 1)
            for i in range(2):
                for hh in range(2):
                    rows = slice(64 * hh, 64 * hh + 64)
                    nc.scalar.activation(oh[rows, i], ps[rows, 4 + 2 * i + hh, 0:SEQ], ACT.Copy)
            act.drain()
            nc.scalar.activation(oh_sq, oh, ACT.Square).then_inc(o2_sq_ready, 1)
            act.wait_ge(o2_sum_ready, 1)
            nc.scalar.activation(oh_std, ps[:, 0, 0:512], ACT.Sqrt, bias=eps, scale=1.0 / 64).then_inc(o2_std_ready, 1)

            def exp2(n):
                act.wait_ge(s2_max_ready, n + 1)
                k = n % AHEAD
                nc.scalar.activation(ae[:, k], ps[:, 1 + k, 0:KEYS], ACT.Exp, bias=a_nmax[:, k:k + 1], scale=0.125,
                                     accum_out=a_sum[:, k:k + 1]).then_inc(s2_exp_ready, 1)

            for n in range(len(UNITS)):
                if n == 0:
                    for k in range(AHEAD - 1):
                        exp2(k)
                if n + AHEAD - 1 < len(UNITS):
                    exp2(n + AHEAD - 1)
                act.wait_ge(p2_turned, n + 1)
                if n >= 2:
                    act.wait_ge(pv2_ready, n - 1)
                nc.scalar.activation(aeT[:, n % 2], ps[:, 4 + n % 2, 0:512], ACT.Copy).then_inc(p2T_ready, 1)

            for c in range(C):
                act.wait_ge(x2_ready, c + 1)
                nc.scalar.activation(sq3[:, c], x2[:, c], ACT.Square).then_inc(sq3_ready, 1)
            act.wait_ge(sum3_ready, 1)
            nc.scalar.activation(std3, ps[:, 0, 0:SEQ], ACT.Sqrt, bias=eps, scale=1.0 / D).then_inc(std3_ready, 1)

            act.wait_ge(gmax_ready, 1)
            for t in range(2):
                last = nc.scalar.activation(R["gexp"][:, t], R["lg"][:, t, 0:GROUPS], ACT.Exp, bias=R["ngmax"][:, t:t + 1],
                                            accum_out=R["gsum"][:, t:t + 1])
            last.then_inc(gexp_ready, 1)
            act.wait_ge(top_ready, 1)
            nc.scalar.activation(R["ex"], R["d"], ACT.Exp).then_inc(top_exp_ready, 1)
            act.wait_ge(h2_turned, 1)
            nc.scalar.activation(h2t.rearrange("p t d -> p (t d)"), ps[:, 4:8, :].rearrange("p b n -> p (b n)"), ACT.Copy).then_inc(h2t_ready, 1)

            def gathered_tokens(n):
                for half in range(2):
                    act.wait_ge(gathered, 2 * n + half + 1)
                    nc.scalar.activation(xs[:, 4 * half:4 * half + 4], ps[:, 6 + half, 0:512].rearrange("p (c s) -> p c s", s=P), ACT.Copy).then_inc(xs_ready, 1)

            def experts(pass_):
                gathered_tokens(pass_ * (PAIRS + 1))
                with act.Fori(0, PAIRS) as pair:
                    n = pass_ * PAIRS + pair
                    act.wait_ge(big_done, n * BIG_SLOTS + BIG_SLOTS + 2)
                    nc.scalar.activation(e_act, ps[:, 4, 0:FE], ACT.Silu).then_inc(e_act_ready, 1)
                    gathered_tokens(pass_ * (PAIRS + 1) + pair + 1)
                    act.wait_ge(hid_turned, n + 1)
                    nc.scalar.activation(hidT, ps[:, 4, 0:FE].rearrange("p (f s) -> p f s", s=P), ACT.Copy).then_inc(hidT_ready, 1)
                    act.wait_ge(sel_turned, n + 1)
                    nc.scalar.activation(selT, ps[:, 5, 0:SEQ], ACT.Copy).then_inc(selT_ready, 1)
                    act.wait_ge(down_ready, n + 1)
                    nc.scalar.activation(ye[:, 0:512], ps[:, 6, 0:512], ACT.Copy).then_inc(ye_ready, 1)
                    act.wait_ge(big_done, n * BIG_SLOTS + 2 * BIG_SLOTS)
                    nc.scalar.activation(ye[:, 512:D], ps[:, 7, 0:512], ACT.Copy).then_inc(ye_ready, 1)

            experts(0)
            act.wait_ge(most_ready, 1)
            with act.If(act.value_load(most[0:1, 0:1], min_val=0, max_val=SEQ) > CAP):
                with act.Fori(1, PASSES) as pass_:
                    experts(pass_)

        @block.vector
        def _(dve):
            dve.wait_ge(consts_loaded, 32)
            pairs = V("lam", DEPTH * 2, 2, 64)
            prod = cut(arena, rest, DEPTH * 2, 64)
            nc.vector.tensor_tensor(prod, pairs[:, :, 0], pairs[:, :, 1], ALU.mult)
            dve.drain()
            nc.vector.tensor_reduce(lam_dot, prod, AX.X, ALU.add).then_inc(lam_dots_ready, 1)
            dve.wait_ge(lam_exp_ready, 1)
            for l in range(DEPTH):
                nc.vector.tensor_tensor(neglam[:, l:l + 1], lam_dot[:, 2 * l + 1:2 * l + 2], lam_dot[:, 2 * l:2 * l + 1], ALU.subtract)
                nc.vector.tensor_scalar(sub_w[:, l:l + 1], V("subln")[:, l:l + 1], 1.0 - LAMBDA_INIT[l], None, ALU.mult)
            dve.drain()
            for l in range(DEPTH):
                nc.vector.tensor_scalar(neglam[:, l:l + 1], neglam[:, l:l + 1], -LAMBDA_INIT[l], None, ALU.add)
            dve.sem_inc(split_ready, SPLIT_CREDITS)
            dve.sem_inc(mod_ready, 1)
            dve.sem_inc(gate_up_used, 3)
            dve.wait_ge(h_loaded, 16)
            dve.sem_inc(h_ready, C)

            def norm(n, std_from, rstd_to):
                dve.wait_ge(std_ready, n + 1)
                nc.vector.reciprocal(rstd_to, std_from)
                dve.drain()

            def normed(n, c, to, by):
                return nc.vector.scalar_tensor_tensor(to[:, c], h[:, c], V("norms")[:, bass.ds(n * C + c, 1)], by, ALU.mult, ALU.mult)

            def residual(ready, scale):
                for o in range(C):
                    ready(o)
                    nc.vector.scalar_tensor_tensor(h[:, o], ps[:, o, 0:T], scale, h[:, o], ALU.mult, ALU.add).then_inc(h_ready, 1)

            def weights_lo(f, round_, j):
                for k in range(2):
                    b, _ = split_of(2 * j + k)
                    dve.wait_ge(hi_ready, f * HALVES + round_ * PER_ROUND + 2 * j + k + 1)
                    nc.vector.tensor_tensor(w_split[b][:, 1], half_of(j, k), w_split[b][:, 0].bitcast(fp32), ALU.subtract).then_inc(split_ready, 1)

            def ffn(f, n):
                weights_lo(f, 0, 0)
                norm(n, std, rstd)
                for c in range(C):
                    if c == 0:
                        normed(n, 0, xn32, rstd).then_inc(xn32_ready, 1)
                    if c + 1 < C:
                        normed(n, c + 1, xn32, rstd).then_inc(xn32_ready, 1)
                    dve.wait_ge(xn_hi_ready, f * C + c + 1)
                    nc.vector.tensor_tensor(xn_lo[:, c], xn32[:, c], xn_hi[:, c].bitcast(fp32), ALU.subtract).then_inc(xn_ready, 1)
                with dve.Fori(0, GU_SLOTS // NS) as it:
                    for j in range(NS):
                        weights_lo(f, it + (j + 1) // NS, (j + 1) % NS)
                        dve.wait_ge(gate_act_ready, f * F + it * NS + j + 1)
                        dve.wait_ge(split_used, f * HALVES + it * PER_ROUND + 2 * j + 2 + USED_CREDITS)
                        to = cut(arena, rest, F * T)[:, bass.ds(it * (NS * T) + j * T, T)]
                        nc.vector.tensor_tensor(to, gate_act[:, j % 4], ps[:, 2 * (j % 4) + 1, 0:T], ALU.mult).then_inc(gate_up_used, 1)

                def hidden_lo(i):
                    dve.wait_ge(hid_hi_ready, f * F + i + 1)
                    at = hid_part(i)
                    nc.vector.tensor_tensor(xn_lo[:, at], hid[:, i], xn_hi[:, at].bitcast(fp32), ALU.subtract).then_inc(hid_split_ready, 1)

                dve.drain()
                for j in range(DOWN_SLOTS):
                    for k in range(2):
                        hidden_lo(2 * j + k)
                    if j + 1 < DOWN_SLOTS:
                        weights_lo(f, 2, j + 1)

                def ready(o):
                    if o < C - 1:
                        dve.wait_ge(y_ready, f * (C - 1) + o + 1)
                    else:
                        dve.wait_ge(split_used, f * HALVES + HALVES + USED_CREDITS)

                residual(ready, 0.5)

            def mod_bias(q):
                dve.wait_ge(mod_turned, q + 1)
                to = small[:, bass.ds(MOD_AT + 4 * q, 4)].rearrange("p (o n) -> p o n", n=2)
                bias = V("b_mod")[:, bass.ds(2 * q, 2)].unsqueeze(2).to_broadcast([P, 2, 2])
                nc.vector.tensor_tensor(to, ps[:, 5, MOD_COLS:MOD_COLS + 4].rearrange("p (o n) -> p o n", n=2), bias, ALU.add).then_inc(mod_ready, 1)

            def mixer(l, n, slots):
                norm(n, mstd, mrstd)
                for c in range(C):
                    normed(n, c, xn, mrstd).then_inc(mix_in_ready, 1)

                for i in range(16):
                    table = "diff" if i < 8 else "ret"
                    dve.wait_ge(proj_evac, l * 20 + i + 1)
                    nc.vector.tensor_tensor(t_cos[:, i % 2], raw[:, i % 4], K(table + "_cos"), ALU.mult)
                    dve.wait_ge(swap_ready, l * 16 + i + 1)
                    nc.vector.tensor_tensor(t_sin[:, i % 2], ps[:, 4 if i % 2 == 0 else 7, 0:T], K(table + "_sin"), ALU.mult)
                    dve.drain()
                    nc.vector.tensor_tensor(rot[:, i], t_cos[:, i % 2], t_sin[:, i % 2], ALU.add).then_inc(rot_ready, 1)

                def masked(u):
                    t0, nt = TT[u % 3]
                    n_keys = t0 + nt
                    dve.wait_ge(scores_ready, l * 12 + u + 1)
                    mask = K("causal")[0:nt, 2 * P - t0:2 * P - t0 + n_keys].unsqueeze(1).to_broadcast([nt, 2, n_keys])
                    at = 2 * (u % 2)
                    nc.vector.scalar_tensor_tensor(s_buf[0:nt, u % 2, :, 0:n_keys], ps[0:nt, at:at + 2, 0:n_keys], 64.0 ** -0.5,
                                                   mask, ALU.mult, ALU.add).then_inc(masked_ready, 1)
                    dve.drain()
                    nc.vector.tensor_reduce(s_max[0:nt, u % 2], s_buf[0:nt, u % 2, :, 0:n_keys], AX.X, ALU.max)
                    dve.drain()
                    nc.vector.tensor_scalar(neg_max[0:nt, u % 2], s_max[0:nt, u % 2], -1.0, None, ALU.mult).then_inc(max_ready, 1)

                def combine(u):
                    t0, nt = TT[u % 3]
                    n_keys = t0 + nt
                    dve.wait_ge(exp_ready, l * 12 + u + 1)
                    nc.vector.reciprocal(e_rsum[0:nt, u % 2], e_sum[0:nt, u % 2])
                    dve.drain()
                    nc.vector.tensor_scalar(neg_r[0:nt, u % 2:u % 2 + 1], e_rsum[0:nt, u % 2, 1:2], neglam[0:nt, bass.ds(l, 1)], None, ALU.mult)
                    if u >= 2:
                        dve.wait_ge(attn_turned, l * 12 + u - 1)
                    nc.vector.tensor_scalar(a_buf[0:nt, u % 2, 0:n_keys], e_buf[0:nt, u % 2, 0, 0:n_keys], e_rsum[0:nt, u % 2, 0:1], None, ALU.mult)
                    dve.drain()
                    nc.vector.scalar_tensor_tensor(a_buf[0:nt, u % 2, 0:n_keys], e_buf[0:nt, u % 2, 1, 0:n_keys], neg_r[0:nt, u % 2:u % 2 + 1],
                                                   a_buf[0:nt, u % 2, 0:n_keys], ALU.mult, ALU.add).then_inc(attn_ready, 1)

                def diff_norm(hd):
                    dve.wait_ge(diff_std_ready, l * 4 + hd + 1)
                    nc.vector.reciprocal(orstd, ostd)
                    dve.drain()
                    nc.vector.scalar_tensor_tensor(y[:, 4 + hd], o_buf, sub_w[:, bass.ds(l, 1)], orstd, ALU.mult, ALU.mult).then_inc(mixed_ready, 1)

                for u in range(12):
                    if u >= 1:
                        mod_bias(l * MOD_MIX + u - 1)
                    masked(u)
                    if u >= 1:
                        combine(u - 1)
                    if u >= 4 and u % 3 == 1:
                        diff_norm(u // 3 - 1)
                combine(11)
                diff_norm(3)

                def decayed(hd):
                    dve.wait_ge(ret_scores_ready, l * 4 + hd + 1)
                    if hd >= 2:
                        dve.wait_ge(ret_o_ready, l * 4 + hd - 1)
                    decay = K("decay", HEADS, DEC)[:, hd]
                    wide = DEC - META
                    nc.vector.tensor_tensor(sT[:, hd % 2, 0:wide], ps[:, hd % 2, 0:wide], decay[:, 0:wide], ALU.mult).then_inc(ret_decayed, 1)
                    nc.vector.tensor_tensor(sT[0:META, hd % 2, wide:DEC], ps[0:META, hd % 2, wide:DEC], decay[0:META, wide:DEC], ALU.mult).then_inc(ret_decayed, 1)

                decayed(0)
                decayed(1)
                for first in range(0, HEADS, 2):
                    both = [(hd, RET[hd % 2]) for hd in range(first, first + 2)]
                    for hd, (o_, _, _, _, centred, _) in both:
                        dve.wait_ge(ret_mean_ready, l * 4 + hd + 1)
                        nc.vector.scalar_tensor_tensor(centred, ps[:, (3, 4)[hd % 2], 0:T], -1.0 / P, o_, ALU.mult, ALU.add).then_inc(ret_centred, 1)
                    if first + 2 < HEADS:
                        decayed(first + 2)
                        decayed(first + 3)
                    for hd, (_, _, std_, rstd_, centred, o_norm) in both:
                        dve.wait_ge(ret_std_ready, l * 4 + hd + 1)
                        nc.vector.reciprocal(rstd_, std_)
                        dve.drain()
                        nc.vector.scalar_tensor_tensor(o_norm, centred, V("gn")[:, bass.ds(l * HEADS + hd, 1)], rstd_, ALU.mult, ALU.mult)
                        dve.drain()
                        nc.vector.tensor_tensor(y[:, hd], o_norm, rgate[:, hd], ALU.mult).then_inc(mixed_ready, 1)

                residual(lambda o: dve.wait_ge(slot_done, slots + IN_SLOTS + MOD_MIX + o + 1), 1.0)

            with dve.Fori(0, DEPTH) as l:
                ffn(2 * l, 3 * l)
                mixer(l, 3 * l + 1, l * MIX_SLOTS)
                ffn(2 * l + 1, 3 * l + 2)

            def wide(a, n, m):
                return a.unsqueeze(2).to_broadcast([P, n, m])

            def flat(a):
                return a.rearrange("p a b -> p (a b)")

            dve.wait_ge(std_ready, 3 * DEPTH + 1)
            nc.vector.reciprocal(rstd, std)
            dve.drain()
            for c in range(C):
                nc.vector.scalar_tensor_tensor(raw2[:, c, 0:SEQ], h[:, c, META:T], V("final")[:, c:c + 1], rstd[:, META:T], ALU.mult, ALU.mult).then_inc(x_ready, 1)
            for q in range(MOD_TAIL):
                mod_bias(DEPTH * MOD_MIX + q)
            nc.vector.scalar_tensor_tensor(a1, mod[:, SC1], 1.0, wide(V("norm1"), C, 2), ALU.add, ALU.mult)
            nc.vector.scalar_tensor_tensor(a2, mod[:, SC2, 0], 1.0, V("norm2"), ALU.add, ALU.mult)
            dve.wait_ge(std2_ready, 1)
            nc.vector.reciprocal(rstd2, std2)
            dve.drain()
            for c in range(C):
                nc.vector.tensor_tensor(scaled2[:, c % 2], raw2[:, c], rstd2, ALU.mult)
                dve.drain()
                for i in range(2):
                    half = slice(i * SEQ, i * SEQ + SEQ)
                    last = nc.vector.tensor_scalar(x2n[:, c, half], scaled2[:, c % 2, half], a1[:, c, i:i + 1], mod[:, c, i:i + 1], ALU.mult, ALU.add)
            last.then_inc(x2n_ready, 1)

            dve.wait_ge(proj2_evac, 5)
            vh = flat(mlp_v).rearrange("p (h d) -> p h d", d=64)
            nc.vector.tensor_tensor(v_sq, vh, vh, ALU.mult)
            dve.drain()
            nc.vector.tensor_reduce(v_ss, v_sq, AX.X, ALU.add).then_inc(v_ss_ready, 1)
            dve.wait_ge(v_std_ready, 1)
            nc.vector.reciprocal(v_rstd, v_std)
            dve.drain()
            nc.vector.tensor_tensor(vh, vh, wide(v_rstd, 8, 64), ALU.mult).then_inc(v_normed, 1)

            dve.wait_ge(proj2_evac, 10)
            nc.vector.reciprocal(a_std, a_std)
            dve.drain()
            nc.vector.scalar_tensor_tensor(flat(aq), flat(aq), V("qn"), flat(a_std[:, 0:2]), ALU.mult, ALU.mult)
            nc.vector.scalar_tensor_tensor(flat(ak), flat(ak), V("kn"), flat(a_std[:, 2:4]), ALU.mult, ALU.mult).then_inc(qk_normed, 1)

            dve.wait_ge(proj2_evac, 13)
            nc.vector.tensor_tensor(mlp_mix, mlp_mix, V("b_s", 2, P).unsqueeze(2).to_broadcast([P, 2, 2, P]), ALU.add)
            dve.drain()
            nc.vector.tensor_tensor(flat(mlp_u), flat(mlp_u), mlp_mix.rearrange("p a b c -> p (a b c)"), ALU.mult)

            def rotate(x, swapped, n):
                cos = K("axial_cos").unsqueeze(1).to_broadcast([P, n, SEQ])
                sin = K("axial_sin").unsqueeze(1).to_broadcast([P, n, SEQ])
                nc.vector.tensor_tensor(a_cos[:, 0:n], x, cos, ALU.mult)
                nc.vector.tensor_tensor(swapped, swapped, sin, ALU.mult)
                dve.drain()
                return nc.vector.tensor_tensor(x, a_cos[:, 0:n], swapped, ALU.add)

            dve.wait_ge(proj2_evac, 18)
            rotate(aq, a_sin, 4)
            dve.drain()
            rotate(ak[:, :, 0:SEQ], k_swapped, 2).then_inc(qk_ready, 1)

            dve.wait_ge(gates_ready, 1)
            nc.vector.scalar_tensor_tensor(log_f, z, 0.0, log_f, ALU.min, ALU.subtract)
            nc.vector.memset(decay_g[:, 0:2, SEQ - 1:SEQ], 0.0)
            nc.vector.memset(decay_g[:, 2:4, 0:1], 0.0)
            dve.drain()
            unit = one.to_broadcast([P, SEQ])
            for i in range(2):
                nc.vector.tensor_tensor_scan(decay_b[:, i], unit, log_f[:, i, 0:SEQ], 0.0, ALU.mult, ALU.add)
                nc.vector.tensor_tensor_scan(decay_b[:, 2 + i, ::-1], unit, log_f[:, 2 + i, 0:SEQ][:, ::-1], 0.0, ALU.mult, ALU.subtract)
                nc.vector.tensor_tensor_scan(decay_g[:, i, 0:SEQ - 1][:, ::-1], unit[:, 1:], log_f[:, i, SEQ + 1:KEYS][:, ::-1], 0.0, ALU.mult, ALU.add)
                last = nc.vector.tensor_tensor_scan(decay_g[:, 2 + i, 1:SEQ], unit[:, 1:], log_f[:, 2 + i, SEQ:KEYS - 1], 0.0, ALU.mult, ALU.add)
            last.then_inc(scans_ready, 1)
            dve.wait_ge(decays_ready, 1)
            nc.vector.tensor_tensor(decay_g, decay_g, hk[:, :, SEQ:KEYS], ALU.mult).then_inc(kd_ready, 1)
            dve.wait_ge(decays_ready, 2)
            for d in range(2):
                last = nc.vector.tensor_tensor(qx[:, 2 * d:2 * d + 2], qx[:, 2 * d:2 * d + 2], hq, ALU.mult)
            last.then_inc(qx_ready, 1)

            dve.wait_ge(slot_done, TAIL + MOD_TAIL + IN2_SLOTS)
            nc.vector.memset(S_acc, 0.0)

            def difference(n):
                if n >= 2:
                    dve.wait_ge(gram_ready, n - 1)
                half = LEVELS[n] if n < len(LEVELS) else P
                for d in range(2):
                    b = flat(decay_b[:, 2 * d:2 * d + 2]).rearrange("p (b m) -> p b m", m=2 * half)
                    to = flat(lev[:, n % 2, 2 * d:2 * d + 2]).rearrange("p (b m) -> p b m", m=2 * half)
                    at = half - 1 + d
                    last = nc.vector.tensor_tensor(to, b, b[:, :, at:at + 1].to_broadcast([P, SEQ // half, 2 * half]), ALU.subtract)
                last.then_inc(diff_ready, 1)

            def level(n):
                dve.wait_ge(level_exp_ready, n + 1)
                half = LEVELS[n] if n < len(LEVELS) else P
                for d in range(2):
                    to = lev[:, n % 2, 2 * d:2 * d + 2].rearrange("p i (b s m) -> p i b s m", s=2, m=half)
                    for side in range(2):
                        by = (hk[:, 2 * d:2 * d + 2, 0:SEQ] if side == d else hq).rearrange("p i (b s m) -> p i b s m", s=2, m=half)
                        last = nc.vector.tensor_tensor(to[:, :, :, side], to[:, :, :, side], by[:, :, :, side], ALU.mult)
                last.then_inc(level_ready, 1)

            def merge(n):
                dve.wait_ge(gram_ready, n + 1)
                banks = 4 * (n % 2)
                if n < len(LEVELS):
                    for d in range(2):
                        dve.drain()
                        mask = K("levels", 2 * len(LEVELS) + 1, P)[:, 2 * n + d].bitcast(u32).unsqueeze(1).to_broadcast([P, 8, P])
                        last = nc.vector.copy_predicated(S_acc, mask, ps[:, banks + 2 * d:banks + 2 * d + 2, :].rearrange("p b (c t) -> p (b c) t", t=P))
                elif n == len(LEVELS):
                    for d in range(2):
                        last = nc.vector.tensor_copy(S_cross[:, d].rearrange("p (b c) t -> p b (c t)", b=2), ps[:, banks + 2 * d:banks + 2 * d + 2, 0:256])
                else:
                    dve.drain()
                    mask = K("levels", 2 * len(LEVELS) + 1, P)[:, 2 * len(LEVELS)].bitcast(u32).unsqueeze(1).to_broadcast([P, 8, P])
                    last = nc.vector.copy_predicated(S_acc, mask, ps[:, banks:banks + 2, :].rearrange("p b (c t) -> p (b c) t", t=P))
                last.then_inc(gram_used, 1)

            difference(0)
            for n in range(N_LEVELS):
                if n < N_LEVELS - 1:
                    level(n)
                else:
                    dve.wait_ge(gram_ready, n - 1)
                    nc.vector.tensor_tensor(lev[:, n % 2, 0:2], hk[:, 0:2, 0:SEQ], hk[:, 2:4, 0:SEQ], ALU.add).then_inc(level_ready, 1)
                if n + 1 < N_LEVELS - 1:
                    difference(n + 1)
                if n >= 1:
                    merge(n - 1)
            merge(N_LEVELS - 1)

            dve.wait_ge(o2_std_ready, 1)
            nc.vector.reciprocal(oh_rstd, oh_std)
            dve.drain()
            nc.vector.scalar_tensor_tensor(flat(oh), flat(oh), V("hgn"), oh_rstd, ALU.mult, ALU.mult)
            dve.drain()
            nc.vector.tensor_tensor(y2[:, 6:8], oh, hg, ALU.mult).then_inc(y2_ready, 1)

            nc.vector.tensor_copy(flat(y2[:, 0:2]), flat(mlp_u)).then_inc(y2_ready, 1)

            def max2(n):
                dve.wait_ge(s2_ready, n + 1)
                k = slice(n % AHEAD, n % AHEAD + 1)
                nc.vector.tensor_reduce(a_max[:, k], ps[:, 1 + n % AHEAD, 0:KEYS], AX.X, ALU.max)
                dve.drain()
                nc.vector.tensor_scalar(a_nmax[:, k], a_max[:, k], -0.125, None, ALU.mult).then_inc(s2_max_ready, 1)

            def out2(n):
                j, hh, i = UNITS[n]
                rows = slice(64 * hh, 64 * hh + 64)
                dve.wait_ge(pv2_ready, n + 1)
                nc.vector.tensor_copy(y2[rows, 2 + j, i * P:i * P + P], ps[rows, 6 + n % 2, 0:P]).then_inc(y2_ready, 1)

            for n in range(AHEAD - 1):
                max2(n)
            for n in range(len(UNITS)):
                k = slice(n % AHEAD, n % AHEAD + 1)
                dve.wait_ge(s2_exp_ready, n + 1)
                nc.vector.reciprocal(a_rsum[:, k], a_sum[:, k])
                dve.drain()
                nc.vector.tensor_scalar(ae[:, n % AHEAD], ae[:, n % AHEAD], a_rsum[:, k], None, ALU.mult).then_inc(p2_ready, 1)
                if n + AHEAD - 1 < len(UNITS):
                    if n >= 1:
                        dve.wait_ge(p2_turned, n)
                    max2(n + AHEAD - 1)
                if n >= 1:
                    out2(n - 1)
            out2(len(UNITS) - 1)

            for o in range(C):
                dve.wait_ge(slot_done, TAIL + MOD_TAIL + IN2_SLOTS + o + 1)
                nc.vector.scalar_tensor_tensor(x2[:, o], ps[:, o, 0:SEQ], mod[:, G1, 0][:, o:o + 1], raw2[:, o, 0:SEQ], ALU.mult, ALU.add).then_inc(x2_ready, 1)
            dve.wait_ge(std3_ready, 1)
            nc.vector.reciprocal(rstd3, std3)
            dve.drain()
            for c in range(C):
                nc.vector.scalar_tensor_tensor(h2[:, c], x2[:, c], a2[:, c:c + 1], rstd3, ALU.mult, ALU.mult)
            dve.drain()
            for c in range(C):
                last = nc.vector.tensor_scalar(h2[:, c], h2[:, c], mod[:, SH2, 0][:, c:c + 1], None, ALU.add)
            last.then_inc(h2_ready, 1)

            dve.wait_ge(logits_ready, 1)
            nc.vector.tensor_tensor(R["lg"], ps[:, 1, 0:72].rearrange("p (t e) -> p t e", t=2), V("b_router").unsqueeze(1).to_broadcast([P, 2, 36]), ALU.add)
            dve.drain()
            groups = R["lg"][:, :, 0:GROUPS]
            nc.vector.tensor_reduce(R["gmax"], groups, AX.X, ALU.max)
            dve.drain()
            nc.vector.tensor_scalar(R["ngmax"], R["gmax"], -1.0, None, ALU.mult).then_inc(gmax_ready, 1)

            def first_greatest(x, top, n, index, scratch, onehot):
                iota = K("iota")[:, 0:n].unsqueeze(1).to_broadcast([P, 2, n])
                nc.vector.tensor_tensor(scratch, x, wide(top, 2, n), ALU.is_lt)
                dve.drain()
                nc.vector.scalar_tensor_tensor(scratch, scratch, 64.0, iota, ALU.mult, ALU.add)
                dve.drain()
                nc.vector.tensor_reduce(index, scratch, AX.X, ALU.min)
                dve.drain()
                nc.vector.tensor_tensor(onehot, iota, wide(index, 2, n), ALU.is_equal)
                dve.drain()

            first_greatest(groups, R["gmax"], GROUPS, R["i4"], R["t4"], R["one4"])
            nc.vector.tensor_scalar(R["t4"], R["one4"], -1.0, 1e30, ALU.add, ALU.mult)
            dve.drain()
            nc.vector.tensor_tensor(R["em"].rearrange("p t (g e) -> p t g e", g=GROUPS), R["lg"][:, :, GROUPS:].rearrange("p t (g e) -> p t g e", g=GROUPS),
                                    R["t4"].unsqueeze(3).to_broadcast([P, 2, GROUPS, PER_GROUP]), ALU.add)
            dve.drain()
            nc.vector.tensor_reduce(R["v1"], R["em"], AX.X, ALU.max)
            dve.drain()
            first_greatest(R["em"], R["v1"], E, R["i32"], R["t32"], R["oh1"])
            nc.vector.scalar_tensor_tensor(R["em"], R["oh1"], -3e30, R["em"], ALU.mult, ALU.add)
            dve.drain()
            nc.vector.tensor_reduce(R["v2"], R["em"], AX.X, ALU.max)
            dve.drain()
            nc.vector.tensor_tensor(R["d"], R["v2"], R["v1"], ALU.subtract).then_inc(top_ready, 1)
            first_greatest(R["em"], R["v2"], E, R["i32"], R["t32"], R["oh2"])
            nc.vector.tensor_tensor(R["chosen"], R["oh1"], R["oh2"], ALU.add).then_inc(chosen_ready, 1)
            dve.wait_ge(gexp_ready, 1)
            dve.wait_ge(top_exp_ready, 1)
            nc.vector.tensor_scalar(R["g1"], R["ex"], 1.0, None, ALU.add)
            dve.drain()
            nc.vector.tensor_tensor(R["g1"], R["g1"], R["gsum"], ALU.mult)
            dve.drain()
            nc.vector.reciprocal(R["g1"], R["g1"])
            dve.drain()
            nc.vector.tensor_tensor(R["g2"], R["g1"], R["ex"], ALU.mult)
            nc.vector.tensor_tensor(R["oh1"], R["oh1"], wide(R["g1"], 2, E), ALU.mult)
            dve.drain()
            nc.vector.tensor_tensor(R["oh2"], R["oh2"], wide(R["g2"], 2, E), ALU.mult)
            dve.drain()
            nc.vector.tensor_tensor(R["gate"], R["oh1"], R["oh2"], ALU.add)
            dve.drain()
            nc.vector.memset(ye, 0.0)
            nc.vector.memset(selT, 0.0)
            nc.vector.memset(R["rank"], -1.0)
            dve.wait_ge(ranks_ready, 1)
            nc.vector.tensor_reduce(R["gmax"][:, 0:1], ps[:, 2, 2 * E:3 * E], AX.X, ALU.max)
            dve.drain()
            ranks = R["rank"][:, :, 0:E]
            nc.vector.scalar_tensor_tensor(ranks, ps[:, 2, 0:2 * E].rearrange("p (t e) -> p t e", t=2), 1.0, R["chosen"], ALU.add, ALU.mult)
            nc.vector.tensor_copy(most[:, :], R["gmax"][:, 0:1])
            dve.drain()
            nc.vector.tensor_scalar(ranks, ranks, -1.0, None, ALU.add).then_inc(most_ready, 1)
            dve.drain()

            dve.sem_inc(ye_ready, 2)
            dve.sem_inc(hidT_ready, 1)
            dve.sem_inc(selT_ready, 1)
            iota = K("iota").unsqueeze(1).unsqueeze(1).to_broadcast([P, 2, 2, CAP])

            def by_slot(a, pair):
                return a[:, :, bass.ds(pair * 2, 2)].unsqueeze(3).to_broadcast([P, 2, 2, CAP])

            def select(pair):
                nc.vector.tensor_tensor(sel, iota, by_slot(R["rank"], pair), ALU.is_equal).then_inc(sel_ready, 1)

            def experts(pass_):
                select(0)
                with dve.Fori(0, PAIRS) as pair:
                    n = pass_ * PAIRS + pair
                    dve.drain()
                    dve.wait_ge(selT_ready, n + 1)
                    nc.vector.tensor_tensor(sel_gate, sel, by_slot(R["gate"], pair), ALU.mult).then_inc(sel_gate_ready, 1)
                    dve.drain()
                    dve.wait_ge(gathered, (pass_ * (PAIRS + 1) + pair) * 2 + 2)
                    select(pair + 1)
                    dve.wait_ge(e_act_ready, n + 1)
                    dve.wait_ge(big_done, n * BIG_SLOTS + BIG_SLOTS + 4)
                    nc.vector.tensor_tensor(e_hid, e_act, ps[:, 5, 0:FE], ALU.mult).then_inc(e_hid_ready, 1)

            experts(0)
            with dve.If(dve.value_load(most[0:1, 0:1], min_val=0, max_val=SEQ) > CAP):
                with dve.Fori(1, PASSES) as pass_:
                    dve.drain()
                    nc.vector.tensor_scalar(R["rank"], R["rank"], -float(CAP), None, ALU.add)
                    dve.drain()
                    dve.wait_ge(gathered, pass_ * (PAIRS + 1) * 2)
                    experts(pass_)
            dve.wait_ge(experts_done, 1)
            for o in range(C):
                nc.vector.scalar_tensor_tensor(x2[:, o], ps[:, o // 2, (o % 2) * SEQ:(o % 2) * SEQ + SEQ], mod[:, G2, 0][:, o:o + 1], x2[:, o],
                                               ALU.mult, ALU.add).then_inc(out_ready, 1)


def tiles(w, rows, cols):
    lead = w.shape[:-2]
    w = w.reshape(*lead, rows, P, cols, P)
    n = len(lead)
    return w.transpose(*range(n), n + 2, n + 1, n, n + 3)


def by_feature(a):
    return a.reshape(-1, P).T


def lay_out(x, meta_tokens, ffn1_norm, ffn1_w_gate, ffn1_w_up, ffn1_w_down, mix_norm, w_in, ret_gn_w, diff_subln_w,
            diff_lambda_q1, diff_lambda_k1, diff_lambda_q2, diff_lambda_k2, w_out, ffn2_norm, ffn2_w_gate, ffn2_w_up,
            ffn2_w_down, final_norm, c_2, ctx_2, c_ctx_2, w_mod_2, b_mod_2, norm1_w_2, w_in_2, w_s_2, b_s_2, q_norm_w_2,
            k_norm_w_2, hgrn_lb_logits_2, hgrn_norm_w_2, w_out_2, norm2_w_2, w_grp_2, b_grp_2, w_exp_2, b_exp_2, w1_2,
            w3_2, w2_2):
    f = np.float32
    ffn = np.empty((2 * DEPTH, GU_SLOTS + DOWN_SLOTS, P, SLOT), f)
    for l in range(DEPTH):
        for i, (g, u, d) in enumerate(((ffn1_w_gate, ffn1_w_up, ffn1_w_down), (ffn2_w_gate, ffn2_w_up, ffn2_w_down))):
            to = ffn[2 * l + i]
            both = to[:GU_SLOTS].reshape(F, P, 2, C, P)
            both[:, :, 0] = tiles(g[l], C, F)
            both[:, :, 1] = tiles(u[l], C, F)
            to[GU_SLOTS:] = d[l].reshape(DOWN_SLOTS, 2, P, D).transpose(0, 2, 1, 3).reshape(DOWN_SLOTS, P, SLOT)

    def features(w, first):
        w = w[:, first * P:(first + 2) * P]
        return tiles(w, C, 2).transpose(1, 0, 2, 3).reshape(P, -1)

    def rows(w, first, n):
        return w[:, first:first + n].reshape(C, P, n).transpose(1, 0, 2).reshape(P, -1)

    win = np.empty((DEPTH, IN_SLOTS, P, SLOT), f)
    for l in range(DEPTH):
        w = w_in[l]
        q = 0
        for first in (16, 18, 20, 22, "dv", 0, 2, 4, 6, "rv", 12, 14):
            if isinstance(first, str):
                v = rows(w, (24 if first == "dv" else 8) * P, 512)
                win[l, q], win[l, q + 1] = v[:, :SLOT], v[:, SLOT:]
                q += 2
            else:
                win[l, q] = features(w, first)
                q += 1
    wout = np.ascontiguousarray(tiles(w_out, C, C).reshape(DEPTH, OUT_SLOTS, P, D))

    mod = np.stack([rows(w_mod_2[0], q * MOD_COLS, MOD_COLS) for q in range(MOD_SLOTS)])
    w = w_in_2[0]
    in2 = np.zeros((IN2_SLOTS, P, SLOT), f)
    key = w[:, 1024:1152].reshape(D, 2, 1, 64)
    twice = np.concatenate([key, key], 2).reshape(D, 256)
    for q, a in enumerate((features(twice, 0), features(w, 4), features(w, 6), rows(w, 256, 256), features(w, 0),
                           features(w, 12), features(w, 14), rows(w, 2048, 256), features(w, 10), rows(w, 1152, 128), features(w, 18))):
        in2[q, :, :a.shape[1]] = a
    out2 = np.ascontiguousarray(tiles(w_out_2[0], C, C).reshape(OUT_SLOTS, P, D))
    expert = np.empty((PAIRS, BIG_SLOTS, P, BIG), f)
    up = expert[:, 0:4].reshape(PAIRS, 2, 2, P, C, FE)
    up[:, 0] = w1_2[0].reshape(PAIRS, 2, C, P, FE).transpose(0, 1, 3, 2, 4)
    up[:, 1] = w3_2[0].reshape(PAIRS, 2, C, P, FE).transpose(0, 1, 3, 2, 4)
    expert[:, 4:6] = w2_2[0].reshape(PAIRS, 2, FE // P, P, D).transpose(0, 1, 3, 2, 4).reshape(PAIRS, 2, P, BIG)

    vec = np.empty((P, N_VEC), f)

    def put(name, a):
        at, n = VEC[name]
        vec[:, at:at + n] = np.asarray(a).reshape(-1, n)

    norms = np.stack([np.stack([ffn1_norm[l], mix_norm[l], ffn2_norm[l]]) for l in range(DEPTH)])
    put("norms", by_feature(norms))
    put("final", by_feature(final_norm))
    put("gn", by_feature(ret_gn_w))
    put("subln", by_feature(diff_subln_w))
    put("lam", np.stack([diff_lambda_q1, diff_lambda_k1, diff_lambda_q2, diff_lambda_k2], 1))
    put("norm1", by_feature(norm1_w_2))
    put("norm2", by_feature(norm2_w_2))
    put("b_mod", by_feature(b_mod_2))
    put("c", np.stack([c_2.reshape(C, P).T, c_ctx_2.reshape(C, P).T], 2).reshape(P, -1))
    for name, a in (("qn", q_norm_w_2), ("kn", k_norm_w_2), ("hgn", hgrn_norm_w_2)):
        put(name, np.concatenate([a[0], a[0]])[:, None])
    put("b_s", np.repeat(b_s_2[0].reshape(2, 2, P).transpose(1, 0, 2).reshape(2, 2 * P), 64, axis=0))
    put("b_router", np.concatenate([b_grp_2, b_exp_2], 1))

    first = np.concatenate([meta_tokens, x[0]], 0)
    return {
        "stream_ffn": ffn, "stream_in": win, "stream_out": wout, "stream_mod": mod, "stream_in2": in2, "stream_out2": out2,
        "stream_expert": expert,
        "h_first": np.ascontiguousarray(first.T.reshape(C, P, T).transpose(1, 0, 2)),
        "ctx_in": np.ascontiguousarray(ctx_2[0].T.reshape(C, P, CTX).transpose(1, 0, 2)),
        "vectors": vec, "tables": constants(),
        "w_router": np.ascontiguousarray(np.concatenate([w_grp_2[0], w_exp_2[0]], 1).reshape(C, P, GROUPS + E).transpose(1, 0, 2)),
        "w_spatial": np.ascontiguousarray(w_s_2[0].transpose(2, 0, 1)),
    }


def kernel(**inputs):
    import concourse.bacc as bacc
    from concourse.bass_utils import run_bass_kernel_spmd

    arrays = lay_out(**{k: np.asarray(v) for k, v in inputs.items()})
    nc = bacc.Bacc("TRN2", target_bir_lowering=False, num_devices=1)
    aps = {name: nc.dram_tensor(name, a.shape, mybir.dt.from_np(a.dtype), kind="ExternalInput").ap() for name, a in arrays.items()}
    out = nc.dram_tensor("out", (P, C, SEQ), mybir.dt.float32, kind="ExternalOutput").ap()
    build(nc, out=out, **aps)
    result = run_bass_kernel_spmd(nc, [arrays], core_ids=[0]).results[0]["out"]
    return np.ascontiguousarray(np.asarray(result).transpose(2, 1, 0)).reshape(1, SEQ, D)
```

```python
import math
from contextlib import ExitStack

import numpy as np

import concourse.bass as bass
from concourse import mybir

P = 128
D = 1024
C = D // P
META, SEQ = 16, 256
T = META + SEQ
DEPTH = 2
FF = 2816
F = FF // P
HEADS = 4
TT = [(0, 128), (128, 128), (256, 16)]
EPS = 1e-6
LAMBDA_INIT = [0.8 - 0.6 * math.exp(-0.3 * l) for l in range(DEPTH)]

SLOT = 2048
NS = 11
GU_SLOTS, DOWN_SLOTS = F, F // 2
IN_SLOTS, OUT_SLOTS = 14, 8
MOD_SLOTS, MOD_MIX = 24, 11
MOD_COLS = SLOT // C
LAYER_SLOTS = 2 * (GU_SLOTS + DOWN_SLOTS) + IN_SLOTS + MOD_MIX + OUT_SLOTS
FFN_SLOTS = GU_SLOTS + DOWN_SLOTS
MIX_SLOTS = IN_SLOTS + MOD_MIX + OUT_SLOTS
HALF = SLOT // 2
PER_ROUND = 2 * NS
HALVES = 2 * FFN_SLOTS
ARENA = 20304
SPLITS = 4
ROUNDS = LAYER_SLOTS // NS
assert LAYER_SLOTS % NS == 0 and (GU_SLOTS + DOWN_SLOTS) % NS == 0
IN2_SLOTS = 11
MOD_TAIL = MOD_SLOTS - DEPTH * MOD_MIX
TAIL_SLOTS = MOD_TAIL + IN2_SLOTS + OUT_SLOTS

E, FE = 32, 512
GROUPS, PER_GROUP = 4, 8
BIG = 4096
BIG_SLOTS = 6
PAIRS = E // 2
CAP = P // 2
PASSES = 256 // CAP
CTX = 256
KEYS = SEQ + CTX
GRID = 64
AHEAD = 3
LEVELS = [64, 32, 16, 8, 4, 2, 1]

VEC = {}


def _columns(table, items):
    at = 0
    for name, n in items:
        table[name] = (at, n)
        at += n
    return at


N_VEC = _columns(VEC, [
    ("norms", 6 * C), ("final", C), ("gn", DEPTH * HEADS), ("subln", DEPTH), ("lam", DEPTH * 4 * 64),
    ("norm1", C), ("norm2", C), ("b_mod", 48), ("c", 2 * C), ("qn", 1), ("kn", 1), ("hgn", 1),
    ("b_s", 2 * P), ("b_router", GROUPS + E)])

CON = {}
DEC = sum(T - t for t, _ in TT)
N_CON = _columns(CON, [
    ("ones", P), ("eps", 1), ("one", 1),
    ("ret_cos", T), ("ret_sin", T), ("diff_cos", T), ("diff_sin", T), ("decay", HEADS * DEC),
    ("causal", P), ("ret_swap", P), ("diff_swap", P), ("axial_swap", P), ("ident", P),
    ("half_ones", P), ("axial_cos", SEQ), ("axial_sin", SEQ),
    ("levels", (2 * len(LEVELS) + 1) * P), ("earlier", P), ("pick", 2), ("iota", CAP)])
FIRST_CON = CON["ret_cos"][0]


def constants():
    f = np.float32
    con = np.zeros((P, N_CON), f)

    def put(name, a):
        at, n = CON[name]
        con[:, at:at + n] = np.asarray(a, f).reshape(P, n)

    pos = np.arange(T, dtype=f)
    p = np.arange(P)
    angle = (f(10000.0) ** (-np.linspace(0.0, 1.0, 64, dtype=f))).astype(f)
    freqs = (pos[:, None] * angle[None, :]).astype(f)
    put("ret_cos", np.cos(freqs).T[p // 2])
    put("ret_sin", np.sin(freqs).T[p // 2] * np.where(p % 2 == 0, -1, 1)[:, None])
    swap = np.zeros((P, P), f)
    swap[p ^ 1, p] = 1
    put("ret_swap", swap)
    inv = (f(500000.0) ** (-np.arange(0, 16, 2, dtype=f) / f(16))).astype(f)
    freqs = (pos[:, None] * inv[None, :]).astype(f)
    r = p % 64
    put("diff_cos", np.where((r < 16)[:, None], np.cos(freqs).T[r % 8], 1))
    put("diff_sin", np.where((r < 16)[:, None], np.sin(freqs).T[r % 8] * np.where(r < 8, -1, 1)[:, None], 0))
    swap = np.zeros((P, P), f)
    swap[np.where(r < 8, p + 8, np.where(r < 16, p - 8, p)), p] = 1
    put("diff_swap", swap)
    inv = (f(1.0) / (f(10000.0) ** (np.arange(0, 32, 2, dtype=f) / f(32)))).astype(f)
    t = np.arange(SEQ)
    axes = np.stack([t // GRID, t % GRID]).astype(f)
    ang = (axes[r // 32] * inv[r % 16][:, None]).astype(f)
    put("axial_cos", np.cos(ang))
    put("axial_sin", np.sin(ang) * np.where(r % 32 < 16, -1, 1)[:, None])
    swap = np.zeros((P, P), f)
    swap[np.where(r % 32 < 16, p + 16, p - 16), p] = 1
    put("axial_swap", swap)
    log_gamma = np.log(f(1.0) - f(2.0) ** (f(-5.0) - np.arange(HEADS, dtype=f))).astype(f)
    parts = []
    for h in range(HEADS):
        for t0, n in TT:
            rel = (np.arange(t0, T)[None, :] - (t0 + p)[:, None]).astype(f)
            parts.append(np.where(rel >= 0, np.exp(log_gamma[h] * np.maximum(rel, 0)), 0) * f(P ** -0.5))
    put("decay", np.concatenate(parts, 1))
    put("causal", np.where(p[None, :] <= p[:, None], 0, -1e30 * 64.0 ** 0.5))
    put("ident", np.eye(P))
    put("ones", np.ones((P, P)))
    put("half_ones", p[:, None] // 64 == p[None, :] // 64)
    s, q = p[:, None], p[None, :]
    masks = []
    for m in LEVELS:
        ahead = (s // (2 * m) == q // (2 * m)) & (s // m % 2 == 0) & (q // m % 2 == 1)
        masks += [ahead, ahead.T]
    put("levels", np.concatenate(masks + [s == q], 1))
    put("earlier", s < q)
    put("pick", p[:, None] % 32 == np.arange(2)[None, :])
    put("iota", np.broadcast_to(np.arange(CAP), (P, CAP)))
    put("eps", np.full((P, 1), EPS))
    put("one", np.ones((P, 1)))
    return con


def build(nc, stream_ffn, stream_in, stream_out, stream_mod, stream_in2, stream_out2, stream_expert,
          h_first, ctx_in, vectors, tables, w_router, w_spatial, out):
    fp32, u32, f32r = mybir.dt.float32, mybir.dt.uint32, mybir.dt.float32r
    ALU, ACT, AX = mybir.AluOpType, mybir.ActivationFunctionType, mybir.AxisListType

    with ExitStack() as ctx:
        def sb(name, shape, dt=fp32):
            return ctx.enter_context(nc.sbuf_tensor(name, shape, dt))

        def sem(name):
            return ctx.enter_context(nc.semaphore(name))

        ring = sb("ring", [P, 12 * SLOT])
        ring_at = nc.sbuf_base - 4 * 12 * SLOT
        arena = sb("arena", [P, ARENA])
        arena_at = nc.sbuf_base - 4 * ARENA
        vec = sb("vec", [P, N_VEC])
        con = sb("con", [P, N_CON])
        small = sb("small", [P, 736])
        ps = ctx.enter_context(nc.psum_tensor("ps", [P, 8, 512], fp32))

        def cut(tensor, at, *shape):
            n = int(np.prod(shape))
            piece = tensor[:, at:at + n]
            if len(shape) == 1:
                return piece
            names = "abcd"[:len(shape)]
            sizes = dict(zip(names[1:], shape[1:]))
            return piece.rearrange(f"p ({' '.join(names)}) -> p {' '.join(names)}", **sizes)

        def layout(tensor, at, items):
            found = {}
            for name, *shape in items:
                found[name] = cut(tensor, at, *shape)
                at += int(np.prod(shape))
            assert at <= tensor.shape[1], (at, tensor.shape)
            return found

        def V(name, *shape):
            at, n = VEC[name]
            return cut(vec, at, *(shape or (n,)))

        def K(name, *shape):
            at, n = CON[name]
            return cut(con, at, *(shape or (n,)))

        def slot(s, *shape):
            return cut(ring, s * SLOT, *shape)

        def parts(name, byte, *shape):
            n = int(np.prod(shape))
            return cut(nc.alloc_sbuf_tensor_at(name, [P, n], f32r, offset=byte), 0, *shape)

        m = layout(arena, 0, [("h", C, T), ("xn", C, T), ("rest", 1)])
        h, xn = m["h"], m["xn"]
        rest = 2 * C * T
        m = layout(arena, rest, [("hid", F, T), ("gate", 4, T), ("sq", C, T), ("std", T), ("rstd", T)])
        hid, gate_act, sq, std, rstd = m["hid"], m["gate"], m["sq"], m["std"], m["rstd"]
        xn_hi = parts("xn_hi", arena_at + 4 * C * T, C, T)
        xn_lo = parts("xn_lo", arena_at + 4 * (rest + F * T + 4 * T), C, T)
        hid0 = parts("hid0", arena_at + 4 * (rest + F * T + 4 * T + C * T), 2, T)
        w_split = [parts(f"w_split{b}", ring_at + 4 * NS * SLOT if b == 0 else arena_at + 4 * (ARENA - b * SLOT), 2, C, P)
                   for b in range(SPLITS)]
        assert rest + F * T + 4 * T + C * T + 2 * T <= ARENA - (SPLITS - 1) * SLOT
        xn32 = cut(arena, rest + (F - C) * T, C, T)
        m = layout(arena, rest, [
            ("rot", 16, T), ("raw", 4, T), ("rgate", HEADS, T), ("dv", 3, 512), ("rv", 3, 512),
            ("s", 2, 2, T), ("e", 2, 2, T), ("a", 2, T), ("aT", 2, 3, T), ("o", T), ("osq", T),
            ("ostd", T), ("orstd", T), ("retstd", T)])
        rot, raw, rgate, dv, rv = m["rot"], m["raw"], m["rgate"], m["dv"], m["rv"]
        s_buf, e_buf, a_buf, aT_buf = m["s"], m["e"], m["a"], m["aT"]
        o_buf, osq, ostd, orstd, ret_std = m["o"], m["osq"], m["ostd"], m["orstd"], m["retstd"]
        at = arena_at + 4 * (rest + 28 * T + 6 * 512)
        mix_hi, mix_lo = parts("mix_hi", at, C, T), parts("mix_lo", at + 4 * C * T, C, T)
        assert rest + 28 * T + 6 * 512 + 2 * C * T <= ARENA and 4 * T >= HALF
        tile_split = [(w_split[0][:, 0], w_split[0][:, 1]),
                      (parts("tile_hi", arena_at + 4 * (rest + 20 * T), C, P), parts("tile_lo", arena_at + 4 * (rest + 24 * T + 3 * 512), C, P))]
        m = layout(arena, rest + 16 * T, [("sT", DEC), ("o", T), ("osq", T)])
        sT, ret_o, ret_sq = m["sT"], m["o"], m["osq"]
        t_cos, t_sin = s_buf[:, 0], s_buf[:, 1]
        m = layout(arena, rest + 28 * T + 6 * 512, [("sq", C, T), ("lo", C, T), ("std", T), ("rstd", T)])
        msq, mstd, mrstd = m["sq"], m["std"], m["rstd"]
        y = xn

        lam_prod = cut(arena, rest, DEPTH, 4, 64)
        m = layout(small, 0, [("lam", DEPTH * 4), ("lam_dot", DEPTH * 2), ("neglam", DEPTH), ("sub", DEPTH),
                              ("max", 2, 2), ("negmax", 2, 2), ("sum", 2, 2), ("rsum", 2, 2), ("nr", 2)])
        lam_dot, neglam, sub_w = m["lam_dot"], m["neglam"], m["sub"]
        s_max, neg_max, e_sum, e_rsum, neg_r = m["max"], m["negmax"], m["sum"], m["rsum"], m["nr"]

        consts_loaded, tables_loaded, h_loaded, out_stored = sem("consts_loaded"), sem("tables_loaded"), sem("h_loaded"), sem("out_stored")
        slot_full = [sem(f"slot_full{s}") for s in range(NS)]
        slot_done = sem("slot_done")
        hi_ready, split_ready, split_used = sem("hi_ready"), sem("split_ready"), sem("split_used")
        hid_hi_ready, hid_split_ready = sem("hid_hi_ready"), sem("hid_split_ready")
        xn32_ready, xn_hi_ready = sem("xn32_ready"), sem("xn_hi_ready")
        mix_hi_ready, mix_split_ready, tile_hi_ready, tile_ready, tile_used = (
            sem(x) for x in ("mix_hi_ready", "mix_split_ready", "tile_hi_ready", "tile_ready", "tile_used"))
        h_ready = sem("h_ready")
        sq_ready, sumsq_ready, std_ready, xn_ready, mix_in_ready = (
            sem(x) for x in ("sq_ready", "sumsq_ready", "std_ready", "xn_ready", "mix_in_ready"))
        gate_act_ready, gate_up_used = sem("gate_act_ready"), sem("gate_up_used")
        y_ready = sem("y_ready")
        proj_evac, swap_ready, rot_ready, v_evac = (sem(x) for x in ("proj_evac", "swap_ready", "rot_ready", "v_evac"))
        scores_ready, max_ready, exp_ready, attn_ready, attn_turned, attnT_ready = (
            sem(x) for x in ("scores_ready", "max_ready", "exp_ready", "attn_ready", "attn_turned", "attnT_ready"))
        diff_o_ready, diff_sq_ready, diff_sum_ready, diff_std_ready = (
            sem(x) for x in ("diff_o_ready", "diff_sq_ready", "diff_sum_ready", "diff_std_ready"))
        ret_scores_ready, ret_decayed, ret_o_ready, ret_o_evac, ret_mean_ready, ret_centred, ret_sq_ready, ret_var_ready, ret_std_ready = (
            sem(x) for x in ("ret_scores_ready", "ret_decayed", "ret_o_ready", "ret_o_evac", "ret_mean_ready", "ret_centred",
                             "ret_sq_ready", "ret_var_ready", "ret_std_ready"))
        lam_dots_ready, lam_exp_ready = sem("lam_dots_ready"), sem("lam_exp_ready")
        diff_mixed, ret_mixed = sem("diff_mixed"), sem("ret_mixed")

        b0 = 2 * C * T
        m = layout(arena, b0, [("raw2", C, KEYS), ("x2n", C, KEYS), ("z", 4, KEYS), ("k", 4, KEYS), ("t1", 4, KEYS),
                               ("q", 2, SEQ), ("u", 2, SEQ), ("g", 2, SEQ)])
        raw2, x2n, z, hk, log_f, hq, mlp_u, hg = (m[x] for x in ("raw2", "x2n", "z", "k", "t1", "q", "u", "g"))
        at_x2n, at_z = b0 + C * KEYS, b0 + 2 * C * KEYS
        at_k, at_t1 = at_z + 4 * KEYS, at_z + 8 * KEYS
        m = layout(arena, 0, [("B", 4, SEQ), ("G", 4, SEQ), ("zv", 4, SEQ), ("kraw", 2, KEYS), ("state", 4, 64)])
        decay_b, decay_g, zv, ak, state = m["B"], m["G"], m["zv"], m["kraw"], m["state"]
        m = layout(ring, NS * SLOT, [("qraw", 4, SEQ), ("vtok", 4, P), ("va", 2, SEQ)])
        aq, av, mlp_v = m["qraw"], m["vtok"], m["va"]
        sq2 = x2n[:, 0:4]
        m = layout(arena, 0, [("std2", KEYS), ("rstd2", KEYS)])
        std2, rstd2 = m["std2"], m["rstd2"]
        scaled2 = cut(arena, at_z, C, KEYS)
        y2 = cut(arena, at_z, C, SEQ)
        m = layout(arena, at_x2n, [("lev", 2, 4, SEQ), ("S", 8, P), ("SX", 2, 4, P)])
        lev, S_acc, S_cross = m["lev"], m["S"], m["SX"]
        m = layout(arena, at_t1, [("kdT", 8, P), ("qx", 4, SEQ)])
        kdT, qx = m["kdT"], m["qx"]
        m = layout(arena, at_x2n, [("oh", 2, SEQ), ("ohsq", 2, SEQ), ("ohstd", 2 * SEQ), ("ohr", 2 * SEQ)])
        oh, oh_sq, oh_std, oh_rstd = m["oh"], m["ohsq"], m["ohstd"], m["ohr"]
        a_sq, a_std = cut(arena, at_k, 4, KEYS), cut(arena, at_t1, 4, KEYS)
        m = layout(arena, 0, [("cos", 4, SEQ), ("sin", 4, SEQ)])
        a_cos, a_sin = m["cos"], m["sin"]
        v_sq = cut(arena, 0, 8, 64)
        m = layout(arena, at_k, [("mix", 2, 2, P), ("kswap", 2, SEQ)])
        mlp_mix, k_swapped = m["mix"], m["kswap"]
        m = layout(arena, at_x2n, [("e", AHEAD, KEYS), ("eT", 2, KEYS)])
        ae, aeT = m["e"], m["eT"]
        m = layout(arena, 0, [("x2", C, SEQ), ("h2", C, SEQ)])
        x2, h2 = m["x2"], m["h2"]
        m = layout(arena, b0, [("h2t", 2, D), ("xs", C, P), ("ye", D), ("selT", SEQ)])
        h2t, xs, ye, selT = m["h2t"], m["xs"], m["ye"], m["selT"]
        m = layout(arena, at_z, [("act", FE), ("hid", FE), ("hidT", 4, P), ("sel", 2, 2, CAP), ("selg", 2, 2, CAP), ("sq3", C, SEQ), ("std3", SEQ), ("rstd3", SEQ)])
        e_act, e_hid, hidT, sel, sel_gate, sq3, std3, rstd3 = (m[x] for x in ("act", "hid", "hidT", "sel", "selg", "sq3", "std3", "rstd3"))
        m = layout(arena, at_t1 + 4 * KEYS, [
            ("lg", 2, GROUPS + E), ("gmax", 2), ("ngmax", 2), ("gsum", 2), ("gexp", 2, GROUPS), ("p", 2), ("t4", 2, GROUPS),
            ("i4", 2), ("one4", 2, GROUPS), ("em", 2, E), ("v1", 2), ("v2", 2), ("t32", 2, E), ("i32", 2), ("oh1", 2, E), ("oh2", 2, E),
            ("d", 2), ("ex", 2), ("g1", 2), ("g2", 2), ("gate", 2, E), ("chosen", 2, E), ("rank", 2, E + 2), ("most", 1)])
        R = m
        most = ctx.enter_context(nc.sbuf_tensor("most", [P, 1], mybir.dt.int32))
        w_r = cut(con, CON["decay"][0], C, GROUPS + E)
        w_sp = cut(vec, VEC["lam"][0], HEADS, P)
        MOD_AT = 64
        m = layout(small, MOD_AT, [("mod", 48, 2), ("a1", C, 2), ("a2", C), ("cc", C, 32), ("ss", 8), ("vstd", 8), ("vr", 8),
                               ("amax", AHEAD), ("anm", AHEAD), ("asum", AHEAD), ("arsum", AHEAD), ("modrow", MOD_COLS)])
        mod_row = m["modrow"]
        mod, a1, a2, cc, v_ss, v_std, v_rstd = (m[x] for x in ("mod", "a1", "a2", "cc", "ss", "vstd", "vr"))
        a_max, a_nmax, a_sum, a_rsum = (m[x] for x in ("amax", "anm", "asum", "arsum"))
        SH1, SC1, G1, SH2, SC2, G2 = (slice(C * i, C * i + C) for i in range(6))

        big_full = [sem(f"big_full{b}") for b in range(BIG_SLOTS)]
        mod_row_ready, mod_turned, mod_ready = sem("mod_row_ready"), sem("mod_turned"), sem("mod_ready")
        ctx_loaded, router_loaded, spatial_loaded = sem("ctx_loaded"), sem("router_loaded"), sem("spatial_loaded")
        cc_ready, x_ready, sq2_ready, sq2_used, std2_ready, x2_scaled, x2n_ready = (
            sem(x) for x in ("cc_ready", "x_ready", "sq2_ready", "sq2_used", "std2_ready", "x2_scaled", "x2n_ready"))
        proj2_evac, gates_ready, scans_ready, decays_ready, kd_ready, kd_turned, kdT_ready, states_summed, state_ready, qx_ready = (
            sem(x) for x in ("proj2_evac", "gates_ready", "scans_ready", "decays_ready", "kd_ready", "kd_turned", "kdT_ready",
                             "states_summed", "state_ready", "qx_ready"))
        diff_ready, level_exp_ready, level_ready, gram_ready, gram_used = (
            sem(x) for x in ("diff_ready", "level_exp_ready", "level_ready", "gram_ready", "gram_used"))
        o2_ready, o2_sq_ready, o2_sum_ready, o2_std_ready = (sem(x) for x in ("o2_ready", "o2_sq_ready", "o2_sum_ready", "o2_std_ready"))
        v_ss_ready, v_std_ready, v_normed, mlp_mixed = (sem(x) for x in ("v_ss_ready", "v_std_ready", "v_normed", "mlp_mixed"))
        qk_sq_ready, qk_sum_ready, qk_normed, qk_swapped, qk_ready = (
            sem(x) for x in ("qk_sq_ready", "qk_sum_ready", "qk_normed", "qk_swapped", "qk_ready"))
        s2_ready, s2_max_ready, s2_exp_ready, p2_ready, p2_turned, p2T_ready, pv2_ready = (
            sem(x) for x in ("s2_ready", "s2_max_ready", "s2_exp_ready", "p2_ready", "p2_turned", "p2T_ready", "pv2_ready"))
        y2_ready, x2_ready, sq3_ready, sum3_ready, std3_ready, h2_scaled, h2_ready = (
            sem(x) for x in ("y2_ready", "x2_ready", "sq3_ready", "sum3_ready", "std3_ready", "h2_scaled", "h2_ready"))
        logits_ready, gmax_ready, gexp_ready, top_ready, top_exp_ready, chosen_ready, ranks_ready, most_ready = (
            sem(x) for x in ("logits_ready", "gmax_ready", "gexp_ready", "top_ready", "top_exp_ready", "chosen_ready", "ranks_ready", "most_ready"))
        h2_turned, h2t_ready, sel_ready, sel_gate_ready, gathered, xs_ready, e_act_ready, e_hid_ready = (
            sem(x) for x in ("h2_turned", "h2t_ready", "sel_ready", "sel_gate_ready", "gathered", "xs_ready", "e_act_ready", "e_hid_ready"))
        hid_turned, hidT_ready, sel_turned, selT_ready, down_ready, ye_ready, big_done, experts_done, out_ready = (
            sem(x) for x in ("hid_turned", "hidT_ready", "sel_turned", "selT_ready", "down_ready", "ye_ready", "big_done", "experts_done", "out_ready"))
        TAIL = DEPTH * MIX_SLOTS
        N_LEVELS = len(LEVELS) + 2
        UNITS = [(j, hh, i) for j in range(4) for i in range(2) for hh in range(2)]

        ident, ones, half_ones = K("ident"), K("ones"), K("half_ones")
        eps, one = K("eps"), K("one")

        def split_of(i):
            if i >= SPLITS:
                return i % SPLITS, SPLITS
            return i, (PER_ROUND % SPLITS if i < PER_ROUND % SPLITS else SPLITS + PER_ROUND % SPLITS)

        ROTATED = 2 * HEADS + 2 * HEADS
        USED_CREDITS = SPLITS + PER_ROUND % SPLITS
        SPLIT_CREDITS = PER_ROUND

        def half_of(j, k):
            return cut(ring, j * SLOT + k * HALF, C, P)

        def hid_split(f):
            return (hid0[:, 0], hid0[:, 1]) if f == 0 else (xn_hi[:, (f + 2) % C], xn_lo[:, (f + 2) % C])

        block = ctx.enter_context(nc.Block())

        @block.sync
        def _(sp):
            sp.dma_start(con[:, 0:FIRST_CON], tables[:, 0:FIRST_CON]).then_inc(consts_loaded, 16)
            sp.dma_start(h, h_first).then_inc(h_loaded, 16)
            sp.dma_start(vec[:, :], vectors).then_inc(consts_loaded, 16)

            def fill(s, src):
                sp.dma_start(slot(s, SLOT)[:, :src.shape[-1]], src).then_inc(slot_full[s], 16)

            def split_away(n):
                sp.wait_ge(split_ready, 2 * n + 2)

            with sp.Fori(0, DEPTH) as l:
                used = l * MIX_SLOTS
                for i in range(2):
                    first = (2 * l + i) * FFN_SLOTS
                    for s in range(NS):
                        if i == 0:
                            split_away(first + s)
                        else:
                            sp.wait_ge(slot_done, used + MIX_SLOTS - NS + s + 1)
                        fill(s, stream_ffn[2 * l + i, s, :, :])
                    with sp.Fori(1, FFN_SLOTS // NS) as r:
                        for s in range(NS):
                            split_away(first + r * NS + s)
                            fill(s, stream_ffn[2 * l + i, r * NS + s, :, :])
                    if i == 1:
                        continue
                    for q in range(MIX_SLOTS):
                        if q < NS:
                            split_away(first + FFN_SLOTS + q)
                        else:
                            sp.wait_ge(slot_done, used + q - NS + 1)
                        if q < IN_SLOTS:
                            fill(q % NS, stream_in[l, q, :, :])
                        elif q < IN_SLOTS + MOD_MIX:
                            fill(q % NS, stream_mod[l * MOD_MIX + (q - IN_SLOTS), :, :])
                        else:
                            fill(q % NS, stream_out[l, q - IN_SLOTS - MOD_MIX, :, :])

            def tail_fill(q, src):
                if q < NS:
                    split_away(2 * DEPTH * FFN_SLOTS + q)
                else:
                    sp.wait_ge(slot_done, TAIL + q - NS + 1)
                fill(q % NS, src)

            for q in range(MOD_TAIL):
                tail_fill(q, stream_mod[DEPTH * MOD_MIX + q, :, :])
            for q in range(IN2_SLOTS):
                if q == NS - MOD_TAIL:
                    sp.wait_ge(lam_exp_ready, 1)
                    sp.dma_start(w_sp, w_spatial).then_inc(spatial_loaded, 16)
                    sp.wait_ge(h_ready, 7 * C)
                    sp.dma_start(raw2[:, :, SEQ:KEYS], ctx_in).then_inc(ctx_loaded, 16)
                    sp.dma_start(w_r, w_router).then_inc(router_loaded, 16)
                tail_fill(MOD_TAIL + q, stream_in2[q, :, :])
            for q in range(OUT_SLOTS):
                tail_fill(MOD_TAIL + IN2_SLOTS + q, stream_out2[q, :, :])
            sp.wait_ge(slot_done, TAIL + TAIL_SLOTS)
            def experts(pass_):
                with sp.Fori(0, PAIRS) as pair:
                    for b in range(BIG_SLOTS):
                        sp.wait_ge(big_done, (pass_ * PAIRS + pair) * BIG_SLOTS + b + 1)
                        sp.dma_start(cut(ring, b * BIG, BIG), stream_expert[pair, b, :, :]).then_inc(big_full[b], 16)

            experts(0)
            sp.wait_ge(most_ready, 1)
            with sp.If(sp.value_load(most[0:1, 0:1], min_val=0, max_val=SEQ) > CAP):
                with sp.Fori(1, PASSES) as pass_:
                    experts(pass_)
            for o in range(C):
                sp.wait_ge(out_ready, o + 1)
                sp.dma_start(out[:, o, :], x2[:, o]).then_inc(out_stored, 16)
            sp.wait_ge(out_stored, C * 16)

        @block.tensor
        def _(pe):
            pe.sem_inc(split_used, USED_CREDITS)
            pe.sem_inc(big_done, BIG_SLOTS)
            pe.wait_ge(consts_loaded, 32)

            def slot_loaded(s, round_):
                pe.wait_ge(slot_full[s], round_ * 16 + 16)

            def norm_sum(n, squares):
                for c in range(C):
                    pe.wait_ge(sq_ready, n * C + c + 1)
                    last = pe.matmul(ps[:, 0, 0:T], ones, squares[:, c], start=c == 0, stop=c == C - 1)
                last.then_inc(sumsq_ready, 1)

            def product(to, w, k, hi, lo, first, last_):
                pe.matmul(to, w[:, 0, k], hi, start=first, stop=False)
                pe.matmul(to, w[:, 0, k], lo, start=False, stop=False)
                return pe.matmul(to, w[:, 1, k], hi, start=False, stop=last_)

            def ffn(f, n):
                norm_sum(n, sq)
                with pe.Fori(0, GU_SLOTS // NS) as it:
                    for j in range(NS):
                        pe.wait_ge(gate_up_used, f * F + it * NS + j + 1)
                        for k in range(2):
                            i = 2 * j + k
                            pe.wait_ge(split_ready, f * HALVES + it * PER_ROUND + i + 1 + SPLIT_CREDITS)
                            w = w_split[split_of(i)[0]]
                            for c in range(C):
                                if i == 0:
                                    pe.wait_ge(xn_ready, f * C + c + 1)
                                last = product(ps[:, 2 * (j % 4) + k, 0:T], w, c, xn_hi[:, c], xn_lo[:, c], c == 0, c == C - 1)
                            last.then_inc(split_used, 1)
                at = f * HALVES + 2 * GU_SLOTS
                for i in range(F):
                    pe.wait_ge(split_ready, at + i + 1 + SPLIT_CREDITS)
                    pe.wait_ge(hid_split_ready, f * F + i + 1)
                    w = w_split[split_of(i)[0]]
                    hi, lo = hid_split(i)
                    if i == 0:
                        pe.wait_ge(gate_up_used, f * F + F + 2)
                    last_pair = 2 * ((NS - 1) % 4)
                    others = [o for o in range(C) if o not in (last_pair, last_pair + 1)]
                    for o in others + [last_pair, last_pair + 1] if i == 0 else range(C):
                        if i == 0 and o == last_pair:
                            pe.wait_ge(gate_up_used, f * F + F + 3)
                        last = product(ps[:, o, 0:T], w, o, hi, lo, i == 0, i == F - 1)
                        if i == F - 1 and o < C - 1:
                            last.then_inc(y_ready, 1)
                    last.then_inc(split_used, 1)

            def mod_rows(at, q, s, loaded):
                slot_loaded(s, loaded)
                if at == 0:
                    pe.wait_ge(cc_ready, 1)
                pe.wait_ge(mod_ready, q + 1)
                w = slot(s, C, MOD_COLS)
                for c in range(C):
                    last = pe.matmul(ps[32 * (c % 4):32 * (c % 4) + 32, 5, 0:MOD_COLS], cc[:, c], w[:, c], start=c < 4, stop=c >= C - 4)
                last.then_inc(slot_done, 1)

            def mod_turn(q):
                pe.wait_ge(mod_row_ready, q + 1)
                for i in range(2):
                    last = pe.matmul(ps[:, 5, MOD_COLS + 2 * i:MOD_COLS + 2 * i + 2], mod_row[:, i * P:i * P + P], K("pick"), start=True, stop=True)
                last.then_inc(mod_turned, 1)

            def mixer(l, n, round_):
                pe.wait_ge(tables_loaded, 16)
                norm_sum(n, msq)
                done = []

                def features(q, tile):
                    slot_loaded(q % NS, round_ + q // NS)
                    w = slot(q % NS, 2, C, P)
                    if tile >= 4:
                        pe.wait_ge(proj_evac, l * 20 + tile - 2)
                    for i in range(2):
                        if tile < ROTATED:
                            pe.wait_ge(tile_ready, l * ROTATED + tile + i + 1)
                        for c in range(C):
                            to = ps[:, (tile + i) % 4, 0:T]
                            if tile >= ROTATED:
                                last = pe.matmul(to, w[:, i, c], xn[:, c], start=c == 0, stop=c == C - 1)
                                continue
                            if tile + i == 0:
                                pe.wait_ge(mix_split_ready, l * C + c + 1)
                            hi, lo = tile_split[i]
                            pe.matmul(to, hi[:, c], mix_hi[:, c], start=c == 0, stop=False)
                            pe.matmul(to, hi[:, c], mix_lo[:, c], start=False, stop=False)
                            last = pe.matmul(to, lo[:, c], mix_hi[:, c], start=False, stop=c == C - 1)
                        if i == 0 and tile < ROTATED:
                            last.then_inc(tile_used, 1)
                    last.then_inc(slot_done, 1)

                def swaps(tile):
                    for i in range(tile, tile + 2):
                        pe.wait_ge(proj_evac, l * 20 + i + 1)
                        if i >= 2:
                            pe.wait_ge(rot_ready, l * 16 + i - 1)
                        pe.matmul(ps[:, 4 if i % 2 == 0 else 7, 0:T], K("diff_swap" if i < 8 else "ret_swap"), raw[:, i % 4],
                                  start=True, stop=True).then_inc(swap_ready, 1)

                def values(q, which):
                    pe.wait_ge(proj_evac, l * 20 + 8 * which + 8)
                    if which == 1:
                        pe.wait_ge(v_evac, l * 6 + 3)
                    for half in range(2):
                        s = (q + half) % NS
                        slot_loaded(s, round_ + (q + half) // NS)
                        w = slot(s, 4, 512)
                        for c in range(4):
                            for t, (t0, nt) in enumerate(TT):
                                k = 4 * half + c
                                bank = (5, 6, 3)[t]
                                last = pe.matmul(ps[0:nt, bank, 0:512], xn[:, k, t0:t0 + nt], w[:, c], start=k == 0, stop=k == C - 1)
                        last.then_inc(slot_done, 1)

                features(0, 0)
                features(1, 2)
                swaps(0)
                features(2, 4)
                swaps(2)
                features(3, 6)
                swaps(4)
                values(4, 0)
                swaps(6)
                features(6, 8)
                pe.wait_ge(v_evac, l * 6 + 3)
                features(7, 10)
                swaps(8)
                features(8, 12)
                swaps(10)
                features(9, 14)
                swaps(12)
                values(10, 1)
                swaps(14)
                features(12, 16)
                pe.wait_ge(v_evac, l * 6 + 6)
                features(13, 18)
                pe.wait_ge(proj_evac, l * 20 + 20)
                pe.wait_ge(v_evac, l * 6 + 6)

                def scores(u):
                    hd, t = divmod(u, 3)
                    t0, nt = TT[t]
                    for g in range(2):
                        rows = slice(64 * g, 64 * g + 64)
                        pe.matmul(ps[0:nt, 2 * (u % 2) + g, 0:t0 + nt], rot[rows, hd, t0:t0 + nt],
                                  rot[rows, 4 + hd, 0:t0 + nt], start=True, stop=False)
                        last = pe.matmul(ps[0:nt, 2 * (u % 2) + g, t0:t0 + nt], ident[0:nt, 0:nt], K("causal")[0:nt, 0:nt], start=False, stop=True)
                    last.then_inc(scores_ready, 1)

                def turn(u):
                    t0, nt = TT[u % 3]
                    pe.wait_ge(attn_ready, l * 12 + u + 1)
                    if u >= 1:
                        pe.wait_ge(attnT_ready, l * 12 + u)
                    for b in range(u % 3 + 1):
                        b0, nb = TT[b]
                        last = pe.matmul(ps[0:nb, 4, b * P:b * P + nt], a_buf[0:nt, u % 2, b0:b0 + nb],
                                         ident[0:nt, 0:nt], start=True, stop=True)
                    last.then_inc(attn_turned, 1)

                def diff_out(hd):
                    pe.wait_ge(attnT_ready, l * 12 + 3 * hd + 3)
                    if hd >= 1:
                        pe.wait_ge(diff_std_ready, l * 4 + hd)
                    for b, (b0, nb) in enumerate(TT):
                        last = pe.matmul(ps[:, 6, b0:T], dv[0:nb, b, hd * P:hd * P + P], aT_buf[0:nb, hd % 2, b, b0:T],
                                         start=b == 0, stop=b == 2)
                    last.then_inc(diff_o_ready, 1)

                def diff_sum(hd):
                    pe.wait_ge(diff_sq_ready, l * 4 + hd + 1)
                    pe.matmul(ps[:, 6, 0:T], ones, osq, start=True, stop=True).then_inc(diff_sum_ready, 1)

                def ret_scores(hd):
                    if hd >= 1:
                        pe.wait_ge(ret_std_ready, l * 4 + hd)
                    at = 0
                    for t0, nt in TT:
                        last = pe.matmul(ps[0:nt, 7, at:at + T - t0], rot[:, 12 + hd, t0:t0 + nt], rot[:, 8 + hd, t0:T], start=True, stop=True)
                        at += T - t0
                    last.then_inc(ret_scores_ready, 1)

                def ret_out(hd):
                    pe.wait_ge(ret_decayed, l * 8 + 2 * hd + 2)
                    at = 0
                    for b, (b0, nb) in enumerate(TT):
                        last = pe.matmul(ps[:, 7, b0:T], rv[0:nb, b, hd * P:hd * P + P], sT[0:nb, at:at + T - b0], start=b == 0, stop=b == 2)
                        at += T - b0
                    last.then_inc(ret_o_ready, 1)

                def ret_mean(hd):
                    pe.wait_ge(ret_o_evac, l * 4 + hd + 1)
                    pe.matmul(ps[:, 7, 0:T], ones, ret_o, start=True, stop=True).then_inc(ret_mean_ready, 1)

                def ret_var(hd):
                    pe.wait_ge(ret_sq_ready, l * 4 + hd + 1)
                    pe.matmul(ps[:, 7, 0:T], ones, ret_sq, start=True, stop=True).then_inc(ret_var_ready, 1)

                scores(0)
                for u in range(12):
                    hd, step = divmod(u, 3)
                    if u + 1 < 12:
                        scores(u + 1)
                    if u < MOD_MIX:
                        q = IN_SLOTS + u
                        mod_rows(u, l * MOD_MIX + u, q % NS, round_ + q // NS)
                    if u >= 1:
                        turn(u - 1)
                    if hd >= 1 and step == 0:
                        ret_var(hd - 1)
                        diff_out(hd - 1)
                    if hd >= 1 and step == 1:
                        diff_sum(hd - 1)
                    if u < MOD_MIX:
                        mod_turn(l * MOD_MIX + u)
                    (ret_scores, ret_out, ret_mean)[step](hd)
                ret_var(HEADS - 1)
                turn(11)
                diff_out(HEADS - 1)
                diff_sum(HEADS - 1)

                pe.wait_ge(ret_mixed, l * 4 + 4)
                pe.wait_ge(diff_mixed, l * 4 + 4)
                for o in range(C):
                    q = IN_SLOTS + MOD_MIX + o
                    slot_loaded(q % NS, round_ + q // NS)
                    w = slot(q % NS, C, P)
                    for c in range(C):
                        last = pe.matmul(ps[:, o, 0:T], w[:, c], y[:, c], start=c == 0, stop=c == C - 1)
                    last.then_inc(slot_done, 1)

            with pe.Fori(0, DEPTH) as l:
                ffn(2 * l, 3 * l)
                mixer(l, 3 * l + 1, l * ROUNDS + FFN_SLOTS // NS)
                ffn(2 * l + 1, 3 * l + 2)

            norm_sum(3 * DEPTH, sq)
            pe.wait_ge(h_ready, 7 * C)

            def tail_slot(q, *shape):
                slot_loaded(q % NS, DEPTH * ROUNDS + q // NS)
                return slot(q % NS, *shape)

            for q in range(MOD_TAIL):
                mod_rows(1, DEPTH * MOD_MIX + q, q, DEPTH * ROUNDS)
                mod_turn(DEPTH * MOD_MIX + q)
            for c in range(C):
                pe.wait_ge(sq2_ready, c + 1)
                pe.matmul(ps[:, 2, 0:KEYS], ones, sq2[:, c % 4], start=c == 0, stop=c == C - 1).then_inc(sq2_used, 1)

            job = 0

            def bank():
                nonlocal job
                if job >= 8:
                    pe.wait_ge(proj2_evac, job - 7)
                job += 1
                return (job - 1) % 8

            def features(q, n, together):
                w = tail_slot(MOD_TAIL + q, 2, C, P)
                for i in range(2):
                    if i == 0 or not together:
                        b = bank()
                    at = i * n if together else 0
                    for c in range(C):
                        if q + i == 0:
                            pe.wait_ge(x2n_ready, c + 1)
                        last = pe.matmul(ps[:, b, at:at + n], w[:, i, c], x2n[:, c, 0:n], start=c == 0, stop=c == C - 1)
                last.then_inc(slot_done, 1)

            def tokens(q, n, tiles_):
                w = tail_slot(MOD_TAIL + q, SLOT)[:, 0:C * n].rearrange("p (c n) -> p c n", c=C)
                for t in range(tiles_):
                    if t * n % 512 == 0:
                        b = bank()
                    at = t * n % 512
                    for c in range(C):
                        last = pe.matmul(ps[:, b, at:at + n], x2n[:, c, t * P:t * P + P], w[:, c], start=c == 0, stop=c == C - 1)
                last.then_inc(slot_done, 1)

            features(0, KEYS, False)
            features(1, SEQ, True)
            features(2, SEQ, True)
            tokens(3, 256, 2)
            features(4, SEQ, True)
            pe.wait_ge(qk_sq_ready, 1)
            for i in range(4):
                pe.matmul(ps[:, bank(), 0:KEYS], half_ones, a_sq[:, i], start=True, stop=True).then_inc(qk_sum_ready, 1)
            features(5, KEYS, False)
            pe.wait_ge(spatial_loaded, 16)
            pe.wait_ge(v_normed, 1)
            b = bank()
            for i in range(2):
                for t in range(2):
                    for hh in range(2):
                        head = 2 * i + hh
                        at = (2 * i + t) * P
                        last = pe.matmul(ps[64 * hh:64 * hh + 64, b, at:at + P], mlp_v[:, t, head * 64:head * 64 + 64], w_sp[:, head],
                                         start=True, stop=True)
            last.then_inc(mlp_mixed, 1)
            features(6, KEYS, False)
            pe.wait_ge(qk_normed, 1)
            for x in (aq[:, 0:2], aq[:, 2:4], ak[:, :, 0:SEQ]):
                pe.matmul(ps[:, bank(), 0:512], K("axial_swap"), x, start=True, stop=True).then_inc(qk_swapped, 1)
            tokens(7, 256, 4)
            features(8, SEQ, True)
            tokens(9, P, 4)
            features(10, SEQ, True)
            pe.wait_ge(proj2_evac, 23)

            pe.wait_ge(kd_ready, 1)
            for i in range(8):
                last = pe.matmul(ps[:, i // 4, (i % 4) * P:(i % 4) * P + P], decay_g[:, i // 2, (i % 2) * P:(i % 2) * P + P], ident,
                                 start=True, stop=True)
            last.then_inc(kd_turned, 1)
            pe.wait_ge(kdT_ready, 1)
            for i in range(4):
                for hh in range(2):
                    head = (i % 2) * 2 + hh
                    for t in range(2):
                        last = pe.matmul(ps[64 * hh:64 * hh + 64, 2, i * 64:i * 64 + 64], kdT[:, 2 * i + t, 64 * hh:64 * hh + 64],
                                         zv[:, 2 + t, head * 64:head * 64 + 64], start=t == 0, stop=t == 1)
            last.then_inc(states_summed, 1)
            pe.wait_ge(state_ready, 1)

            for n in range(N_LEVELS):
                pe.wait_ge(level_ready, n + 1)
                if n >= 2:
                    pe.wait_ge(gram_used, n - 1)
                banks = 4 * (n % 2)
                for d in range(2):
                    for i in range(2):
                        for c in range(2):
                            for hh in range(2):
                                rows = slice(64 * hh, 64 * hh + 64)
                                y_ = lev[rows, n % 2, 2 * d + i]
                                b = banks + 2 * d + hh
                                if n < len(LEVELS):
                                    left = right = y_[:, c * P:c * P + P]
                                    at = (2 * i + c) * P
                                elif n == len(LEVELS):
                                    if c == 1:
                                        continue
                                    left, right = (y_[:, 0:P], y_[:, P:2 * P]) if d == 0 else (y_[:, P:2 * P], y_[:, 0:P])
                                    at = i * P
                                else:
                                    if d == 1:
                                        continue
                                    left, right = y_[:, c * P:c * P + P], hq[rows, i, c * P:c * P + P]
                                    at = (2 * i + c) * P
                                last = pe.matmul(ps[:, b, at:at + P], left, right, start=True, stop=True)
                last.then_inc(gram_ready, 1)
            pe.wait_ge(gram_used, N_LEVELS)
            pe.wait_ge(qx_ready, 1)
            for i in range(2):
                for hh in range(2):
                    rows = slice(64 * hh, 64 * hh + 64)
                    cols = slice((2 * i + hh) * 64, (2 * i + hh) * 64 + 64)
                    b = 4 + 2 * i + hh
                    pe.matmul(ps[rows, b, 0:SEQ], state[rows, i], qx[rows, i], start=True, stop=False)
                    pe.matmul(ps[rows, b, 0:SEQ], state[rows, 2 + i], qx[rows, 2 + i], start=False, stop=False)
                    for c in range(2):
                        pe.matmul(ps[rows, b, c * P:c * P + P], zv[:, c, cols], S_acc[:, hh * 4 + 2 * i + c], start=False, stop=False)
                    pe.matmul(ps[rows, b, P:2 * P], zv[:, 0, cols], S_cross[:, 0, hh * 2 + i], start=False, stop=False)
                    last = pe.matmul(ps[rows, b, 0:P], zv[:, 1, cols], S_cross[:, 1, hh * 2 + i], start=False, stop=True)
            last.then_inc(o2_ready, 1)
            pe.wait_ge(o2_sq_ready, 1)
            pe.matmul(ps[:, 0, 0:512], half_ones, oh_sq, start=True, stop=True).then_inc(o2_sum_ready, 1)

            pe.wait_ge(qk_ready, 1)

            def scores2(n):
                j, hh, i = UNITS[n]
                rows = slice(64 * hh, 64 * hh + 64)
                if n >= AHEAD:
                    pe.wait_ge(s2_exp_ready, n - AHEAD + 1)
                pe.matmul(ps[:, 1 + n % AHEAD, 0:KEYS], aq[rows, j, i * P:i * P + P], ak[rows, j // 2, 0:KEYS], start=True, stop=True).then_inc(s2_ready, 1)

            def turn2(n):
                pe.wait_ge(p2_ready, n + 1)
                if n >= 2:
                    pe.wait_ge(p2T_ready, n - 1)
                for t in range(4):
                    last = pe.matmul(ps[:, 4 + n % 2, t * P:t * P + P], ae[:, n % AHEAD, t * P:t * P + P], ident, start=True, stop=True)
                last.then_inc(p2_turned, 1)

            def values2(n):
                j, hh, i = UNITS[n]
                pe.wait_ge(p2T_ready, n + 1)
                if n >= 2:
                    pe.wait_ge(y2_ready, 2 + n - 1)
                kv = j // 2
                for t in range(4):
                    last = pe.matmul(ps[64 * hh:64 * hh + 64, 6 + n % 2, 0:P], av[:, t, kv * 64:kv * 64 + 64], aeT[:, n % 2, t * P:t * P + P],
                                     start=t == 0, stop=t == 3)
                last.then_inc(pv2_ready, 1)

            for n in range(AHEAD - 1):
                scores2(n)
            for n in range(len(UNITS)):
                if n + AHEAD - 1 < len(UNITS):
                    scores2(n + AHEAD - 1)
                turn2(n)
                if n >= 1:
                    values2(n - 1)
            values2(len(UNITS) - 1)

            pe.wait_ge(y2_ready, 2 + len(UNITS))
            for o in range(C):
                w = tail_slot(MOD_TAIL + IN2_SLOTS + o, C, P)
                for c in range(C):
                    last = pe.matmul(ps[:, o, 0:SEQ], w[:, c], y2[:, c], start=c == 0, stop=c == C - 1)
                last.then_inc(slot_done, 1)
            for c in range(C):
                pe.wait_ge(sq3_ready, c + 1)
                last = pe.matmul(ps[:, 0, 0:SEQ], ones, sq3[:, c], start=c == 0, stop=c == C - 1)
            last.then_inc(sum3_ready, 1)
            pe.wait_ge(router_loaded, 16)
            for t in range(2):
                for c in range(C):
                    if t == 0:
                        pe.wait_ge(h2_ready, c + 1)
                    last = pe.matmul(ps[:, 1, t * 36:t * 36 + 36], h2[:, c, t * P:t * P + P], w_r[:, c], start=c == 0, stop=c == C - 1)
            last.then_inc(logits_ready, 1)
            for t in range(2):
                for c in range(C):
                    last = pe.matmul(ps[:, 4 + 2 * t + c // 4, (c % 4) * P:(c % 4) * P + P], h2[:, c, t * P:t * P + P], ident, start=True, stop=True)
            last.then_inc(h2_turned, 1)
            pe.wait_ge(chosen_ready, 1)
            pe.matmul(ps[:, 2, 0:E], K("earlier"), R["chosen"][:, 0], start=True, stop=True)
            pe.matmul(ps[:, 2, E:2 * E], ones, R["chosen"][:, 0], start=True, stop=False)
            pe.matmul(ps[:, 2, E:2 * E], K("earlier"), R["chosen"][:, 1], start=False, stop=True)
            pe.matmul(ps[:, 2, 2 * E:3 * E], ones, R["chosen"][:, 0], start=True, stop=False)
            pe.matmul(ps[:, 2, 2 * E:3 * E], ones, R["chosen"][:, 1], start=False, stop=True).then_inc(ranks_ready, 1)

            pe.wait_ge(h2t_ready, 1)
            pe.wait_ge(most_ready, 1)
            for b in range(4):
                pe.matmul(ps[:, b, 0:512], ident, ye[:, 0:512], start=True, stop=False)

            def gather(n):
                pe.wait_ge(sel_ready, n + 1)
                for c in range(C):
                    for t in range(2):
                        last = pe.matmul(ps[:, 6 + c // 4, (c % 4) * P:(c % 4) * P + P], h2t[:, t, c * P:c * P + P], sel[:, t],
                                         start=t == 0, stop=t == 1)
                    if c % 4 == 3:
                        last.then_inc(gathered, 1)

            def scatter(last_pair):
                for o in range(C):
                    last = pe.matmul(ps[:, o // 2, (o % 2) * SEQ:(o % 2) * SEQ + SEQ], ye[:, o * P:o * P + P], selT, start=False,
                                     stop=last_pair and o % 2 == 1)
                return last

            def experts(pass_):
                gather(pass_ * (PAIRS + 1))
                with pe.Fori(0, PAIRS) as pair:
                    n = pass_ * PAIRS + pair
                    g = pass_ * (PAIRS + 1) + pair
                    pe.wait_ge(xs_ready, 2 * g + 2)
                    for part in range(2):
                        pe.wait_ge((hidT_ready, selT_ready)[part], n + 1)
                        for e in range(2):
                            pe.wait_ge(big_full[2 * part + e], n * 16 + 16)
                        for c in range(C):
                            for e in range(2):
                                rows = slice(CAP * e, CAP * e + CAP)
                                last = pe.matmul(ps[rows, 4 + part, 0:FE], xs[:, c, rows], cut(ring, (2 * part + e) * BIG, C, FE)[:, c],
                                                 start=c == 0, stop=c == C - 1)
                                if c == C - 1:
                                    last.then_inc(big_done, 1)
                        if part == 0:
                            pe.wait_ge(selT_ready, n + 1)
                            pe.wait_ge(ye_ready, 2 * n + 2)
                            scatter(False)
                    gather(g + 1)
                    pe.wait_ge(e_hid_ready, n + 1)
                    for f in range(FE // P):
                        last = pe.matmul(ps[:, 4, f * P:f * P + P], e_hid[:, f * P:f * P + P], ident, start=True, stop=True)
                    last.then_inc(hid_turned, 1)
                    pe.wait_ge(sel_gate_ready, n + 1)
                    for t in range(2):
                        last = pe.matmul(ps[:, 5, t * P:t * P + P], sel_gate[:, t], ident, start=True, stop=True)
                    last.then_inc(sel_turned, 1)
                    pe.wait_ge(hidT_ready, n + 2)
                    for half in range(2):
                        pe.wait_ge(xs_ready, 2 * g + 3 + half)
                        if half == 0:
                            for e in range(2):
                                pe.wait_ge(big_full[4 + e], n * 16 + 16)
                        for f in range(FE // P):
                            for e in range(2):
                                rows = slice(CAP * e, CAP * e + CAP)
                                w = cut(ring, (4 + e) * BIG, FE // P, D)
                                last = pe.matmul(ps[rows, 6 + half, 0:512], hidT[:, f, rows], w[:, f, half * 512:half * 512 + 512],
                                                 start=f == 0, stop=f == FE // P - 1)
                                if half == 1 and f == FE // P - 1:
                                    last.then_inc(big_done, 1)
                        if half == 0:
                            last.then_inc(down_ready, 1)
                pe.wait_ge(ye_ready, (pass_ + 1) * PAIRS * 2 + 2)
                pe.wait_ge(selT_ready, (pass_ + 1) * PAIRS + 1)

            experts(0)
            with pe.If(pe.value_load(most[0:1, 0:1], min_val=0, max_val=SEQ) > CAP):
                with pe.Fori(1, PASSES) as pass_:
                    experts(pass_)
            scatter(True).then_inc(experts_done, 1)

        @block.scalar
        def _(act):
            act.wait_ge(consts_loaded, 32)
            act.wait_ge(lam_dots_ready, 1)
            nc.scalar.activation(lam_dot, lam_dot, ACT.Exp).then_inc(lam_exp_ready, 1)
            nc.scalar.activation(cc[:, :, 0:2], V("c", C, 2), ACT.Silu).then_inc(cc_ready, 1)
            act.wait_ge(slot_full[0], 16)
            act.dma_start(con[:, FIRST_CON:], tables[:, FIRST_CON:]).then_inc(tables_loaded, 16)

            def norm(n, squares, std_to, meanwhile=None):
                for c in range(C):
                    act.wait_ge(h_ready, n * C + c + 1)
                    nc.scalar.activation(squares[:, c], h[:, c], ACT.Square).then_inc(sq_ready, 1)
                    if c == 0 and meanwhile:
                        meanwhile()
                act.wait_ge(sumsq_ready, n + 1)
                nc.scalar.activation(std_to, ps[:, 0, 0:T], ACT.Sqrt, bias=eps, scale=1.0 / D).then_inc(std_ready, 1)

            def weights_hi(f, round_, j, loaded):
                act.wait_ge(slot_full[j], loaded * 16 + 16)
                for k in range(2):
                    b, ago = split_of(2 * j + k)
                    act.wait_ge(split_used, f * HALVES + round_ * PER_ROUND + 2 * j + k + 1 - ago + USED_CREDITS)
                    nc.scalar.activation(w_split[b][:, 0], half_of(j, k), ACT.Copy).then_inc(hi_ready, 1)

            def ffn(f, n, loaded):
                norm(n, sq, std, lambda: weights_hi(f, 0, 0, loaded))
                for c in range(C):
                    act.wait_ge(xn32_ready, f * C + c + 1)
                    nc.scalar.activation(xn_hi[:, c], xn32[:, c], ACT.Copy).then_inc(xn_hi_ready, 1)
                with act.Fori(0, GU_SLOTS // NS) as it:
                    for j in range(NS):
                        nxt = (j + 1) % NS
                        weights_hi(f, it + (j + 1) // NS, nxt, loaded + it + (j + 1) // NS)
                        act.wait_ge(split_used, f * HALVES + it * PER_ROUND + 2 * j + 1 + USED_CREDITS)
                        nc.scalar.activation(gate_act[:, j % 4], ps[:, 2 * (j % 4), 0:T], ACT.Silu).then_inc(gate_act_ready, 1)

                def hidden_hi(i):
                    act.wait_ge(gate_up_used, f * F + i + 1 + 3)
                    if i > 0:
                        act.wait_ge(split_used, f * HALVES + 2 * GU_SLOTS + max(0, i + 1 - C) + USED_CREDITS)
                    nc.scalar.activation(hid_split(i)[0], hid[:, i], ACT.Copy).then_inc(hid_hi_ready, 1)

                for j in range(DOWN_SLOTS):
                    for k in range(2):
                        hidden_hi(2 * j + k)
                    if j + 1 < DOWN_SLOTS:
                        weights_hi(f, 2, j + 1, loaded + 2)

            def mod_evac(slots):
                act.wait_ge(slot_done, slots)
                nc.scalar.activation(mod_row, ps[:, 5, 0:MOD_COLS], ACT.Copy).then_inc(mod_row_ready, 1)

            def mixer(l, n, slots, rounds):
                def tiles_hi(q):
                    tile = 2 * q if q < 4 else 2 * q - 4
                    act.wait_ge(slot_full[q % NS], (rounds + q // NS) * 16 + 16)
                    for i in range(2):
                        if tile > 0 and i == 0:
                            act.wait_ge(tile_used, l * (ROTATED // 2) + tile // 2)
                        if tile > 0 and i == 1:
                            act.wait_ge(slot_done, slots + (q if q != 6 else 4))
                        nc.scalar.activation(tile_split[i][0], half_of(q % NS, i), ACT.Copy).then_inc(tile_hi_ready, 1)

                norm(n, msq, mstd, lambda: tiles_hi(0))
                for c in range(C):
                    act.wait_ge(mix_in_ready, l * C + c + 1)
                    nc.scalar.activation(mix_hi[:, c], xn[:, c], ACT.Copy).then_inc(mix_hi_ready, 1)

                def features(q, tile):
                    if q < 9 and q != 3:
                        tiles_hi(q + 1)
                    act.wait_ge(slot_done, slots + q + 1)
                    for i in range(tile, tile + 2):
                        if i < 16:
                            if i >= 4:
                                act.wait_ge(rot_ready, l * 16 + i - 3)
                            nc.scalar.activation(raw[:, i % 4], ps[:, i % 4, 0:T], ACT.Copy).then_inc(proj_evac, 1)
                        else:
                            nc.scalar.activation(rgate[:, i - 16], ps[:, i % 4, 0:T], ACT.Silu).then_inc(proj_evac, 1)

                def values(q, to):
                    act.wait_ge(slot_done, slots + q + 2)
                    for t, (_, nt) in enumerate(TT):
                        nc.scalar.activation(to[0:nt, t], ps[0:nt, (5, 6, 3)[t], 0:512], ACT.Copy).then_inc(v_evac, 1)

                for q in range(4):
                    features(q, 2 * q)
                tiles_hi(6)
                values(4, dv)
                for q in range(6, 10):
                    features(q, 2 * q - 4)
                values(10, rv)
                for q in range(12, 14):
                    features(q, 2 * q - 8)

                def turned(u):
                    hd, t = divmod(u, 3)
                    t0, nt = TT[t]
                    act.wait_ge(attn_turned, l * 12 + u + 1)
                    if t == 0 and hd >= 2:
                        act.wait_ge(diff_o_ready, l * 4 + hd - 1)
                    full = min(t + 1, 2)
                    copy = nc.scalar.activation(aT_buf[:, hd % 2, 0:full, t0:t0 + nt],
                                                ps[:, 4, 0:full * P].rearrange("p (b i) -> p b i", b=full)[:, :, 0:nt], ACT.Copy)
                    if t == 2:
                        copy = nc.scalar.activation(aT_buf[0:META, hd % 2, 2, t0:t0 + nt], ps[0:META, 4, 2 * P:2 * P + nt], ACT.Copy)
                    copy.then_inc(attnT_ready, 1)

                def diff_evac(hd):
                    act.wait_ge(diff_o_ready, l * 4 + hd + 1)
                    if hd >= 1:
                        act.wait_ge(diff_mixed, l * 4 + hd)
                    nc.scalar.activation(o_buf, ps[:, 6, 0:T], ACT.Copy)
                    nc.scalar.activation(osq, ps[:, 6, 0:T], ACT.Square).then_inc(diff_sq_ready, 1)
                    act.wait_ge(diff_sum_ready, l * 4 + hd + 1)
                    nc.scalar.activation(ostd, ps[:, 6, 0:T], ACT.Sqrt, bias=eps, scale=1.0 / P).then_inc(diff_std_ready, 1)

                def exponentials(u):
                    nt = TT[u % 3][1]
                    n_keys = TT[u % 3][0] + nt
                    act.wait_ge(max_ready, l * 12 + u + 1)
                    for g in range(2):
                        last = nc.scalar.activation(e_buf[0:nt, u % 2, g, 0:n_keys], ps[0:nt, 2 * (u % 2) + g, 0:n_keys], ACT.Exp,
                                                    bias=neg_max[0:nt, u % 2, g:g + 1], scale=64.0 ** -0.5, accum_out=e_sum[0:nt, u % 2, g:g + 1])
                    last.then_inc(exp_ready, 1)

                def ret_evac(hd):
                    act.wait_ge(ret_o_ready, l * 4 + hd + 1)
                    if hd >= 1:
                        act.wait_ge(ret_mixed, l * 4 + hd)
                    nc.scalar.activation(ret_o, ps[:, 7, 0:T], ACT.Copy).then_inc(ret_o_evac, 1)

                def ret_squares(hd):
                    act.wait_ge(ret_centred, l * 4 + hd + 1)
                    nc.scalar.activation(ret_sq, ret_o, ACT.Square).then_inc(ret_sq_ready, 1)

                def ret_deviation(hd):
                    act.wait_ge(ret_var_ready, l * 4 + hd + 1)
                    nc.scalar.activation(ret_std, ps[:, 7, 0:T], ACT.Sqrt, bias=eps, scale=1.0 / P).then_inc(ret_std_ready, 1)

                exponentials(0)
                for u in range(12):
                    hd, step = divmod(u, 3)
                    if hd >= 1 and step == 0:
                        ret_squares(hd - 1)
                    if u < MOD_MIX:
                        mod_evac(slots + IN_SLOTS + u + 1)
                    if u >= 1:
                        turned(u - 1)
                    if hd >= 1 and step == 0:
                        ret_deviation(hd - 1)
                    if step == 2:
                        ret_evac(hd)
                    if u + 1 < 12:
                        exponentials(u + 1)
                    if hd >= 1 and step == 0:
                        diff_evac(hd - 1)
                ret_squares(HEADS - 1)
                ret_deviation(HEADS - 1)
                turned(11)
                diff_evac(HEADS - 1)

            with act.Fori(0, DEPTH) as l:
                ffn(2 * l, 3 * l, l * ROUNDS)
                mixer(l, 3 * l + 1, l * MIX_SLOTS, l * ROUNDS + FFN_SLOTS // NS)
                ffn(2 * l + 1, 3 * l + 2, l * ROUNDS + (FFN_SLOTS + MIX_SLOTS) // NS)

            norm(3 * DEPTH, sq, std)
            for q in range(MOD_TAIL):
                mod_evac(TAIL + q + 1)
            act.wait_ge(ctx_loaded, 16)
            for c in range(C):
                act.wait_ge(x_ready, c + 1)
                if c >= 4:
                    act.wait_ge(sq2_used, c - 3)
                nc.scalar.activation(sq2[:, c % 4], raw2[:, c], ACT.Square).then_inc(sq2_ready, 1)
            act.wait_ge(sq2_used, C)
            nc.scalar.activation(std2, ps[:, 2, 0:KEYS], ACT.Sqrt, bias=eps, scale=1.0 / D).then_inc(std2_ready, 1)

            for c in range(C):
                act.wait_ge(x2_scaled, c + 1)
                for i in range(2):
                    half = slice(i * SEQ, i * SEQ + SEQ)
                    last = nc.scalar.activation(x2n[:, c, half], scaled2[:, c, half], ACT.Identity, bias=mod[:, c, i:i + 1])
                last.then_inc(x2n_ready, 1)

            job = 0

            def evac(q, *copies):
                nonlocal job
                act.wait_ge(slot_done, TAIL + MOD_TAIL + q + 1)
                for to, n, func in copies:
                    nc.scalar.activation(to, ps[:, job % 8, 0:n], func).then_inc(proj2_evac, 1)
                    job += 1

            def flat(a):
                return a.rearrange("p a b -> p (a b)")

            evac(0, (ak[:, 0], KEYS, ACT.Copy), (ak[:, 1], KEYS, ACT.Copy))
            evac(1, (flat(aq[:, 0:2]), 512, ACT.Copy))
            evac(2, (flat(aq[:, 2:4]), 512, ACT.Copy))
            act.drain()
            nc.scalar.activation(a_sq[:, 0:2], aq, ACT.Square)
            nc.scalar.activation(a_sq[:, 2:4], ak, ACT.Square).then_inc(qk_sq_ready, 1)
            evac(3, (flat(mlp_v), 512, ACT.Gelu_apprx_tanh))
            evac(4, (flat(mlp_u), 512, ACT.Gelu_apprx_tanh))
            act.wait_ge(v_ss_ready, 1)
            nc.scalar.activation(v_std, v_ss, ACT.Sqrt, bias=eps, scale=1.0 / 64).then_inc(v_std_ready, 1)
            for i in range(4):
                act.wait_ge(qk_sum_ready, i + 1)
                nc.scalar.activation(a_std[:, i], ps[:, job % 8, 0:KEYS], ACT.Sqrt, bias=eps, scale=1.0 / 64).then_inc(proj2_evac, 1)
                job += 1
            evac(5, (z[:, 0], KEYS, ACT.Copy), (z[:, 1], KEYS, ACT.Copy))
            act.wait_ge(mlp_mixed, 1)
            nc.scalar.activation(mlp_mix.rearrange("p a b c -> p (a b c)"), ps[:, job % 8, 0:512], ACT.Copy).then_inc(proj2_evac, 1)
            job += 1
            evac(6, (z[:, 2], KEYS, ACT.Copy), (z[:, 3], KEYS, ACT.Copy))
            for i, to in enumerate((a_sin[:, 0:2], a_sin[:, 2:4], k_swapped)):
                act.wait_ge(qk_swapped, i + 1)
                nc.scalar.activation(flat(to), ps[:, job % 8, 0:512], ACT.Copy).then_inc(proj2_evac, 1)
                job += 1
            act.wait_ge(qk_ready, 1)
            nc.scalar.activation(hk, z, ACT.Sigmoid, scale=-1.0)
            nc.scalar.activation(log_f, z, ACT.Abs)
            act.drain()
            nc.scalar.activation(log_f, log_f, ACT.Exp, scale=-1.0)
            act.drain()
            nc.scalar.activation(log_f, log_f, ACT.Ln, bias=one).then_inc(gates_ready, 1)
            evac(7, (flat(zv[:, 0:2]), 512, ACT.Copy), (flat(zv[:, 2:4]), 512, ACT.Copy))
            evac(8, (flat(hq), 512, ACT.Silu))
            evac(9, (flat(av), 512, ACT.Copy))
            evac(10, (flat(hg), 512, ACT.Silu))

            act.wait_ge(scans_ready, 1)
            nc.scalar.activation(decay_g, decay_g, ACT.Exp).then_inc(decays_ready, 1)
            nc.scalar.activation(qx[:, 0:2], decay_b[:, 0:2], ACT.Exp)
            nc.scalar.activation(qx[:, 2:4], decay_b[:, 2:4], ACT.Exp, scale=-1.0).then_inc(decays_ready, 1)
            act.wait_ge(kd_turned, 1)
            for i in range(2):
                last = nc.scalar.activation(flat(kdT[:, 4 * i:4 * i + 4]), ps[:, i, 0:512], ACT.Copy)
            last.then_inc(kdT_ready, 1)
            act.wait_ge(states_summed, 1)
            nc.scalar.activation(flat(state), ps[:, 2, 0:SEQ], ACT.Copy).then_inc(state_ready, 1)
            for n in range(N_LEVELS - 1):
                act.wait_ge(diff_ready, n + 1)
                width = 2 * LEVELS[n] if n < len(LEVELS) else SEQ
                pairs = flat(lev[:, n % 2]).rearrange("p (b s m) -> p b s m", s=2, m=width // 2)
                nc.scalar.activation(pairs[:, :, 0], pairs[:, :, 0], ACT.Exp, scale=-1.0)
                nc.scalar.activation(pairs[:, :, 1], pairs[:, :, 1], ACT.Exp).then_inc(level_exp_ready, 1)
            act.wait_ge(o2_ready, 1)
            for i in range(2):
                for hh in range(2):
                    rows = slice(64 * hh, 64 * hh + 64)
                    nc.scalar.activation(oh[rows, i], ps[rows, 4 + 2 * i + hh, 0:SEQ], ACT.Copy)
            act.drain()
            nc.scalar.activation(oh_sq, oh, ACT.Square).then_inc(o2_sq_ready, 1)
            act.wait_ge(o2_sum_ready, 1)
            nc.scalar.activation(oh_std, ps[:, 0, 0:512], ACT.Sqrt, bias=eps, scale=1.0 / 64).then_inc(o2_std_ready, 1)

            def exp2(n):
                act.wait_ge(s2_max_ready, n + 1)
                k = n % AHEAD
                nc.scalar.activation(ae[:, k], ps[:, 1 + k, 0:KEYS], ACT.Exp, bias=a_nmax[:, k:k + 1], scale=0.125,
                                     accum_out=a_sum[:, k:k + 1]).then_inc(s2_exp_ready, 1)

            for n in range(len(UNITS)):
                if n == 0:
                    for k in range(AHEAD - 1):
                        exp2(k)
                if n + AHEAD - 1 < len(UNITS):
                    exp2(n + AHEAD - 1)
                act.wait_ge(p2_turned, n + 1)
                if n >= 2:
                    act.wait_ge(pv2_ready, n - 1)
                nc.scalar.activation(aeT[:, n % 2], ps[:, 4 + n % 2, 0:512], ACT.Copy).then_inc(p2T_ready, 1)

            for c in range(C):
                act.wait_ge(x2_ready, c + 1)
                nc.scalar.activation(sq3[:, c], x2[:, c], ACT.Square).then_inc(sq3_ready, 1)
            act.wait_ge(sum3_ready, 1)
            nc.scalar.activation(std3, ps[:, 0, 0:SEQ], ACT.Sqrt, bias=eps, scale=1.0 / D).then_inc(std3_ready, 1)

            for c in range(C):
                act.wait_ge(h2_scaled, c + 1)
                nc.scalar.activation(h2[:, c], h2[:, c], ACT.Identity, bias=mod[:, SH2, 0][:, c:c + 1]).then_inc(h2_ready, 1)

            act.wait_ge(gmax_ready, 1)
            for t in range(2):
                last = nc.scalar.activation(R["gexp"][:, t], R["lg"][:, t, 0:GROUPS], ACT.Exp, bias=R["ngmax"][:, t:t + 1],
                                            accum_out=R["gsum"][:, t:t + 1])
            last.then_inc(gexp_ready, 1)
            act.wait_ge(top_ready, 1)
            nc.scalar.activation(R["ex"], R["d"], ACT.Exp).then_inc(top_exp_ready, 1)
            act.wait_ge(h2_turned, 1)
            nc.scalar.activation(h2t.rearrange("p t d -> p (t d)"), ps[:, 4:8, :].rearrange("p b n -> p (b n)"), ACT.Copy).then_inc(h2t_ready, 1)

            def gathered_tokens(n):
                for half in range(2):
                    act.wait_ge(gathered, 2 * n + half + 1)
                    nc.scalar.activation(xs[:, 4 * half:4 * half + 4], ps[:, 6 + half, 0:512].rearrange("p (c s) -> p c s", s=P), ACT.Copy).then_inc(xs_ready, 1)

            def experts(pass_):
                gathered_tokens(pass_ * (PAIRS + 1))
                with act.Fori(0, PAIRS) as pair:
                    n = pass_ * PAIRS + pair
                    act.wait_ge(big_done, n * BIG_SLOTS + BIG_SLOTS + 2)
                    nc.scalar.activation(e_act, ps[:, 4, 0:FE], ACT.Silu).then_inc(e_act_ready, 1)
                    gathered_tokens(pass_ * (PAIRS + 1) + pair + 1)
                    act.wait_ge(hid_turned, n + 1)
                    nc.scalar.activation(hidT, ps[:, 4, 0:FE].rearrange("p (f s) -> p f s", s=P), ACT.Copy).then_inc(hidT_ready, 1)
                    act.wait_ge(sel_turned, n + 1)
                    nc.scalar.activation(selT, ps[:, 5, 0:SEQ], ACT.Copy).then_inc(selT_ready, 1)
                    act.wait_ge(down_ready, n + 1)
                    nc.scalar.activation(ye[:, 0:512], ps[:, 6, 0:512], ACT.Copy).then_inc(ye_ready, 1)
                    act.wait_ge(big_done, n * BIG_SLOTS + 2 * BIG_SLOTS)
                    nc.scalar.activation(ye[:, 512:D], ps[:, 7, 0:512], ACT.Copy).then_inc(ye_ready, 1)

            experts(0)
            act.wait_ge(most_ready, 1)
            with act.If(act.value_load(most[0:1, 0:1], min_val=0, max_val=SEQ) > CAP):
                with act.Fori(1, PASSES) as pass_:
                    experts(pass_)

        @block.vector
        def _(dve):
            dve.sem_inc(split_ready, SPLIT_CREDITS)
            dve.sem_inc(mod_ready, 1)
            dve.sem_inc(gate_up_used, 3)
            dve.wait_ge(h_loaded, 16)
            dve.sem_inc(h_ready, C)
            dve.wait_ge(consts_loaded, 32)
            nc.vector.memset(cc, 0.0)
            pairs = V("lam", DEPTH * 2, 2, 64)
            prod = cut(arena, rest, DEPTH * 2, 64)
            nc.vector.tensor_tensor(prod, pairs[:, :, 0], pairs[:, :, 1], ALU.mult)
            dve.drain()
            nc.vector.tensor_reduce(lam_dot, prod, AX.X, ALU.add).then_inc(lam_dots_ready, 1)
            dve.wait_ge(lam_exp_ready, 1)
            for l in range(DEPTH):
                nc.vector.tensor_tensor(neglam[:, l:l + 1], lam_dot[:, 2 * l + 1:2 * l + 2], lam_dot[:, 2 * l:2 * l + 1], ALU.subtract)
                nc.vector.tensor_scalar(sub_w[:, l:l + 1], V("subln")[:, l:l + 1], 1.0 - LAMBDA_INIT[l], None, ALU.mult)
            dve.drain()
            for l in range(DEPTH):
                nc.vector.tensor_scalar(neglam[:, l:l + 1], neglam[:, l:l + 1], -LAMBDA_INIT[l], None, ALU.add)

            def norm(n, std_from, rstd_to):
                dve.wait_ge(std_ready, n + 1)
                nc.vector.reciprocal(rstd_to, std_from)
                dve.drain()

            def normed(n, c, to, by):
                return nc.vector.scalar_tensor_tensor(to[:, c], h[:, c], V("norms")[:, bass.ds(n * C + c, 1)], by, ALU.mult, ALU.mult)

            def residual(ready, scale):
                for o in range(C):
                    ready(o)
                    nc.vector.scalar_tensor_tensor(h[:, o], ps[:, o, 0:T], scale, h[:, o], ALU.mult, ALU.add).then_inc(h_ready, 1)

            def weights_lo(f, round_, j):
                for k in range(2):
                    b, _ = split_of(2 * j + k)
                    dve.wait_ge(hi_ready, f * HALVES + round_ * PER_ROUND + 2 * j + k + 1)
                    nc.vector.tensor_tensor(w_split[b][:, 1], half_of(j, k), w_split[b][:, 0].bitcast(fp32), ALU.subtract).then_inc(split_ready, 1)

            def ffn(f, n):
                weights_lo(f, 0, 0)
                norm(n, std, rstd)
                for c in range(C):
                    if c == 0:
                        normed(n, 0, xn32, rstd).then_inc(xn32_ready, 1)
                    if c + 1 < C:
                        normed(n, c + 1, xn32, rstd).then_inc(xn32_ready, 1)
                    dve.wait_ge(xn_hi_ready, f * C + c + 1)
                    nc.vector.tensor_tensor(xn_lo[:, c], xn32[:, c], xn_hi[:, c].bitcast(fp32), ALU.subtract).then_inc(xn_ready, 1)
                with dve.Fori(0, GU_SLOTS // NS) as it:
                    for j in range(NS):
                        weights_lo(f, it + (j + 1) // NS, (j + 1) % NS)
                        dve.wait_ge(gate_act_ready, f * F + it * NS + j + 1)
                        dve.wait_ge(split_used, f * HALVES + it * PER_ROUND + 2 * j + 2 + USED_CREDITS)
                        to = cut(arena, rest, F * T)[:, bass.ds(it * (NS * T) + j * T, T)]
                        nc.vector.tensor_tensor(to, gate_act[:, j % 4], ps[:, 2 * (j % 4) + 1, 0:T], ALU.mult).then_inc(gate_up_used, 1)

                def hidden_lo(i):
                    dve.wait_ge(hid_hi_ready, f * F + i + 1)
                    hi, lo = hid_split(i)
                    nc.vector.tensor_tensor(lo, hid[:, i], hi.bitcast(fp32), ALU.subtract).then_inc(hid_split_ready, 1)

                dve.drain()
                for j in range(DOWN_SLOTS):
                    for k in range(2):
                        hidden_lo(2 * j + k)
                    if j + 1 < DOWN_SLOTS:
                        weights_lo(f, 2, j + 1)

                def ready(o):
                    if o < C - 1:
                        dve.wait_ge(y_ready, f * (C - 1) + o + 1)
                    else:
                        dve.wait_ge(split_used, f * HALVES + HALVES + USED_CREDITS)

                residual(ready, 0.5)

            def mod_bias(q):
                dve.wait_ge(mod_turned, q + 1)
                to = small[:, bass.ds(MOD_AT + 4 * q, 4)].rearrange("p (o n) -> p o n", n=2)
                bias = V("b_mod")[:, bass.ds(2 * q, 2)].unsqueeze(2).to_broadcast([P, 2, 2])
                nc.vector.tensor_tensor(to, ps[:, 5, MOD_COLS:MOD_COLS + 4].rearrange("p (o n) -> p o n", n=2), bias, ALU.add).then_inc(mod_ready, 1)

            def mixer(l, n, slots):
                dve.wait_ge(tables_loaded, 16)
                def tiles_lo(q):
                    tile = 2 * q if q < 4 else 2 * q - 4
                    for i in range(2):
                        dve.wait_ge(tile_hi_ready, l * ROTATED + tile + i + 1)
                        hi, lo = tile_split[i]
                        nc.vector.tensor_tensor(lo, half_of(q % NS, i), hi.bitcast(fp32), ALU.subtract).then_inc(tile_ready, 1)

                tiles_lo(0)
                norm(n, mstd, mrstd)
                for c in range(C):
                    if c == 0:
                        normed(n, 0, xn, mrstd).then_inc(mix_in_ready, 1)
                    if c + 1 < C:
                        normed(n, c + 1, xn, mrstd).then_inc(mix_in_ready, 1)
                    dve.wait_ge(mix_hi_ready, l * C + c + 1)
                    nc.vector.tensor_tensor(mix_lo[:, c], xn[:, c], mix_hi[:, c].bitcast(fp32), ALU.subtract).then_inc(mix_split_ready, 1)
                tiles_lo(1)
                for i in range(16):
                    if i % 2 == 0 and i // 2 + 2 < 8:
                        tiles_lo((2, 3, 6, 7, 8, 9)[i // 2])
                    table = "diff" if i < 8 else "ret"
                    dve.wait_ge(proj_evac, l * 20 + i + 1)
                    nc.vector.tensor_tensor(t_cos[:, i % 2], raw[:, i % 4], K(table + "_cos"), ALU.mult)
                    dve.wait_ge(swap_ready, l * 16 + i + 1)
                    nc.vector.tensor_tensor(t_sin[:, i % 2], ps[:, 4 if i % 2 == 0 else 7, 0:T], K(table + "_sin"), ALU.mult)
                    dve.drain()
                    nc.vector.tensor_tensor(rot[:, i], t_cos[:, i % 2], t_sin[:, i % 2], ALU.add).then_inc(rot_ready, 1)

                def greatest(u):
                    t0, nt = TT[u % 3]
                    n_keys = t0 + nt
                    dve.wait_ge(scores_ready, l * 12 + u + 1)
                    at = 2 * (u % 2)
                    nc.vector.tensor_reduce(s_max[0:nt, u % 2], ps[0:nt, at:at + 2, 0:n_keys], AX.X, ALU.max)
                    dve.drain()
                    nc.vector.tensor_scalar(neg_max[0:nt, u % 2], s_max[0:nt, u % 2], -(64.0 ** -0.5), None, ALU.mult).then_inc(max_ready, 1)

                def combine(u):
                    t0, nt = TT[u % 3]
                    n_keys = t0 + nt
                    dve.wait_ge(exp_ready, l * 12 + u + 1)
                    nc.vector.reciprocal(e_rsum[0:nt, u % 2], e_sum[0:nt, u % 2])
                    dve.drain()
                    nc.vector.tensor_scalar(neg_r[0:nt, u % 2:u % 2 + 1], e_rsum[0:nt, u % 2, 1:2], neglam[0:nt, bass.ds(l, 1)], None, ALU.mult)
                    if u >= 2:
                        dve.wait_ge(attn_turned, l * 12 + u - 1)
                    nc.vector.tensor_scalar(a_buf[0:nt, u % 2, 0:n_keys], e_buf[0:nt, u % 2, 0, 0:n_keys], e_rsum[0:nt, u % 2, 0:1], None, ALU.mult)
                    dve.drain()
                    nc.vector.scalar_tensor_tensor(a_buf[0:nt, u % 2, 0:n_keys], e_buf[0:nt, u % 2, 1, 0:n_keys], neg_r[0:nt, u % 2:u % 2 + 1],
                                                   a_buf[0:nt, u % 2, 0:n_keys], ALU.mult, ALU.add).then_inc(attn_ready, 1)

                def diff_norm(hd):
                    dve.wait_ge(diff_std_ready, l * 4 + hd + 1)
                    nc.vector.reciprocal(orstd, ostd)
                    dve.drain()
                    nc.vector.scalar_tensor_tensor(y[:, 4 + hd], o_buf, sub_w[:, bass.ds(l, 1)], orstd, ALU.mult, ALU.mult).then_inc(diff_mixed, 1)

                def decayed(hd):
                    dve.wait_ge(ret_scores_ready, l * 4 + hd + 1)
                    decay = K("decay", HEADS, DEC)[:, hd]
                    whole = DEC - META
                    nc.vector.tensor_tensor(sT[:, 0:whole], ps[:, 7, 0:whole], decay[:, 0:whole], ALU.mult).then_inc(ret_decayed, 1)
                    nc.vector.tensor_tensor(sT[0:META, whole:DEC], ps[0:META, 7, whole:DEC], decay[0:META, whole:DEC], ALU.mult).then_inc(ret_decayed, 1)

                def centred(hd):
                    dve.wait_ge(ret_mean_ready, l * 4 + hd + 1)
                    nc.vector.scalar_tensor_tensor(ret_o, ps[:, 7, 0:T], -1.0 / P, ret_o, ALU.mult, ALU.add).then_inc(ret_centred, 1)

                def ret_norm(hd):
                    dve.wait_ge(ret_std_ready, l * 4 + hd + 1)
                    nc.vector.reciprocal(ret_std, ret_std)
                    dve.drain()
                    nc.vector.scalar_tensor_tensor(ret_o, ret_o, V("gn")[:, bass.ds(l * HEADS + hd, 1)], ret_std, ALU.mult, ALU.mult)
                    dve.drain()
                    nc.vector.tensor_tensor(y[:, hd], ret_o, rgate[:, hd], ALU.mult).then_inc(ret_mixed, 1)

                greatest(0)
                for u in range(12):
                    hd, step = divmod(u, 3)
                    if hd >= 1 and step == 0:
                        centred(hd - 1)
                    if u >= 1:
                        mod_bias(l * MOD_MIX + u - 1)
                        combine(u - 1)
                    if step == 1:
                        decayed(hd)
                    if u + 1 < 12:
                        greatest(u + 1)
                    if hd >= 1 and step == 0:
                        ret_norm(hd - 1)
                    if hd >= 1 and step == 1:
                        diff_norm(hd - 1)
                centred(HEADS - 1)
                combine(11)
                ret_norm(HEADS - 1)
                diff_norm(HEADS - 1)

                residual(lambda o: dve.wait_ge(slot_done, slots + IN_SLOTS + MOD_MIX + o + 1), 1.0)

            with dve.Fori(0, DEPTH) as l:
                ffn(2 * l, 3 * l)
                mixer(l, 3 * l + 1, l * MIX_SLOTS)
                ffn(2 * l + 1, 3 * l + 2)

            def wide(a, n, m):
                return a.unsqueeze(2).to_broadcast([P, n, m])

            def flat(a):
                return a.rearrange("p a b -> p (a b)")

            dve.wait_ge(std_ready, 3 * DEPTH + 1)
            nc.vector.reciprocal(rstd, std)
            dve.drain()
            for c in range(C):
                nc.vector.scalar_tensor_tensor(raw2[:, c, 0:SEQ], h[:, c, META:T], V("final")[:, c:c + 1], rstd[:, META:T], ALU.mult, ALU.mult).then_inc(x_ready, 1)
            for q in range(MOD_TAIL):
                mod_bias(DEPTH * MOD_MIX + q)
            nc.vector.scalar_tensor_tensor(a1, mod[:, SC1], 1.0, wide(V("norm1"), C, 2), ALU.add, ALU.mult)
            nc.vector.scalar_tensor_tensor(a2, mod[:, SC2, 0], 1.0, V("norm2"), ALU.add, ALU.mult)
            dve.wait_ge(std2_ready, 1)
            nc.vector.reciprocal(rstd2, std2)
            dve.drain()
            for c in range(C):
                for i in range(2):
                    half = slice(i * SEQ, i * SEQ + SEQ)
                    last = nc.vector.scalar_tensor_tensor(scaled2[:, c, half], raw2[:, c, half], a1[:, c, i:i + 1], rstd2[:, half], ALU.mult, ALU.mult)
                last.then_inc(x2_scaled, 1)

            dve.wait_ge(proj2_evac, 5)
            vh = flat(mlp_v).rearrange("p (h d) -> p h d", d=64)
            nc.vector.tensor_tensor(v_sq, vh, vh, ALU.mult)
            dve.drain()
            nc.vector.tensor_reduce(v_ss, v_sq, AX.X, ALU.add).then_inc(v_ss_ready, 1)
            dve.wait_ge(v_std_ready, 1)
            nc.vector.reciprocal(v_rstd, v_std)
            dve.drain()
            nc.vector.tensor_tensor(vh, vh, wide(v_rstd, 8, 64), ALU.mult).then_inc(v_normed, 1)

            dve.wait_ge(proj2_evac, 10)
            nc.vector.reciprocal(a_std, a_std)
            dve.drain()
            nc.vector.scalar_tensor_tensor(flat(aq), flat(aq), V("qn"), flat(a_std[:, 0:2]), ALU.mult, ALU.mult)
            nc.vector.scalar_tensor_tensor(flat(ak), flat(ak), V("kn"), flat(a_std[:, 2:4]), ALU.mult, ALU.mult).then_inc(qk_normed, 1)

            dve.wait_ge(proj2_evac, 13)
            nc.vector.tensor_tensor(mlp_mix, mlp_mix, V("b_s", 2, P).unsqueeze(2).to_broadcast([P, 2, 2, P]), ALU.add)
            dve.drain()
            nc.vector.tensor_tensor(flat(mlp_u), flat(mlp_u), mlp_mix.rearrange("p a b c -> p (a b c)"), ALU.mult)

            def rotate(x, swapped, n):
                cos = K("axial_cos").unsqueeze(1).to_broadcast([P, n, SEQ])
                sin = K("axial_sin").unsqueeze(1).to_broadcast([P, n, SEQ])
                nc.vector.tensor_tensor(a_cos[:, 0:n], x, cos, ALU.mult)
                nc.vector.tensor_tensor(swapped, swapped, sin, ALU.mult)
                dve.drain()
                return nc.vector.tensor_tensor(x, a_cos[:, 0:n], swapped, ALU.add)

            dve.wait_ge(proj2_evac, 18)
            rotate(aq, a_sin, 4)
            dve.drain()
            rotate(ak[:, :, 0:SEQ], k_swapped, 2).then_inc(qk_ready, 1)

            dve.wait_ge(gates_ready, 1)
            nc.vector.scalar_tensor_tensor(log_f, z, 0.0, log_f, ALU.min, ALU.subtract)
            nc.vector.memset(decay_g[:, 0:2, SEQ - 1:SEQ], 0.0)
            nc.vector.memset(decay_g[:, 2:4, 0:1], 0.0)
            dve.drain()
            unit = one.to_broadcast([P, SEQ])
            for i in range(2):
                nc.vector.tensor_tensor_scan(decay_b[:, i], unit, log_f[:, i, 0:SEQ], 0.0, ALU.mult, ALU.add)
                nc.vector.tensor_tensor_scan(decay_b[:, 2 + i, ::-1], unit, log_f[:, 2 + i, 0:SEQ][:, ::-1], 0.0, ALU.mult, ALU.subtract)
                nc.vector.tensor_tensor_scan(decay_g[:, i, 0:SEQ - 1][:, ::-1], unit[:, 1:], log_f[:, i, SEQ + 1:KEYS][:, ::-1], 0.0, ALU.mult, ALU.add)
                last = nc.vector.tensor_tensor_scan(decay_g[:, 2 + i, 1:SEQ], unit[:, 1:], log_f[:, 2 + i, SEQ:KEYS - 1], 0.0, ALU.mult, ALU.add)
            last.then_inc(scans_ready, 1)
            dve.wait_ge(decays_ready, 1)
            nc.vector.tensor_tensor(decay_g, decay_g, hk[:, :, SEQ:KEYS], ALU.mult).then_inc(kd_ready, 1)
            dve.wait_ge(decays_ready, 2)
            for d in range(2):
                last = nc.vector.tensor_tensor(qx[:, 2 * d:2 * d + 2], qx[:, 2 * d:2 * d + 2], hq, ALU.mult)
            last.then_inc(qx_ready, 1)

            dve.wait_ge(slot_done, TAIL + MOD_TAIL + IN2_SLOTS)
            nc.vector.memset(S_acc, 0.0)

            def difference(n):
                if n >= 2:
                    dve.wait_ge(gram_ready, n - 1)
                half = LEVELS[n] if n < len(LEVELS) else P
                for d in range(2):
                    b = flat(decay_b[:, 2 * d:2 * d + 2]).rearrange("p (b m) -> p b m", m=2 * half)
                    to = flat(lev[:, n % 2, 2 * d:2 * d + 2]).rearrange("p (b m) -> p b m", m=2 * half)
                    at = half - 1 + d
                    last = nc.vector.tensor_tensor(to, b, b[:, :, at:at + 1].to_broadcast([P, SEQ // half, 2 * half]), ALU.subtract)
                last.then_inc(diff_ready, 1)

            def level(n):
                dve.wait_ge(level_exp_ready, n + 1)
                half = LEVELS[n] if n < len(LEVELS) else P
                for d in range(2):
                    to = lev[:, n % 2, 2 * d:2 * d + 2].rearrange("p i (b s m) -> p i b s m", s=2, m=half)
                    for side in range(2):
                        by = (hk[:, 2 * d:2 * d + 2, 0:SEQ] if side == d else hq).rearrange("p i (b s m) -> p i b s m", s=2, m=half)
                        last = nc.vector.tensor_tensor(to[:, :, :, side], to[:, :, :, side], by[:, :, :, side], ALU.mult)
                last.then_inc(level_ready, 1)

            def merge(n):
                dve.wait_ge(gram_ready, n + 1)
                banks = 4 * (n % 2)
                if n < len(LEVELS):
                    for d in range(2):
                        dve.drain()
                        mask = K("levels", 2 * len(LEVELS) + 1, P)[:, 2 * n + d].bitcast(u32).unsqueeze(1).to_broadcast([P, 8, P])
                        last = nc.vector.copy_predicated(S_acc, mask, ps[:, banks + 2 * d:banks + 2 * d + 2, :].rearrange("p b (c t) -> p (b c) t", t=P))
                elif n == len(LEVELS):
                    for d in range(2):
                        last = nc.vector.tensor_copy(S_cross[:, d].rearrange("p (b c) t -> p b (c t)", b=2), ps[:, banks + 2 * d:banks + 2 * d + 2, 0:256])
                else:
                    dve.drain()
                    mask = K("levels", 2 * len(LEVELS) + 1, P)[:, 2 * len(LEVELS)].bitcast(u32).unsqueeze(1).to_broadcast([P, 8, P])
                    last = nc.vector.copy_predicated(S_acc, mask, ps[:, banks:banks + 2, :].rearrange("p b (c t) -> p (b c) t", t=P))
                last.then_inc(gram_used, 1)

            difference(0)
            for n in range(N_LEVELS):
                if n < N_LEVELS - 1:
                    level(n)
                else:
                    dve.wait_ge(gram_ready, n - 1)
                    nc.vector.tensor_tensor(lev[:, n % 2, 0:2], hk[:, 0:2, 0:SEQ], hk[:, 2:4, 0:SEQ], ALU.add).then_inc(level_ready, 1)
                if n + 1 < N_LEVELS - 1:
                    difference(n + 1)
                if n >= 1:
                    merge(n - 1)
            merge(N_LEVELS - 1)

            dve.wait_ge(o2_std_ready, 1)
            nc.vector.reciprocal(oh_rstd, oh_std)
            dve.drain()
            nc.vector.scalar_tensor_tensor(flat(oh), flat(oh), V("hgn"), oh_rstd, ALU.mult, ALU.mult)
            dve.drain()
            nc.vector.tensor_tensor(y2[:, 6:8], oh, hg, ALU.mult).then_inc(y2_ready, 1)

            nc.vector.tensor_copy(flat(y2[:, 0:2]), flat(mlp_u)).then_inc(y2_ready, 1)

            def max2(n):
                dve.wait_ge(s2_ready, n + 1)
                k = slice(n % AHEAD, n % AHEAD + 1)
                nc.vector.tensor_reduce(a_max[:, k], ps[:, 1 + n % AHEAD, 0:KEYS], AX.X, ALU.max)
                dve.drain()
                nc.vector.tensor_scalar(a_nmax[:, k], a_max[:, k], -0.125, None, ALU.mult).then_inc(s2_max_ready, 1)

            def out2(n):
                j, hh, i = UNITS[n]
                rows = slice(64 * hh, 64 * hh + 64)
                dve.wait_ge(pv2_ready, n + 1)
                nc.vector.tensor_copy(y2[rows, 2 + j, i * P:i * P + P], ps[rows, 6 + n % 2, 0:P]).then_inc(y2_ready, 1)

            for n in range(AHEAD - 1):
                max2(n)
            for n in range(len(UNITS)):
                k = slice(n % AHEAD, n % AHEAD + 1)
                dve.wait_ge(s2_exp_ready, n + 1)
                nc.vector.reciprocal(a_rsum[:, k], a_sum[:, k])
                dve.drain()
                nc.vector.tensor_scalar(ae[:, n % AHEAD], ae[:, n % AHEAD], a_rsum[:, k], None, ALU.mult).then_inc(p2_ready, 1)
                if n + AHEAD - 1 < len(UNITS):
                    if n >= 1:
                        dve.wait_ge(p2_turned, n)
                    max2(n + AHEAD - 1)
                if n >= 1:
                    out2(n - 1)
            out2(len(UNITS) - 1)

            for o in range(C):
                dve.wait_ge(slot_done, TAIL + MOD_TAIL + IN2_SLOTS + o + 1)
                nc.vector.scalar_tensor_tensor(x2[:, o], ps[:, o, 0:SEQ], mod[:, G1, 0][:, o:o + 1], raw2[:, o, 0:SEQ], ALU.mult, ALU.add).then_inc(x2_ready, 1)
            dve.wait_ge(std3_ready, 1)
            nc.vector.reciprocal(rstd3, std3)
            dve.drain()
            for c in range(C):
                nc.vector.scalar_tensor_tensor(h2[:, c], x2[:, c], a2[:, c:c + 1], rstd3, ALU.mult, ALU.mult).then_inc(h2_scaled, 1)

            dve.wait_ge(logits_ready, 1)
            nc.vector.tensor_tensor(R["lg"], ps[:, 1, 0:72].rearrange("p (t e) -> p t e", t=2), V("b_router").unsqueeze(1).to_broadcast([P, 2, 36]), ALU.add)
            dve.drain()
            groups = R["lg"][:, :, 0:GROUPS]
            nc.vector.tensor_reduce(R["gmax"], groups, AX.X, ALU.max)
            dve.drain()
            nc.vector.tensor_scalar(R["ngmax"], R["gmax"], -1.0, None, ALU.mult).then_inc(gmax_ready, 1)

            def first_greatest(x, top, n, index, scratch, onehot):
                iota = K("iota")[:, 0:n].unsqueeze(1).to_broadcast([P, 2, n])
                nc.vector.tensor_tensor(scratch, x, wide(top, 2, n), ALU.is_lt)
                dve.drain()
                nc.vector.scalar_tensor_tensor(scratch, scratch, 64.0, iota, ALU.mult, ALU.add)
                dve.drain()
                nc.vector.tensor_reduce(index, scratch, AX.X, ALU.min)
                dve.drain()
                nc.vector.tensor_tensor(onehot, iota, wide(index, 2, n), ALU.is_equal)
                dve.drain()

            first_greatest(groups, R["gmax"], GROUPS, R["i4"], R["t4"], R["one4"])
            nc.vector.tensor_scalar(R["t4"], R["one4"], -1.0, 1e30, ALU.add, ALU.mult)
            dve.drain()
            nc.vector.tensor_tensor(R["em"].rearrange("p t (g e) -> p t g e", g=GROUPS), R["lg"][:, :, GROUPS:].rearrange("p t (g e) -> p t g e", g=GROUPS),
                                    R["t4"].unsqueeze(3).to_broadcast([P, 2, GROUPS, PER_GROUP]), ALU.add)
            dve.drain()
            nc.vector.tensor_reduce(R["v1"], R["em"], AX.X, ALU.max)
            dve.drain()
            first_greatest(R["em"], R["v1"], E, R["i32"], R["t32"], R["oh1"])
            nc.vector.scalar_tensor_tensor(R["em"], R["oh1"], -3e30, R["em"], ALU.mult, ALU.add)
            dve.drain()
            nc.vector.tensor_reduce(R["v2"], R["em"], AX.X, ALU.max)
            dve.drain()
            nc.vector.tensor_tensor(R["d"], R["v2"], R["v1"], ALU.subtract).then_inc(top_ready, 1)
            first_greatest(R["em"], R["v2"], E, R["i32"], R["t32"], R["oh2"])
            nc.vector.tensor_tensor(R["chosen"], R["oh1"], R["oh2"], ALU.add).then_inc(chosen_ready, 1)
            dve.wait_ge(gexp_ready, 1)
            dve.wait_ge(top_exp_ready, 1)
            nc.vector.tensor_scalar(R["g1"], R["ex"], 1.0, None, ALU.add)
            dve.drain()
            nc.vector.tensor_tensor(R["g1"], R["g1"], R["gsum"], ALU.mult)
            dve.drain()
            nc.vector.reciprocal(R["g1"], R["g1"])
            dve.drain()
            nc.vector.tensor_tensor(R["g2"], R["g1"], R["ex"], ALU.mult)
            nc.vector.tensor_tensor(R["oh1"], R["oh1"], wide(R["g1"], 2, E), ALU.mult)
            dve.drain()
            nc.vector.tensor_tensor(R["oh2"], R["oh2"], wide(R["g2"], 2, E), ALU.mult)
            dve.drain()
            nc.vector.tensor_tensor(R["gate"], R["oh1"], R["oh2"], ALU.add)
            dve.drain()
            nc.vector.memset(ye, 0.0)
            nc.vector.memset(selT, 0.0)
            nc.vector.memset(R["rank"], -1.0)
            dve.wait_ge(ranks_ready, 1)
            nc.vector.tensor_reduce(R["gmax"][:, 0:1], ps[:, 2, 2 * E:3 * E], AX.X, ALU.max)
            dve.drain()
            ranks = R["rank"][:, :, 0:E]
            nc.vector.scalar_tensor_tensor(ranks, ps[:, 2, 0:2 * E].rearrange("p (t e) -> p t e", t=2), 1.0, R["chosen"], ALU.add, ALU.mult)
            nc.vector.tensor_copy(most[:, :], R["gmax"][:, 0:1])
            dve.drain()
            nc.vector.tensor_scalar(ranks, ranks, -1.0, None, ALU.add).then_inc(most_ready, 1)
            dve.drain()

            dve.sem_inc(ye_ready, 2)
            dve.sem_inc(hidT_ready, 1)
            dve.sem_inc(selT_ready, 1)
            iota = K("iota").unsqueeze(1).unsqueeze(1).to_broadcast([P, 2, 2, CAP])

            def by_slot(a, pair):
                return a[:, :, bass.ds(pair * 2, 2)].unsqueeze(3).to_broadcast([P, 2, 2, CAP])

            def select(pair):
                nc.vector.tensor_tensor(sel, iota, by_slot(R["rank"], pair), ALU.is_equal).then_inc(sel_ready, 1)

            def experts(pass_):
                select(0)
                with dve.Fori(0, PAIRS) as pair:
                    n = pass_ * PAIRS + pair
                    dve.drain()
                    dve.wait_ge(selT_ready, n + 1)
                    nc.vector.tensor_tensor(sel_gate, sel, by_slot(R["gate"], pair), ALU.mult).then_inc(sel_gate_ready, 1)
                    dve.drain()
                    dve.wait_ge(gathered, (pass_ * (PAIRS + 1) + pair) * 2 + 2)
                    select(pair + 1)
                    dve.wait_ge(e_act_ready, n + 1)
                    dve.wait_ge(big_done, n * BIG_SLOTS + BIG_SLOTS + 4)
                    nc.vector.tensor_tensor(e_hid, e_act, ps[:, 5, 0:FE], ALU.mult).then_inc(e_hid_ready, 1)

            experts(0)
            with dve.If(dve.value_load(most[0:1, 0:1], min_val=0, max_val=SEQ) > CAP):
                with dve.Fori(1, PASSES) as pass_:
                    dve.drain()
                    nc.vector.tensor_scalar(R["rank"], R["rank"], -float(CAP), None, ALU.add)
                    dve.drain()
                    dve.wait_ge(gathered, pass_ * (PAIRS + 1) * 2)
                    experts(pass_)
            dve.wait_ge(experts_done, 1)
            for o in range(C):
                nc.vector.scalar_tensor_tensor(x2[:, o], ps[:, o // 2, (o % 2) * SEQ:(o % 2) * SEQ + SEQ], mod[:, G2, 0][:, o:o + 1], x2[:, o],
                                               ALU.mult, ALU.add).then_inc(out_ready, 1)


def tiles(w, rows, cols):
    lead = w.shape[:-2]
    w = w.reshape(*lead, rows, P, cols, P)
    n = len(lead)
    return w.transpose(*range(n), n + 2, n + 1, n, n + 3)


def by_feature(a):
    return a.reshape(-1, P).T


def lay_out(x, meta_tokens, ffn1_norm, ffn1_w_gate, ffn1_w_up, ffn1_w_down, mix_norm, w_in, ret_gn_w, diff_subln_w,
            diff_lambda_q1, diff_lambda_k1, diff_lambda_q2, diff_lambda_k2, w_out, ffn2_norm, ffn2_w_gate, ffn2_w_up,
            ffn2_w_down, final_norm, c_2, ctx_2, c_ctx_2, w_mod_2, b_mod_2, norm1_w_2, w_in_2, w_s_2, b_s_2, q_norm_w_2,
            k_norm_w_2, hgrn_lb_logits_2, hgrn_norm_w_2, w_out_2, norm2_w_2, w_grp_2, b_grp_2, w_exp_2, b_exp_2, w1_2,
            w3_2, w2_2):
    f = np.float32
    ffn = np.empty((2 * DEPTH, GU_SLOTS + DOWN_SLOTS, P, SLOT), f)
    for l in range(DEPTH):
        for i, (g, u, d) in enumerate(((ffn1_w_gate, ffn1_w_up, ffn1_w_down), (ffn2_w_gate, ffn2_w_up, ffn2_w_down))):
            to = ffn[2 * l + i]
            both = to[:GU_SLOTS].reshape(F, P, 2, C, P)
            both[:, :, 0] = tiles(g[l], C, F)
            both[:, :, 1] = tiles(u[l], C, F)
            to[GU_SLOTS:] = d[l].reshape(DOWN_SLOTS, 2, P, D).transpose(0, 2, 1, 3).reshape(DOWN_SLOTS, P, SLOT)

    def features(w, first):
        w = w[:, first * P:(first + 2) * P]
        return tiles(w, C, 2).transpose(1, 0, 2, 3).reshape(P, -1)

    def rows(w, first, n):
        return w[:, first:first + n].reshape(C, P, n).transpose(1, 0, 2).reshape(P, -1)

    win = np.empty((DEPTH, IN_SLOTS, P, SLOT), f)
    for l in range(DEPTH):
        w = w_in[l]
        q = 0
        for first in (16, 18, 20, 22, "dv", 0, 2, 4, 6, "rv", 12, 14):
            if isinstance(first, str):
                v = rows(w, (24 if first == "dv" else 8) * P, 512)
                win[l, q], win[l, q + 1] = v[:, :SLOT], v[:, SLOT:]
                q += 2
            else:
                win[l, q] = features(w, first)
                q += 1
    wout = np.ascontiguousarray(tiles(w_out, C, C).reshape(DEPTH, OUT_SLOTS, P, D))

    mod = np.stack([rows(w_mod_2[0], q * MOD_COLS, MOD_COLS) for q in range(MOD_SLOTS)])
    w = w_in_2[0]
    in2 = np.zeros((IN2_SLOTS, P, SLOT), f)
    key = w[:, 1024:1152].reshape(D, 2, 1, 64)
    twice = np.concatenate([key, key], 2).reshape(D, 256)
    for q, a in enumerate((features(twice, 0), features(w, 4), features(w, 6), rows(w, 256, 256), features(w, 0),
                           features(w, 12), features(w, 14), rows(w, 2048, 256), features(w, 10), rows(w, 1152, 128), features(w, 18))):
        in2[q, :, :a.shape[1]] = a
    out2 = np.ascontiguousarray(tiles(w_out_2[0], C, C).reshape(OUT_SLOTS, P, D))
    expert = np.empty((PAIRS, BIG_SLOTS, P, BIG), f)
    up = expert[:, 0:4].reshape(PAIRS, 2, 2, P, C, FE)
    up[:, 0] = w1_2[0].reshape(PAIRS, 2, C, P, FE).transpose(0, 1, 3, 2, 4)
    up[:, 1] = w3_2[0].reshape(PAIRS, 2, C, P, FE).transpose(0, 1, 3, 2, 4)
    expert[:, 4:6] = w2_2[0].reshape(PAIRS, 2, FE // P, P, D).transpose(0, 1, 3, 2, 4).reshape(PAIRS, 2, P, BIG)

    vec = np.empty((P, N_VEC), f)

    def put(name, a):
        at, n = VEC[name]
        vec[:, at:at + n] = np.asarray(a).reshape(-1, n)

    norms = np.stack([np.stack([ffn1_norm[l], mix_norm[l], ffn2_norm[l]]) for l in range(DEPTH)])
    put("norms", by_feature(norms))
    put("final", by_feature(final_norm))
    put("gn", by_feature(ret_gn_w))
    put("subln", by_feature(diff_subln_w))
    put("lam", np.stack([diff_lambda_q1, diff_lambda_k1, diff_lambda_q2, diff_lambda_k2], 1))
    put("norm1", by_feature(norm1_w_2))
    put("norm2", by_feature(norm2_w_2))
    put("b_mod", by_feature(b_mod_2))
    put("c", np.stack([c_2.reshape(C, P).T, c_ctx_2.reshape(C, P).T], 2).reshape(P, -1))
    for name, a in (("qn", q_norm_w_2), ("kn", k_norm_w_2), ("hgn", hgrn_norm_w_2)):
        put(name, np.concatenate([a[0], a[0]])[:, None])
    put("b_s", np.repeat(b_s_2[0].reshape(2, 2, P).transpose(1, 0, 2).reshape(2, 2 * P), 64, axis=0))
    put("b_router", np.concatenate([b_grp_2, b_exp_2], 1))

    first = np.concatenate([meta_tokens, x[0]], 0)
    return {
        "stream_ffn": ffn, "stream_in": win, "stream_out": wout, "stream_mod": mod, "stream_in2": in2, "stream_out2": out2,
        "stream_expert": expert,
        "h_first": np.ascontiguousarray(first.T.reshape(C, P, T).transpose(1, 0, 2)),
        "ctx_in": np.ascontiguousarray(ctx_2[0].T.reshape(C, P, CTX).transpose(1, 0, 2)),
        "vectors": vec, "tables": constants(),
        "w_router": np.ascontiguousarray(np.concatenate([w_grp_2[0], w_exp_2[0]], 1).reshape(C, P, GROUPS + E).transpose(1, 0, 2)),
        "w_spatial": np.ascontiguousarray(w_s_2[0].transpose(2, 0, 1)),
    }


def kernel(**inputs):
    import concourse.bacc as bacc
    from concourse.bass_utils import run_bass_kernel_spmd

    arrays = lay_out(**{k: np.asarray(v) for k, v in inputs.items()})
    nc = bacc.Bacc("TRN2", target_bir_lowering=False, num_devices=1)
    aps = {name: nc.dram_tensor(name, a.shape, mybir.dt.from_np(a.dtype), kind="ExternalInput").ap() for name, a in arrays.items()}
    out = nc.dram_tensor("out", (P, C, SEQ), mybir.dt.float32, kind="ExternalOutput").ap()
    build(nc, out=out, **aps)
    result = run_bass_kernel_spmd(nc, [arrays], core_ids=[0]).results[0]["out"]
    return np.ascontiguousarray(np.asarray(result).transpose(2, 1, 0)).reshape(1, SEQ, D)
```
